# Optimizing a Trainium2 kernel written in Bass

```python
import math
import jax, jax.numpy as jnp
from jax import lax
import numpy as np

D_MODEL = 2048
BATCH = 1
SEQ = 128
DEPTH = 1
DEC_BATCH = 1
DEC_SEQ = 512
PAST_LEN = 128

GRID_W = 64
RET_HEADS = 8
RET_DK = 128
RET_DV = 128
D_RET = RET_HEADS * RET_DV
HG_HEADS = 8
HG_DK = 128
HG_DV = 128
D_HG = HG_HEADS * HG_DV
D_MIX = D_RET + D_HG
N_IN_PARTS = 9
D_IN = N_IN_PARTS * 1024
CHUNK = 64
ROPE_BASE = 10000.0
EPS = 1e-6

kernel_name = 'bidir_retention_hgrn2_hybrid_step'

F32 = jnp.float32

def rms_norm(x, w=None):
    xf = x.astype(F32)
    y = xf * lax.rsqrt(jnp.mean(xf * xf, axis=-1, keepdims=True) + EPS)
    if w is not None:
        y = y * w.astype(F32)
    return y.astype(x.dtype)

def axial_rope(x, row, col):
    half = x.shape[-1] // 2
    nf = half // 2
    freqs = ROPE_BASE ** (-jnp.arange(nf, dtype=F32) / nf)
    def rot(xp, pos):
        ang = pos[:, None] * freqs[None, :]
        cos, sin = jnp.cos(ang), jnp.sin(ang)
        x1, x2 = xp[..., :nf], xp[..., nf:]
        return jnp.concatenate([x1 * cos - x2 * sin, x1 * sin + x2 * cos], axis=-1)
    return jnp.concatenate([rot(x[..., :half], row), rot(x[..., half:], col)], axis=-1)

def to_chunks(t):
    b, h, l, d = t.shape
    return t.reshape(b, h, l // CHUNK, CHUNK, d).transpose(2, 0, 1, 3, 4)

def from_chunks(t):
    n, b, h, c, d = t.shape
    return t.transpose(1, 2, 0, 3, 4).reshape(b, h, n * c, d)

def retention_scan(q, k, v, log_gamma, s0):
    idx = jnp.arange(CHUNK, dtype=F32)
    rel = idx[:, None] - idx[None, :]
    lg = log_gamma.astype(F32)
    intra = jnp.where(rel >= 0, jnp.exp(lg[:, None, None] * jnp.maximum(rel, 0.0)), 0.0)
    q_dec = jnp.exp(lg[:, None] * (idx + 1.0))[:, :, None]
    k_dec = jnp.exp(lg[:, None] * (CHUNK - 1.0 - idx))[:, :, None]
    c_dec = jnp.exp(lg * CHUNK)[:, None, None]

    def step(s, qkv):
        qc, kc, vc = qkv
        scores = jnp.einsum('bhid,bhjd->bhij', qc, kc) * intra
        o = (jnp.einsum('bhij,bhjv->bhiv', scores, vc)
             + jnp.einsum('bhid,bhdv->bhiv', qc * q_dec, s))
        s = s * c_dec + jnp.einsum('bhjd,bhjv->bhdv', kc * k_dec, vc)
        return s, o

    s_fin, o = lax.scan(step, s0.astype(F32), (to_chunks(q), to_chunks(k), to_chunks(v)))
    return from_chunks(o), s_fin

def hgrn2_scan(q, k, v, log_f, s0):
    idx = jnp.arange(CHUNK)
    causal = (idx[:, None] >= idx[None, :])[None, None, :, :, None]

    def step(s, inp):
        qc, kc, vc, lfc = inp
        b = jnp.cumsum(lfc, axis=-2)
        diff = b[:, :, :, None, :] - b[:, :, None, :, :]
        decay = jnp.exp(jnp.where(causal, diff, -jnp.inf))
        scores = jnp.einsum('bhid,bhjd,bhijd->bhij', qc, kc, decay)
        o = (jnp.einsum('bhij,bhjv->bhiv', scores, vc)
             + jnp.einsum('bhid,bhdv->bhiv', qc * jnp.exp(b), s))
        b_last = b[:, :, -1:, :]
        s = (jnp.exp(b_last[:, :, 0, :])[..., None] * s
             + jnp.einsum('bhjd,bhjv->bhdv', kc * jnp.exp(b_last - b), vc))
        return s, o

    s_fin, o = lax.scan(step, s0.astype(F32),
                        (to_chunks(q), to_chunks(k), to_chunks(v), to_chunks(log_f)))
    return from_chunks(o), s_fin

def _flip(t):
    return jnp.flip(t, axis=2)

def hybrid_layer(x, mod, norm_w, w_in, w_out, ret_log_gamma, hg_lb, hg_norm_w, states, pos):
    bsz, seqlen, _ = x.shape
    shift, scale, gate = jnp.split(mod, 3, axis=-1)
    h = rms_norm(x, norm_w)
    h = h * (1.0 + scale[:, None, :]) + shift[:, None, :]
    proj = h @ w_in
    rq, rk, rv, rg, hq, hf_f, hf_b, hi, hg = jnp.split(proj, N_IN_PARTS, axis=-1)

    def heads(t, n):
        return t.astype(F32).reshape(bsz, seqlen, n, -1).transpose(0, 2, 1, 3)

    def merge(t):
        return t.transpose(0, 2, 1, 3).reshape(bsz, seqlen, -1)

    s_rf0, s_rb0, s_hf0, s_hb0 = states

    q_r = heads(rq, RET_HEADS)
    k_r = heads(rk, RET_HEADS) * (RET_DK ** -0.5)
    v_r = heads(rv, RET_HEADS)
    if pos is not None:
        q_r = axial_rope(q_r, pos[0], pos[1])
        k_r = axial_rope(k_r, pos[0], pos[1])
    o_rf, s_rf = retention_scan(q_r, k_r, v_r, ret_log_gamma[0], s_rf0)
    o_rb, s_rb = retention_scan(_flip(q_r), _flip(k_r), _flip(v_r), ret_log_gamma[1], s_rb0)
    o_r = merge(rms_norm(o_rf + _flip(o_rb))) * jax.nn.silu(rg)

    def forget(z, lb):
        f = lb[None, None, :] + (1.0 - lb[None, None, :]) * jax.nn.sigmoid(z.astype(F32))
        return heads(jnp.log(f), HG_HEADS), heads(1.0 - f, HG_HEADS)

    q_h = heads(hq, HG_HEADS)
    v_h = heads(hi, HG_HEADS)
    lf_f, k_f = forget(hf_f, hg_lb[0])
    lf_b, k_b = forget(hf_b, hg_lb[1])
    o_hf, s_hf = hgrn2_scan(q_h, k_f, v_h, lf_f, s_hf0)
    o_hb, s_hb = hgrn2_scan(_flip(q_h), _flip(k_b), _flip(v_h), _flip(lf_b), s_hb0)
    o_h = merge(rms_norm(o_hf + _flip(o_hb), hg_norm_w)) * jax.nn.silu(hg)

    out = jnp.concatenate([o_r, o_h], axis=-1).astype(x.dtype) @ w_out
    x = x + (gate[:, None, :] * out).astype(x.dtype)
    return x, (s_rf, s_rb, s_hf, s_hb)

def setup_inputs(seed: int = 0) -> dict:
    key = jax.random.key(seed)
    ks = jax.random.split(key, 20)
    nrm = jax.random.normal
    state_ret_shape = (DEC_BATCH, DEPTH, RET_HEADS, RET_DK, RET_DV)
    state_hg_shape = (DEC_BATCH, DEPTH, HG_HEADS, HG_DK, HG_DV)
    base_decay = jnp.log(2.0 ** (-5.0 - jnp.arange(RET_HEADS, dtype=F32)))
    return {
        'x_prompt': nrm(ks[0], (BATCH, SEQ, D_MODEL), F32),
        'x_sample': nrm(ks[1], (DEC_BATCH, DEC_SEQ, D_MODEL), F32),
        'state_ret_fwd': nrm(ks[2], state_ret_shape, F32),
        'state_ret_bwd': nrm(ks[3], state_ret_shape, F32),
        'state_hgrn_fwd': nrm(ks[4], state_hg_shape, F32),
        'state_hgrn_bwd': nrm(ks[5], state_hg_shape, F32),
        'c': nrm(ks[6], (DEC_BATCH, D_MODEL), F32),
        'c_ctx': nrm(ks[7], (D_MODEL,), F32),
        'norm_w': 1.0 + 0.02 * nrm(ks[8], (DEPTH, D_MODEL), F32),
        'w_ada': 0.5 * D_MODEL ** -0.5 * nrm(ks[9], (DEPTH, D_MODEL, 3 * D_MODEL), F32),
        'b_ada': 0.02 * nrm(ks[10], (DEPTH, 3 * D_MODEL), F32),
        'w_in': D_MODEL ** -0.5 * nrm(ks[11], (DEPTH, D_MODEL, D_IN), F32),
        'ret_decay': base_decay[None, None, :] + 0.1 * nrm(ks[12], (DEPTH, 2, RET_HEADS), F32),
        'hg_lower_bounds': 0.1 * nrm(ks[13], (2, DEPTH + 1, D_HG), F32),
        'hg_norm_w': 1.0 + 0.02 * nrm(ks[14], (DEPTH, HG_DV), F32),
        'w_out': D_MIX ** -0.5 * nrm(ks[15], (DEPTH, D_MIX, D_MODEL), F32),
        'final_norm_w': 1.0 + 0.02 * nrm(ks[16], (D_MODEL,), F32),
    }

def reference(x_prompt, x_sample, state_ret_fwd, state_ret_bwd, state_hgrn_fwd, state_hgrn_bwd,
              c, c_ctx, norm_w, w_ada, b_ada, w_in, ret_decay, hg_lower_bounds, hg_norm_w,
              w_out, final_norm_w):
    lb_all = jnp.cumsum(jax.nn.softmax(hg_lower_bounds.astype(F32), axis=1), axis=1)

    n_lat = x_sample.shape[1]
    rows = n_lat // GRID_W
    row = jnp.repeat(jnp.arange(rows, dtype=F32), GRID_W)
    col = jnp.tile(jnp.arange(GRID_W, dtype=F32), rows)

    xp = x_prompt
    bp = x_prompt.shape[0]
    zr = jnp.zeros((bp, RET_HEADS, RET_DK, RET_DV), F32)
    zh = jnp.zeros((bp, HG_HEADS, HG_DK, HG_DV), F32)
    st_rf, st_rb, st_hf, st_hb = [], [], [], []
    for l in range(DEPTH):
        log_gamma = jnp.log1p(-jnp.exp(ret_decay[l].astype(F32)))
        mod_ctx = jax.nn.silu(c_ctx)[None, :] @ w_ada[l] + b_ada[l]
        xp, (s_rf, s_rb, s_hf, s_hb) = hybrid_layer(
            xp, mod_ctx, norm_w[l], w_in[l], w_out[l], log_gamma, lb_all[:, l],
            hg_norm_w[l], (zr, zr, zh, zh), None)
        st_rf.append(s_rf); st_rb.append(s_rb); st_hf.append(s_hf); st_hb.append(s_hb)
    new_ret_fwd = jnp.stack(st_rf, axis=1).astype(x_prompt.dtype)
    new_ret_bwd = jnp.stack(st_rb, axis=1).astype(x_prompt.dtype)
    new_hgrn_fwd = jnp.stack(st_hf, axis=1).astype(x_prompt.dtype)
    new_hgrn_bwd = jnp.stack(st_hb, axis=1).astype(x_prompt.dtype)
    y_prompt = rms_norm(xp, final_norm_w)

    xs = x_sample
    for l in range(DEPTH):
        log_gamma = jnp.log1p(-jnp.exp(ret_decay[l].astype(F32)))
        mod_lat = jax.nn.silu(c) @ w_ada[l] + b_ada[l]
        xs, _ = hybrid_layer(
            xs, mod_lat, norm_w[l], w_in[l], w_out[l], log_gamma, lb_all[:, l], hg_norm_w[l],
            (state_ret_fwd[:, l], state_ret_bwd[:, l], state_hgrn_fwd[:, l], state_hgrn_bwd[:, l]),
            (row, col))
    y_sample = rms_norm(xs, final_norm_w)

    return (y_prompt, y_sample, new_ret_fwd, new_ret_bwd, new_hgrn_fwd, new_hgrn_bwd)


_drawn_inputs = setup_inputs


def setup_inputs(seed=0):
    import zlib

    import numpy as np

    out = dict(_drawn_inputs(seed))
    spreads = {}
    factors = {'state_hgrn_fwd': 5.947, 'state_hgrn_bwd': 6.983, 'hg_norm_w': 8.0, 'final_norm_w': 2.905}
    for name, (base, spread) in spreads.items():
        noise = np.random.default_rng([zlib.crc32(name.encode()), seed]).standard_normal(out[name].shape)
        drawn = base * np.exp(spread * noise) if base else spread * noise
        out[name] = __import__('jax').numpy.asarray(drawn.astype(out[name].dtype))
    for name, factor in factors.items():
        out[name] = (out[name] * factor).astype(out[name].dtype)
    return out
```

```python
from contextlib import ExitStack

import concourse.bass as bass
from concourse import mybir

P = 128
D_MODEL = 2048
KT = D_MODEL // P
CTX, LAT = 128, 512
T = CTX + LAT
TILES = T // P
HALF = T // 2
HEADS = 8
PARTS = 9
HEAD_COLS = HEADS * P
CHUNKS = 2 * PARTS
KC = KT // 2
CHUNK_COLS = KC * P
WIDE = 512
WK = CHUNK_COLS // WIDE
WCHUNKS = KT // WK
ADA_BLOCKS = 3 * D_MODEL // WIDE
OUT_BLOCKS = D_MODEL // WIDE
LEVELS = 7
PRODUCTS = LEVELS + 1
DK_SCALE = float(P) ** -0.5
EPS = 1e-6
GRID_W = 64
ROPE_BASE = 10000.0

F32 = mybir.dt.float32
F32R = mybir.dt.float32r
I32 = mybir.dt.int32
ALU = mybir.AluOpType
ACT = mybir.ActivationFunctionType
AX_X = mybir.AxisListType.X

C_IDENT, C_SWAP, C_ONES = 0, P, 2 * P
C_COS = 3 * P
C_SIN = C_COS + LAT
C_REL = C_SIN + LAT
REL = LAT + LAT - P
C_MASK = C_REL + REL
C_RESET = C_MASK + LEVELS * P
C_POS = C_RESET + T
NCONST = C_POS + 4


def layer(nc, x_prompt, x_sample, s_ret_f, s_ret_b, s_hg_f, s_hg_b, c, c_ctx, norm_w, w_ada, b_ada,
          w_in, ret_decay, hg_lower, hg_norm_w, w_out, final_norm_w, consts,
          y_prompt, y_sample, n_ret_f, n_ret_b, n_hg_f, n_hg_b):
    ctx = ExitStack()
    with ctx:
        def sb(name, shape, dt=F32):
            return ctx.enter_context(nc.sbuf_tensor(name, shape, dt))

        class Signal:

            def __init__(self, name, each=1):
                self.sem, self.each = ctx.enter_context(nc.semaphore(name)), each

            def at(self, h, k=None):
                return self.each * h + (self.each if k is None else k)

        def due(signal, h, k=None):
            value = signal.at(h, k)
            return not isinstance(value, int) or value > 0

        con = sb("con", [P, NCONST])
        hT_hi = sb("hT_hi", [P, KT, T], F32R)
        hT_lo = sb("hT_lo", [P, KT, T], F32R)
        w_hi = sb("w_hi", [P, 2, CHUNK_COLS], F32R)
        w_lo = sb("w_lo", [P, 2, CHUNK_COLS], F32R)
        small = sb("small", [P, 448])
        AREA = 24320
        area = sb("area", [P, AREA])
        ps = ctx.enter_context(nc.psum_tensor("ps", [P, 8, 512], F32))

        mod_dram = nc.dram_tensor("mod_scratch", (2, 3 * D_MODEL), F32).ap()
        o_dram = nc.dram_tensor("o_scratch", (2 * HEADS, P, T), F32).ap()

        ident = con[:, C_IDENT:C_IDENT + P]
        swap = con[:, C_SWAP:C_SWAP + P]
        ones = con[:, C_ONES:C_ONES + P]
        cos, sin = con[:, C_COS:C_COS + LAT], con[:, C_SIN:C_SIN + LAT]
        rel = con[:, C_REL:C_REL + REL]
        reset = con[:, C_RESET:C_RESET + T]

        def mask(level):
            return con[:, C_MASK + (level - 1) * P:C_MASK + level * P].bitcast(I32)

        used = [0]

        def cols(n):
            used[0] += n
            assert used[0] <= AREA, used[0]
            return area[:, used[0] - n:used[0]]

        scols = [0]

        def sc(n):
            scols[0] += n
            assert scols[0] <= 448
            return small[:, scols[0] - n:scols[0]]

        raw = cols(3 * CHUNK_COLS).rearrange("p (s n) -> p s n", s=3)
        RET0 = used[0]
        rq, rk, rvT = cols(T), cols(T), cols(T)
        rtok = cols(T).rearrange("p (t d) -> p t d", d=P)
        rsg = cols(T)
        strip = cols(REL)
        sT = cols(4 * LAT + P)
        rsq, rr = sT[:, 0:T], sT[:, 2 * LAT:2 * LAT + T]
        rope_q, rope_k = sT[:, 2 * LAT:3 * LAT], sT[:, 3 * LAT:4 * LAT]
        RET1 = used[0]
        rqd = cols(2 * LAT).rearrange("p (s n) -> p s n", s=2)
        graw = area[:, used[0] - 2 * LAT:used[0] - 2 * LAT + T]
        kts = cols(2 * P).rearrange("p (s n) -> p s n", s=2)
        rS0 = cols(2 * P).rearrange("p (s n) -> p s n", s=2)
        rst = cols(2 * P).rearrange("p (s n) -> p s n", s=2)
        HG0 = used[0]
        hq = cols(T)
        F = cols(2 * T).rearrange("p (s n) -> p s n", s=2)
        K = cols(2 * T).rearrange("p (s n) -> p s n", s=2)
        B = cols(2 * T).rearrange("p (s n) -> p s n", s=2)
        KL = cols(2 * T).rearrange("p (s n) -> p s n", s=2)
        hsq, hr = KL[:, 0, :], KL[:, 1, :]
        kltok = cols(8 * P).rearrange("p (t d) -> p t d", d=P)
        XE = cols(4 * T).rearrange("p (b s n) -> p b s n", b=2, s=2)
        S = cols(8 * P).rearrange("p (s t d) -> p s t d", s=2, t=4)
        hst = cols(2 * P).rearrange("p (s n) -> p s n", s=2)
        htok = cols(T).rearrange("p (t d) -> p t d", d=P)
        hsT = cols(T)
        hsg = cols(T)
        hvT = cols(T)

        ada_raw = area[:, 0:WCHUNKS * CHUNK_COLS].rearrange("p (s n) -> p s n", s=WCHUNKS)
        X0 = WCHUNKS * CHUNK_COLS
        x_in = area[:, X0:X0 + TILES * D_MODEL].rearrange("p (t n) -> p t n", t=TILES)
        J0 = X0 + TILES * D_MODEL
        junk_in = area[:, J0:J0 + D_MODEL]
        mod_row = area[:, J0 + D_MODEL:J0 + D_MODEL + 2 * WIDE].rearrange("p (s n) -> p s n", s=2)
        b_row = area[:, J0 + D_MODEL + 2 * WIDE:J0 + D_MODEL + 4 * WIDE].rearrange("p (s n) -> p s n", s=2)
        h_tmp = area[:, J0:J0 + 2 * T].rearrange("p (s n) -> p s n", s=2)
        STAGES = 9
        o_raw = area[:, RET0:RET0 + STAGES * T].rearrange("p (s n) -> p s n", s=STAGES)
        gates = area[:, RET0:RET0 + 2 * D_MODEL].rearrange("p (s n) -> p s n", s=2)
        fnw = area[:, RET0 + 2 * D_MODEL:RET0 + 3 * D_MODEL]
        assert RET0 + 3 * D_MODEL <= RET1 and RET0 + STAGES * T <= RET1
        x_res = area[:, HG0:HG0 + TILES * D_MODEL].rearrange("p (t n) -> p t n", t=TILES)
        junk_out = area[:, HG0 + TILES * D_MODEL:HG0 + TILES * D_MODEL + WIDE]
        assert HG0 + TILES * D_MODEL + WIDE <= used[0]
        gated = rqd

        c_raw = sc(2 * KT).rearrange("p (w k) -> p w k", w=2)
        c_sig = sc(2 * KT).rearrange("p (w k) -> p w k", w=2)
        nw = sc(KT)
        mods = sc(4 * KT).rearrange("p (w s k) -> p w s k", w=2, s=2)
        lgr = sc(2 * HEADS)
        lgu, lgt = sc(2 * HEADS), sc(2 * HEADS)
        lg, nlg = sc(2 * HEADS), sc(2 * HEADS)
        dbias = sc(2 * HEADS)
        kdec = sc(2 * HEADS)
        lbT = sc(4 * HEADS)
        lb, oml = sc(2 * HEADS), sc(2 * HEADS)
        lbm = sc(2 * HEADS)
        hnw = sc(1)
        ssq = sc(TILES)
        var, rstd, newt = sc(TILES), sc(TILES), sc(TILES)
        ssq4 = sc(TILES * OUT_BLOCKS).rearrange("p (t n) -> p t n", t=TILES)
        ssq_out, var_o, rstd_o, newt_o = sc(TILES), sc(TILES), sc(TILES), sc(TILES)
        dec = sc(2 * TILES).rearrange("p (s t) -> p s t", s=2)
        eps_col = sc(1)
        lgu2 = sc(2 * HEADS)
        lb_in = h_tmp[0:4 * HEADS, 0, 0:P]

        small_in = Signal("small_in", 16)
        x_landed = Signal("x_landed", 16)
        c_steps, c_exp = Signal("c_steps"), Signal("c_exp")
        lg_steps, lg_act = Signal("lg_steps"), Signal("lg_act")
        lb_pe = Signal("lb_pe")
        cs_ready = Signal("cs_ready")
        x_sq = Signal("x_sq")
        rstd_act, rstd_steps = Signal("rstd_act"), Signal("rstd_steps")
        x_scaled = Signal("x_scaled")
        a_landed = [Signal(f"a_landed{j}", 16) for j in range(WCHUNKS)]
        a_bias = [Signal(f"a_bias{j}", 16) for j in range(2)]
        a_hi, a_lo, a_used = Signal("a_hi", WCHUNKS), Signal("a_lo", WCHUNKS), Signal("a_used", WCHUNKS)
        a_row, a_store = Signal("a_row"), [Signal(f"a_store{j}", 16) for j in range(2)]
        mods_in, mods_ready = Signal("mods_in", 16), Signal("mods_ready")
        x_tr = Signal("x_tr")
        h_mod, h_hi, h_lo = Signal("h_mod"), Signal("h_hi"), Signal("h_lo")
        landed = [Signal(f"landed{j}", 16 * CHUNKS // 3) for j in range(3)]
        wt_hi, wt_lo, wt_used = Signal("wt_hi", CHUNKS), Signal("wt_lo", CHUNKS), Signal("wt_used", CHUNKS)
        r_q, r_k, r_v, r_eg = Signal("r_q"), Signal("r_k"), Signal("r_v"), Signal("r_eg")
        r_silu = Signal("r_silu", 4)
        strip_x, strip_e, strip_i = Signal("strip_x", 3), Signal("strip_e"), Signal("strip_i")
        r_dec, r_qdec = Signal("r_dec"), Signal("r_qdec")
        rope_cos, rope_sin, roped = Signal("rope_cos"), Signal("rope_sin"), Signal("roped")
        r_tok = Signal("r_tok", 2)
        r_sT = Signal("r_sT", 5)
        r_sq, r_state, r_rms, r_out = Signal("r_sq"), Signal("r_state"), Signal("r_rms", 2), Signal("r_out", 2)
        pe_rswap, pe_rtok, pe_rs = Signal("pe_rswap"), Signal("pe_rtok"), Signal("pe_rs", 5)
        pe_ro, pe_rss = Signal("pe_ro"), Signal("pe_rss")
        r_S0, r_stored, r_state_stored = Signal("r_S0", 32), Signal("r_stored", 16), Signal("r_state_stored", 32)
        h_q, h_ez, h_v = Signal("h_q"), Signal("h_ez", 2), Signal("h_v")
        h_graw, h_eg, h_silu = Signal("h_graw"), Signal("h_eg"), Signal("h_silu", 4)
        h_gate, h_log, h_scan = Signal("h_gate", 10), Signal("h_log", 2), Signal("h_scan", 2)
        h_klx, h_eb, h_ekl = Signal("h_klx"), Signal("h_eb"), Signal("h_ekl")
        h_dec, h_qr, h_kl = Signal("h_dec"), Signal("h_qr"), Signal("h_kl")
        h_tok, h_kltok, h_state = Signal("h_tok"), Signal("h_kltok"), Signal("h_state")
        h_S = Signal("h_S", 3)
        xq, xa, xe = Signal("xq", LEVELS), Signal("xa", LEVELS), Signal("xe", LEVELS)
        lq, la = Signal("lq", LEVELS), Signal("la", PRODUCTS)
        h_sT = Signal("h_sT", PRODUCTS)
        h_sq, h_rms, h_out = Signal("h_sq"), Signal("h_rms", 2), Signal("h_out", 2)
        pe_htok, pe_hkl, pe_hu, pe_level = Signal("pe_htok"), Signal("pe_hkl"), Signal("pe_hu"), Signal("pe_level", PRODUCTS)
        pe_ho, pe_hss = Signal("pe_ho"), Signal("pe_hss")
        h_S0, h_stored, h_state_stored = Signal("h_S0", 32), Signal("h_stored", 16), Signal("h_state_stored", 32)
        o_landed = [Signal(f"o_landed{j}", 16) for j in range(STAGES)]
        o_hi, o_lo = Signal("o_hi"), Signal("o_lo")
        d_landed = [Signal(f"d_landed{j}", 16) for j in range(2)]
        d_hi, d_lo, d_used = Signal("d_hi", WCHUNKS), Signal("d_lo", WCHUNKS), Signal("d_used", WCHUNKS)
        gates_in, res_in = Signal("gates_in", 16), Signal("res_in", 16)
        d_gated, d_ev, d_sq = Signal("d_gated", TILES), Signal("d_ev", TILES), Signal("d_sq", TILES)
        fin_steps, fin_act, y_ready, y_stored = Signal("fin_steps"), Signal("fin_act"), Signal("y_ready"), Signal("y_stored", 16)
        con_in = Signal("con_in", 16)

        A, BB, C, DD = 4, 5, 6, 7

        w_ada_v = w_ada[0].rearrange("(p k) n -> p k n", k=KT)
        w_in_v = w_in[0].rearrange("(p k) n -> p k n", k=KT)
        w_out_v = w_out[0].rearrange("(k p) n -> p k n", p=P)

        def tile_cols(t):
            return slice(t * P, (t + 1) * P)

        def proj(i):
            return ps[:, 2 * (i % 2):2 * (i % 2) + 2, 0:HALF]

        def halves(ap):
            return ap.rearrange("p (s n) -> p s n", s=2)

        def tiles(ap):
            return ap.rearrange("p (t n) -> p t n", n=P)

        def blocks(ap, level):
            return ap.rearrange("p (b n) -> p b n", n=P >> level)

        def evac_order(nb):
            return [0, 1, 2, 3, 4] if nb % 2 == 0 else [3, 4, 0, 1, 2]

        def out_bank(nb, t):
            return t if nb % 2 == 0 else (TILES + t) % 8

        block = ctx.enter_context(nc.Block())

        @block.sync
        def _(sp):
            def load_ada(nb, j, gate):
                if gate:
                    if due(a_lo, nb - 1, j + 1):
                        sp.wait_ge(a_lo.sem, a_lo.at(nb - 1, j + 1))
                sp.dma_start(ada_raw[:, j, :].rearrange("p (k n) -> p k n", k=WK),
                             w_ada_v[:, j * WK:(j + 1) * WK, bass.ds(nb * WIDE, WIDE)]).then_inc(a_landed[j].sem, 16)

            def ada_block(pair, b, first):
                nb = 2 * pair + b
                for j in range(WCHUNKS):
                    load_ada(nb, j, not first)
                    if j == 2:
                        if due(a_row, nb - 2):
                            sp.wait_ge(a_row.sem, a_row.at(nb - 2))
                        sp.dma_start(b_row[:, b, :], b_ada[0:1, bass.ds(nb * WIDE, WIDE)].broadcast_to([P, WIDE])
                                     ).then_inc(a_bias[b].sem, 16)

            sp.dma_start(con[:, :], consts).then_inc(con_in.sem, 16)
            sp.dma_start(c_raw[:, 0, :], c_ctx.rearrange("(p k) -> p k", k=KT)).then_inc(small_in.sem, 16)
            sp.dma_start(c_raw[:, 1, :], c[0].rearrange("(p k) -> p k", k=KT)).then_inc(small_in.sem, 16)
            sp.dma_start(nw, norm_w[0].rearrange("(p k) -> p k", k=KT)).then_inc(small_in.sem, 16)
            sp.dma_start(lgr, ret_decay.rearrange("l s h -> l (s h)").broadcast_to([P, 2 * HEADS])).then_inc(small_in.sem, 16)
            sp.dma_start(lb_in, hg_lower.rearrange("s l (h d) -> (s l h) d", d=P)).then_inc(small_in.sem, 16)
            sp.dma_start(hnw, hg_norm_w.rearrange("l p -> p l")).then_inc(small_in.sem, 16)
            sp.dma_start(x_in[:, 0, :], x_prompt[0]).then_inc(x_landed.sem, 16)
            sp.dma_start(x_in[:, 1:TILES, :], x_sample[0].rearrange("(t p) n -> p t n", p=P)).then_inc(x_landed.sem, 16)

            ada_block(0, 0, True)
            ada_block(0, 1, False)
            with sp.Fori(1, ADA_BLOCKS // 2) as pair:
                for b in range(2):
                    ada_block(pair, b, False)
            for b in range(2):
                sp.wait_ge(a_store[b].sem, a_store[b].at(ADA_BLOCKS // 2 - 1))
            for w in range(2):
                for s in range(2):
                    sp.dma_start(mods[:, w, s, :], mod_dram[w, s * D_MODEL:(s + 1) * D_MODEL].rearrange("(p k) -> p k", k=KT)
                                 ).then_inc(mods_in.sem, 16)

            def load(h, n):
                if n < 3:
                    if isinstance(h, int) and h == 0:
                        sp.wait_ge(a_lo.sem, a_lo.at(ADA_BLOCKS - 1))
                    else:
                        if due(wt_lo, h - 1, CHUNKS + n - 2):
                            sp.wait_ge(wt_lo.sem, wt_lo.at(h - 1, CHUNKS + n - 2))
                else:
                    if due(wt_lo, h, n - 2):
                        sp.wait_ge(wt_lo.sem, wt_lo.at(h, n - 2))
                i, half = n // 2, n % 2
                sp.dma_start(raw[:, n % 3, :].rearrange("p (k n) -> p k n", k=KC),
                             w_in_v[:, half * KC:(half + 1) * KC, bass.ds(i * HEAD_COLS + h * P, P)]
                             ).then_inc(landed[n % 3].sem, 16)

            def store_states(h, new_f, new_b, buf, ready, stored):
                sp.wait_ge(ready.sem, ready.at(h))
                for s, new in enumerate((new_f, new_b)):
                    sp.dma_start(new[0, 0, bass.ds(h, 1)].rearrange("h d v -> (h d) v"), buf[:, s, :]).then_inc(stored.sem, 16)

            def items(n, h, prev):
                if n == 4 and prev is not None:
                    store_states(prev, n_ret_f, n_ret_b, rst, r_state, r_state_stored)
                if n == 6 and prev is not None:
                    sp.wait_ge(r_out.sem, r_out.at(prev))
                    sp.dma_start(o_dram[bass.ds(prev, 1)].rearrange("h d t -> (h d) t"), rr).then_inc(r_stored.sem, 16)
                if n == 6 and h is not None:
                    if due(pe_ro, h - 1):
                        sp.wait_ge(pe_ro.sem, pe_ro.at(h - 1))
                    for s, old in enumerate((s_ret_f, s_ret_b)):
                        sp.dma_start(rS0[:, s, :], old[0, 0, bass.ds(h, 1)].rearrange("h d v -> (h d) v")).then_inc(r_S0.sem, 16)
                if n == 8 and prev is not None:
                    store_states(prev, n_hg_f, n_hg_b, hst, h_state, h_state_stored)
                if n == 17 and prev is not None:
                    sp.wait_ge(h_out.sem, h_out.at(prev))
                    sp.dma_start(o_dram[bass.ds(prev + HEADS, 1)].rearrange("h d t -> (h d) t"), hr).then_inc(h_stored.sem, 16)
                if n == 17 and h is not None:
                    if due(pe_ho, h - 1):
                        sp.wait_ge(pe_ho.sem, pe_ho.at(h - 1))
                    for s, old, at in ((0, s_hg_f, 0), (1, s_hg_b, 3)):
                        sp.dma_start(S[:, s, at, :], old[0, 0, bass.ds(h, 1)].rearrange("h d v -> (h d) v")).then_inc(h_S0.sem, 16)

            def head(h, prev):
                for n in range(CHUNKS):
                    load(h, n)
                    items(n, h, prev)

            head(0, None)
            head(1, 0)
            with sp.Fori(2, HEADS) as h:
                head(h, h - 1)
            last = HEADS - 1
            items(4, None, last)
            items(6, None, last)

            def load_o(kt):
                if kt >= STAGES:
                    if due(o_lo, kt - STAGES):
                        sp.wait_ge(o_lo.sem, o_lo.at(kt - STAGES))
                if kt < HEADS:
                    sp.wait_ge(r_stored.sem, r_stored.at(kt))
                else:
                    if due(h_stored, kt - HEADS):
                        sp.wait_ge(h_stored.sem, h_stored.at(kt - HEADS))
                sp.dma_start(o_raw[:, kt % STAGES, :], o_dram[kt]).then_inc(o_landed[kt % STAGES].sem, 16)

            sp.wait_ge(r_stored.sem, r_stored.at(last))
            for kt in range(2 * HEADS - 1):
                load_o(kt)
            items(8, None, last)
            items(17, None, last)
            sp.wait_ge(h_state_stored.sem, h_state_stored.at(last))
            load_o(2 * HEADS - 1)

            def load_w_out(m):
                nb, j = m // WCHUNKS, m % WCHUNKS
                if m < 2:
                    sp.wait_ge(wt_lo.sem, wt_lo.at(last))
                else:
                    if due(d_lo, 0, m - 1):
                        sp.wait_ge(d_lo.sem, d_lo.at(0, m - 1))
                sp.dma_start(raw[:, m % 2, :].rearrange("p (k n) -> p k n", k=WK),
                             w_out_v[:, j * WK:(j + 1) * WK, nb * WIDE:(nb + 1) * WIDE]).then_inc(d_landed[m % 2].sem, 16)

            for m in range(OUT_BLOCKS * WCHUNKS):
                load_w_out(m)
                if m == 3:
                    sp.wait_ge(h_stored.sem, h_stored.at(last))
                    sp.dma_start(x_res[:, 0, :], x_prompt[0]).then_inc(res_in.sem, 16)
                    sp.dma_start(x_res[:, 1:TILES, :], x_sample[0].rearrange("(t p) n -> p t n", p=P)).then_inc(res_in.sem, 16)
                    sp.wait_ge(o_lo.sem, o_lo.at(2 * HEADS - 1))
                    for w in range(2):
                        sp.dma_start(gates[:, w, :], mod_dram[w:w + 1, 2 * D_MODEL:3 * D_MODEL].broadcast_to([P, D_MODEL])
                                     ).then_inc(gates_in.sem, 16)
                    sp.dma_start(fnw, final_norm_w.rearrange("(l n) -> l n", l=1).broadcast_to([P, D_MODEL])).then_inc(gates_in.sem, 16)
            for t in range(TILES):
                sp.wait_ge(y_ready.sem, y_ready.at(t))
                out = y_prompt[0] if t == 0 else y_sample[0, (t - 1) * P:t * P, :]
                sp.dma_start(out, x_res[:, t, :]).then_inc(y_stored.sem, 16)
            sp.wait_ge(y_stored.sem, y_stored.at(TILES - 1))
            sp.wait_ge(r_state_stored.sem, r_state_stored.at(last))
            sp.wait_ge(h_state_stored.sem, h_state_stored.at(last))

        @block.scalar
        def _(act):
            act.preload_act_table_set("natural_log_exp_and_others")
            act.wait_ge(small_in.sem, small_in.at(5))
            act.activation(c_sig, c_raw, ACT.Exp, scale=-1.0).then_inc(c_exp.sem, 1)
            act.activation(lgt, lgr, ACT.Exp).then_inc(lg_act.sem, 1)
            act.wait_ge(lg_steps.sem, lg_steps.at(0, 1))
            act.activation(lg, lgu, ACT.Ln).then_inc(lg_act.sem, 1)
            act.wait_ge(lg_steps.sem, lg_steps.at(0, 10))
            act.activation(lbT, lbT, ACT.Exp).then_inc(lg_act.sem, 1)
            act.wait_ge(lg_steps.sem, lg_steps.at(0, 15))
            act.activation(kdec, kdec, ACT.Exp).then_inc(lg_act.sem, 1)
            act.wait_ge(x_landed.sem, x_landed.at(1))
            for t in range(TILES):
                if t:
                    if due(x_sq, t - 1):
                        act.wait_ge(x_sq.sem, x_sq.at(t - 1))
                act.activation(junk_in, x_in[:, t, :], ACT.Square, accum_out=ssq[:, t:t + 1]).then_inc(x_sq.sem, 1)
            act.wait_ge(rstd_steps.sem, rstd_steps.at(0, 1))
            act.activation(rstd, var, ACT.Ln).then_inc(rstd_act.sem, 1)
            act.wait_ge(rstd_act.sem, rstd_act.at(0))
            act.activation(rstd, rstd, ACT.Exp, scale=-0.5).then_inc(rstd_act.sem, 1)

            def ada_block(pair, b, first):
                nb = 2 * pair + b
                for j in range(WCHUNKS):
                    act.wait_ge(a_landed[j].sem, a_landed[j].at(nb))
                    if not (first and j < 2):
                        if due(a_used, nb, j - 1):
                            act.wait_ge(a_used.sem, a_used.at(nb, j - 1))
                    act.activation(w_hi[:, j % 2, :], ada_raw[:, j, :], ACT.Copy).then_inc(a_hi.sem, 1)
                    if j == 4 and not first:
                        store_row(pair - 1 + b, 1 - b)

            def store_row(pair, b):
                nb = 2 * pair + b
                act.wait_ge(a_row.sem, a_row.at(nb))
                act.dma_start(mod_dram[:, bass.ds(nb * WIDE, WIDE)], mod_row[0:P:P // 2, b, :]).then_inc(a_store[b].sem, 16)

            ada_block(0, 0, True)
            ada_block(0, 1, False)
            with act.Fori(1, ADA_BLOCKS // 2) as pair:
                for b in range(2):
                    ada_block(pair, b, False)
            store_row(ADA_BLOCKS // 2 - 1, 1)

            for k in range(KT):
                act.wait_ge(h_mod.sem, h_mod.at(k))
                act.activation(hT_hi[:, k, :], h_tmp[:, k % 2, :], ACT.Copy).then_inc(h_hi.sem, 1)

            def split(h, n):
                act.wait_ge(landed[n % 3].sem, landed[n % 3].at(h, 16 * (n // 3 + 1)))
                if n >= 2:
                    if due(wt_used, h, n - 1):
                        act.wait_ge(wt_used.sem, wt_used.at(h, n - 1))
                elif isinstance(h, int) and h == 0:
                    act.wait_ge(a_used.sem, a_used.at(ADA_BLOCKS - 1))
                else:
                    if due(wt_used, h - 1, CHUNKS + n - 1):
                        act.wait_ge(wt_used.sem, wt_used.at(h - 1, CHUNKS + n - 1))
                act.activation(w_hi[:, n % 2, :], raw[:, n % 3, :], ACT.Copy).then_inc(wt_hi.sem, 1)

            def projected(h, i):
                act.wait_ge(wt_used.sem, wt_used.at(h, 2 * i + 2))

            def items(n, h, prev):
                if prev is not None:
                    if n == 0:
                        projected(prev, 8)
                        act.wait_ge(pe_ro.sem, pe_ro.at(prev))
                        act.activation(halves(graw), proj(8), ACT.Copy).then_inc(h_graw.sem, 1)
                        act.wait_ge(pe_rss.sem, pe_rss.at(prev))
                        act.activation(rr[:, P:T], ps[:, C, :], ACT.Ln, scale=1.0 / P, bias=eps_col)
                        act.activation(rr[:, 0:P], ps[:, DD, 0:P], ACT.Ln, scale=1.0 / P, bias=eps_col).then_inc(r_rms.sem, 1)
                        act.wait_ge(r_rms.sem, r_rms.at(prev, 1))
                        act.activation(rr, rr, ACT.Exp, scale=-0.5).then_inc(r_rms.sem, 1)
                        act.wait_ge(h_graw.sem, h_graw.at(prev))
                        if due(h_out, prev - 1):
                            act.wait_ge(h_out.sem, h_out.at(prev - 1))
                        act.activation(hsg, graw, ACT.Exp, scale=-1.0).then_inc(h_eg.sem, 1)
                    if n == 1:
                        act.wait_ge(pe_htok.sem, pe_htok.at(prev))
                        if due(pe_ho, prev - 1):
                            act.wait_ge(pe_ho.sem, pe_ho.at(prev - 1))
                        act.activation(htok[:, 1:TILES, :], tiles(ps[:, A, :]), ACT.Copy)
                        act.activation(htok[:, 0, :], ps[:, BB, 0:P], ACT.Copy).then_inc(h_tok.sem, 1)
                    if n == 2:
                        act.wait_ge(pe_hkl.sem, pe_hkl.at(prev))
                        act.activation(kltok[:, 0:4, :], tiles(ps[:, C, :]), ACT.Copy)
                        act.activation(kltok[:, 4:8, :], tiles(ps[:, DD, :]), ACT.Copy).then_inc(h_kltok.sem, 1)
                    if n == 3:
                        act.wait_ge(pe_hu.sem, pe_hu.at(prev))
                        if due(h_state_stored, prev - 1):
                            act.wait_ge(h_state_stored.sem, h_state_stored.at(prev - 1))
                        act.activation(hst[:, 0, :], ps[:, C, 0:P], ACT.Copy)
                        act.activation(hst[:, 1, :], ps[:, DD, 0:P], ACT.Copy).then_inc(h_state.sem, 1)
                    if 1 <= n <= LEVELS:
                        level = n - 1
                        act.wait_ge(xq.sem, xq.at(prev, level + 1))
                        act.wait_ge(xa.sem, xa.at(prev, level + 1))
                        x = XE[:, level % 2]
                        act.activation(x, x, ACT.Exp).then_inc(xe.sem, 1)
                    if n == 11:
                        act.wait_ge(pe_ho.sem, pe_ho.at(prev))
                        act.activation(hsq[:, P:T], ps[:, C, :], ACT.Square)
                        act.activation(hsq[:, 0:P], ps[:, DD, 0:P], ACT.Square).then_inc(h_sq.sem, 1)
                    if n == 12:
                        act.wait_ge(pe_hss.sem, pe_hss.at(prev))
                        act.activation(hr[:, P:T], ps[:, A, :], ACT.Ln, scale=1.0 / P, bias=eps_col)
                        act.activation(hr[:, 0:P], ps[:, BB, 0:P], ACT.Ln, scale=1.0 / P, bias=eps_col).then_inc(h_rms.sem, 1)
                        act.wait_ge(h_rms.sem, h_rms.at(prev, 1))
                        act.activation(hr, hr, ACT.Exp, scale=-0.5).then_inc(h_rms.sem, 1)
                if h is None:
                    return
                if n == 2:
                    projected(h, 0)
                    if due(pe_ro, h - 1):
                        act.wait_ge(pe_ro.sem, pe_ro.at(h - 1))
                    act.activation(halves(rq), proj(0), ACT.Copy).then_inc(r_q.sem, 1)
                if n == 4:
                    projected(h, 1)
                    act.activation(halves(rk), proj(1), ACT.Copy, scale=DK_SCALE).then_inc(r_k.sem, 1)
                if n == 6:
                    projected(h, 2)
                    act.activation(halves(rvT), proj(2), ACT.Copy).then_inc(r_v.sem, 1)
                if n == 8:
                    projected(h, 3)
                    if due(r_out, h - 1):
                        act.wait_ge(r_out.sem, r_out.at(h - 1))
                    act.activation(halves(rsg), proj(3), ACT.Exp, scale=-1.0).then_inc(r_eg.sem, 1)
                if n == 10:
                    projected(h, 4)
                    if due(pe_level, h - 1):
                        act.wait_ge(pe_level.sem, pe_level.at(h - 1))
                    act.activation(halves(hq), proj(4), ACT.Copy).then_inc(h_q.sem, 1)
                if n == 12 or n == 14:
                    s = (n - 12) // 2
                    projected(h, 5 + s)
                    if due(pe_ho, h - 1):
                        act.wait_ge(pe_ho.sem, pe_ho.at(h - 1))
                    act.activation(halves(F[:, s, :]), proj(5 + s), ACT.Exp, scale=-1.0).then_inc(h_ez.sem, 1)
                if n == 16:
                    projected(h, 7)
                    if due(pe_htok, h - 1):
                        act.wait_ge(pe_htok.sem, pe_htok.at(h - 1))
                    act.activation(halves(hvT), proj(7), ACT.Copy).then_inc(h_v.sem, 1)
                if n == 13:
                    act.wait_ge(strip_x.sem, strip_x.at(h, 3))
                    act.activation(strip, strip, ACT.Exp).then_inc(strip_e.sem, 1)
                    if due(h_silu, h - 1):
                        act.wait_ge(h_silu.sem, h_silu.at(h - 1))
                    for s in range(2):
                        col = bass.ds(s * HEADS + h, 1)
                        i = act.activation(rqd[:, s, :], rel[:, REL - LAT:REL], ACT.Exp, bias=dbias[:, col],
                                           scale=(lg if s == 0 else nlg)[:, col])
                    i.then_inc(r_dec.sem, 1)
                if n == 14:
                    act.wait_ge(pe_rtok.sem, pe_rtok.at(h))
                    act.activation(rtok[:, 1:TILES, :], tiles(ps[:, C, :]), ACT.Copy)
                    act.activation(rtok[:, 0, :], ps[:, DD, 0:P], ACT.Copy).then_inc(r_tok.sem, 1)
                    for s in range(2):
                        i = act.activation(kts[:, s, :], ps[:, DD, P:2 * P], ACT.Copy, scale=kdec[:, bass.ds(s * HEADS + h, 1)])
                    i.then_inc(r_tok.sem, 1)
                if n == 14 or n == 16:
                    s = (n - 14) // 2
                    act.wait_ge(h_gate.sem, h_gate.at(h, 5 * s + 5))
                    act.activation(F[:, s, :], F[:, s, :], ACT.Ln).then_inc(h_log.sem, 1)
                if n == 17:
                    act.wait_ge(pe_ro.sem, pe_ro.at(h))
                    act.activation(rsq[:, P:T], ps[:, A, :], ACT.Square)
                    act.activation(rsq[:, 0:P], ps[:, BB, 0:P], ACT.Square).then_inc(r_sq.sem, 1)
                    if due(r_state_stored, h - 1):
                        act.wait_ge(r_state_stored.sem, r_state_stored.at(h - 1))
                    act.activation(rst, ps[:, DD, 0:2 * P].rearrange("p (s n) -> p s n", s=2), ACT.Copy).then_inc(r_state.sem, 1)
                    act.wait_ge(h_scan.sem, h_scan.at(h))
                    act.activation(F, B, ACT.Exp).then_inc(h_eb.sem, 1)
                    act.wait_ge(h_klx.sem, h_klx.at(h))
                    act.activation(KL, KL, ACT.Exp).then_inc(h_ekl.sem, 1)

            def head(h, prev):
                for n in range(CHUNKS):
                    split(h, n)
                    if n == 0:
                        if prev is not None:
                            items(CHUNKS - 1, prev, None)
                    else:
                        items(n - 1, h, prev)

            head(0, None)
            head(1, 0)
            with act.Fori(2, HEADS) as h:
                head(h, h - 1)
            last = HEADS - 1
            items(CHUNKS - 1, last, None)

            def split_o(kt):
                act.wait_ge(o_landed[kt % STAGES].sem, o_landed[kt % STAGES].at(kt // STAGES))
                if kt == 0:
                    act.wait_ge(wt_used.sem, wt_used.at(last))
                act.activation(hT_hi[:, kt, :], o_raw[:, kt % STAGES, :], ACT.Copy).then_inc(o_hi.sem, 1)

            for n in range(13):
                items(n, None, last)
                if n >= 2:
                    split_o(n - 2)
            for kt in range(11, 2 * HEADS):
                split_o(kt)

            def square(m):
                nb, t = m // TILES, evac_order(m // TILES)[m % TILES]
                act.wait_ge(d_ev.sem, d_ev.at(0, m + 1))
                if m:
                    act.wait_ge(d_sq.sem, d_sq.at(0, m))
                act.activation(junk_out, x_res[:, t, nb * WIDE:(nb + 1) * WIDE], ACT.Square,
                               accum_out=ssq4[:, t, nb:nb + 1]).then_inc(d_sq.sem, 1)

            for m in range(OUT_BLOCKS * WCHUNKS):
                nb, j = m // WCHUNKS, m % WCHUNKS
                act.wait_ge(d_landed[m % 2].sem, d_landed[m % 2].at(m // 2))
                if m >= 2:
                    if due(d_used, 0, m - 1):
                        act.wait_ge(d_used.sem, d_used.at(0, m - 1))
                act.activation(w_hi[:, m % 2, :], raw[:, m % 2, :], ACT.Copy).then_inc(d_hi.sem, 1)
                if nb and 2 <= j < 2 + TILES:
                    square((nb - 1) * TILES + j - 2)
            for t in range(TILES):
                square((OUT_BLOCKS - 1) * TILES + t)
            act.wait_ge(fin_steps.sem, fin_steps.at(0, 2))
            act.activation(rstd_o, var_o, ACT.Ln).then_inc(fin_act.sem, 1)
            act.wait_ge(fin_act.sem, fin_act.at(0))
            act.activation(rstd_o, rstd_o, ACT.Exp, scale=-0.5).then_inc(fin_act.sem, 1)

        @block.vector
        def _(dve):
            v = nc.vector
            v.memset(eps_col, EPS)

            def newton(out, x, tmp, step):
                step(v.tensor_tensor(tmp, out, out, ALU.mult))
                step(v.tensor_tensor(tmp, tmp, x, ALU.mult))
                step(v.tensor_scalar(tmp, tmp, -0.5, 1.5, ALU.mult, ALU.add))
                step(v.tensor_tensor(out, out, tmp, ALU.mult))

            def c_step(i, count=[0]):
                count[0] += 1
                i.then_inc(c_steps.sem, 1)
                dve.wait_ge(c_steps.sem, c_steps.at(0, count[0]))

            dve.wait_ge(c_exp.sem, c_exp.at(0))
            c_step(v.tensor_scalar(c_sig, c_sig, 1.0, None, ALU.add))
            c_step(v.reciprocal(c_sig, c_sig))
            c_step(v.tensor_tensor(c_sig, c_sig, c_raw, ALU.mult))
            for w in range(2):
                i = v.tensor_copy(hT_hi[:, :, w * 64:w * 64 + 64], c_sig[:, w, :].unsqueeze(2).broadcast_to([P, KT, 64]))
            c_step(i)
            for w in range(2):
                i = v.tensor_tensor(hT_lo[:, :, w * 64:w * 64 + 64], c_sig[:, w, :].unsqueeze(2).broadcast_to([P, KT, 64]),
                                    hT_hi[:, :, w * 64:w * 64 + 64].bitcast(F32), ALU.subtract)
            i.then_inc(cs_ready.sem, 1)

            def lg_step(i, count=[0]):
                count[0] += 1
                i.then_inc(lg_steps.sem, 1)
                dve.wait_ge(lg_steps.sem, lg_steps.at(0, count[0]))

            dve.wait_ge(lg_act.sem, lg_act.at(0))
            lg_step(v.tensor_scalar(lgu, lgt, -1.0, 1.0, ALU.mult, ALU.add))
            lg_step(v.tensor_scalar(nlg, lgu, -1.0, 1.0, ALU.mult, ALU.add))
            lg_step(v.tensor_tensor(nlg, nlg, lgt, ALU.subtract))
            lg_step(v.reciprocal(lgu2, lgu))
            lg_step(v.tensor_tensor(nlg, nlg, lgu2, ALU.mult))
            dve.wait_ge(lg_act.sem, lg_act.at(1))
            lg_step(v.tensor_tensor(lg, lg, nlg, ALU.add))
            lg_step(v.tensor_scalar(nlg, lg, -1.0, None, ALU.mult))
            dve.wait_ge(lb_pe.sem, lb_pe.at(0))
            lbp = ps[:, A, 0:4 * HEADS].rearrange("p (s l h) -> p s l h", s=2, l=2)
            lbv = lbT.rearrange("p (s l h) -> p s l h", s=2, l=2)
            lbm3 = lbm.rearrange("p (s h) -> p s h", s=2)
            lg_step(v.tensor_copy(lbT, ps[:, A, 0:4 * HEADS]))
            lg_step(v.tensor_tensor(lbm3, lbv[:, :, 0, :], lbv[:, :, 1, :], ALU.max))
            for l in range(2):
                i = v.tensor_tensor(lbv[:, :, l, :], lbv[:, :, l, :], lbm3, ALU.subtract)
            lg_step(i)
            dve.wait_ge(lg_act.sem, lg_act.at(2))
            lg_step(v.tensor_tensor(lbm3, lbv[:, :, 0, :], lbv[:, :, 1, :], ALU.add))
            lg_step(v.reciprocal(lbm, lbm))
            lg_step(v.tensor_tensor(lb.rearrange("p (s h) -> p s h", s=2), lbv[:, :, 0, :], lbm3, ALU.mult))
            lg_step(v.tensor_scalar(oml, lb, -1.0, 1.0, ALU.mult, ALU.add))
            for s in range(2):
                g = slice(s * HEADS, (s + 1) * HEADS)
                v.tensor_scalar(dbias[:, g], lg[:, g], con[:, C_POS + s:C_POS + s + 1], None, ALU.mult)
                i = v.tensor_scalar(kdec[:, g], lg[:, g], con[:, C_POS + 2 + s:C_POS + 3 + s], None, ALU.mult)
            lg_step(i)

            def rstd_step(i, count=[0]):
                count[0] += 1
                i.then_inc(rstd_steps.sem, 1)
                dve.wait_ge(rstd_steps.sem, rstd_steps.at(0, count[0]))

            dve.wait_ge(x_sq.sem, x_sq.at(TILES - 1))
            rstd_step(v.tensor_scalar(var, ssq, 1.0 / D_MODEL, EPS, ALU.mult, ALU.add))
            dve.wait_ge(rstd_act.sem, rstd_act.at(1))
            newton(rstd, var, newt, rstd_step)
            for t in range(TILES):
                v.tensor_scalar(x_in[:, t, :], x_in[:, t, :], rstd[:, t:t + 1], None, ALU.mult).then_inc(x_scaled.sem, 1)

            def ada_block(pair, b, first):
                nb = 2 * pair + b
                for j in range(WCHUNKS):
                    dve.wait_ge(a_hi.sem, a_hi.at(nb, j + 1))
                    v.tensor_tensor(w_lo[:, j % 2, :], ada_raw[:, j, :], w_hi[:, j % 2, :].bitcast(F32),
                                    ALU.subtract).then_inc(a_lo.sem, 1)
                    if j == 1 and not first:
                        mod_block(pair - 1 + b, 1 - b)

            def mod_block(pair, b):
                dve.wait_ge(a_used.sem, a_used.at(2 * pair + b))
                dve.wait_ge(a_bias[b].sem, a_bias[b].at(pair))
                if due(a_store[b], pair - 1):
                    dve.wait_ge(a_store[b].sem, a_store[b].at(pair - 1))
                v.tensor_tensor(mod_row[:, b, :], ps[:, b, :], b_row[:, b, :], ALU.add).then_inc(a_row.sem, 1)

            ada_block(0, 0, True)
            ada_block(0, 1, False)
            with dve.Fori(1, ADA_BLOCKS // 2) as pair:
                for b in range(2):
                    ada_block(pair, b, False)
            mod_block(ADA_BLOCKS // 2 - 1, 1)

            dve.wait_ge(mods_in.sem, mods_in.at(3))
            for w in range(2):
                i = v.scalar_tensor_tensor(out=mods[:, w, 1, :], in0=mods[:, w, 1, :], scalar=1.0, in1=nw,
                                           op0=ALU.add, op1=ALU.mult)
            i.then_inc(mods_ready.sem, 1)
            dve.wait_ge(mods_ready.sem, mods_ready.at(0))

            def low_part(k):
                dve.wait_ge(h_hi.sem, h_hi.at(k))
                v.tensor_tensor(hT_lo[:, k, :], h_tmp[:, k % 2, :], hT_hi[:, k, :].bitcast(F32), ALU.subtract).then_inc(h_lo.sem, 1)

            for k in range(KT):
                dve.wait_ge(x_tr.sem, x_tr.at(k))
                if k >= 2:
                    if due(h_lo, k - 2):
                        dve.wait_ge(h_lo.sem, h_lo.at(k - 2))
                bank = 4 + 2 * (k % 2)
                for w, src, dst in ((1, ps[:, bank, :], h_tmp[:, k % 2, P:T]), (0, ps[:, bank + 1, 0:P], h_tmp[:, k % 2, 0:P])):
                    i = v.tensor_scalar(dst, src, mods[:, w, 1, k:k + 1], mods[:, w, 0, k:k + 1], ALU.mult, ALU.add)
                i.then_inc(h_mod.sem, 1)
                if k:
                    low_part(k - 1)
            low_part(KT - 1)

            def split(h, n):
                dve.wait_ge(wt_hi.sem, wt_hi.at(h, n + 1))
                v.tensor_tensor(w_lo[:, n % 2, :], raw[:, n % 3, :], w_hi[:, n % 2, :].bitcast(F32),
                                ALU.subtract).then_inc(wt_lo.sem, 1)

            def reciprocal_half(buf, half, signal):
                part = buf[:, half * HALF:(half + 1) * HALF]
                v.reciprocal(part, part).then_inc(signal.sem, 1)

            def items(n, h, prev):
                if prev is not None:
                    if n == 0:
                        dve.wait_ge(r_rms.sem, r_rms.at(prev, 2))
                        v.tensor_tensor(rr[:, P:T], ps[:, A, :], rr[:, P:T], ALU.mult)
                        v.tensor_tensor(rr[:, 0:P], ps[:, BB, 0:P], rr[:, 0:P], ALU.mult).then_inc(r_out.sem, 1)
                        dve.wait_ge(r_out.sem, r_out.at(prev, 1))
                        dve.wait_ge(r_silu.sem, r_silu.at(prev))
                        v.tensor_tensor(rr, rr, rsg, ALU.mult).then_inc(r_out.sem, 1)
                        dve.wait_ge(h_eb.sem, h_eb.at(prev))
                        v.tensor_copy(dec[:, 0, :], tiles(F[:, 0, :])[:, :, P - 1])
                        v.tensor_copy(dec[:, 1, :], tiles(F[:, 1, :])[:, :, 0]).then_inc(h_dec.sem, 1)
                        dve.wait_ge(h_dec.sem, h_dec.at(prev))
                        for s in range(2):
                            i = v.tensor_tensor(F[:, s, :], F[:, s, :], hq, ALU.mult)
                        i.then_inc(h_qr.sem, 1)
                    if n == 1:
                        dve.wait_ge(h_eg.sem, h_eg.at(prev))
                        v.tensor_scalar(hsg, hsg, 1.0, None, ALU.add).then_inc(h_silu.sem, 1)
                        dve.wait_ge(h_silu.sem, h_silu.at(prev, 1))
                        reciprocal_half(hsg, 0, h_silu)
                    if n == 2:
                        reciprocal_half(hsg, 1, h_silu)
                        dve.wait_ge(h_silu.sem, h_silu.at(prev, 3))
                        v.tensor_tensor(hsg, hsg, graw, ALU.mult).then_inc(h_silu.sem, 1)
                    if 1 <= n <= LEVELS:
                        level = n - 1
                        half = P >> (level + 1)
                        buf = XE[:, level % 2, 0, :]
                        bf, bb, x = blocks(B[:, 0, :], level), blocks(B[:, 1, :], level), blocks(buf, level)
                        nblk = T // (2 * half)
                        if due(pe_level, prev, level - 1):
                            dve.wait_ge(pe_level.sem, pe_level.at(prev, level - 1))
                        v.tensor_tensor(x[:, :, half:2 * half], bf[:, :, half:2 * half],
                                        bf[:, :, half - 1:half].broadcast_to([P, nblk, half]), ALU.subtract)
                        v.tensor_tensor(x[:, :, 0:half], bb[:, :, 0:half],
                                        bb[:, :, half:half + 1].broadcast_to([P, nblk, half]), ALU.subtract).then_inc(xq.sem, 1)
                        dve.wait_ge(xe.sem, xe.at(prev, level + 1))
                        v.tensor_tensor(buf, buf, hq, ALU.mult).then_inc(lq.sem, 1)
                    if n == 3:
                        dve.wait_ge(pe_hu.sem, pe_hu.at(prev))
                        dve.wait_ge(h_S0.sem, h_S0.at(prev))
                        if due(pe_ho, prev - 1):
                            dve.wait_ge(pe_ho.sem, pe_ho.at(prev - 1))
                        for i in range(3):
                            v.scalar_tensor_tensor(out=S[:, 0, i + 1, :], in0=S[:, 0, i, :], scalar=dec[:, 0, i + 1:i + 2],
                                                   in1=ps[:, C, tile_cols(i + 1)], op0=ALU.mult, op1=ALU.add)
                            v.scalar_tensor_tensor(out=S[:, 1, 2 - i, :], in0=S[:, 1, 3 - i, :], scalar=dec[:, 1, 4 - i:5 - i],
                                                   in1=ps[:, DD, tile_cols(3 - i)], op0=ALU.mult, op1=ALU.add).then_inc(h_S.sem, 1)
                            dve.wait_ge(h_S.sem, h_S.at(prev, i + 1))
                    if 3 <= n < 3 + PRODUCTS:
                        level = n - 3
                        scored, placed = pe_level.at(prev, level + 1), h_sT.at(prev, level)
                        if not isinstance(prev, int):
                            scored, placed = dve.to_reg(scored), dve.to_reg(placed)
                        if level:
                            dve.wait_ge(con_in.sem, con_in.at(0))
                        dve.wait_ge(pe_level.sem, scored)
                        out = tiles(hsT[:, P:T])
                        if level == 0:
                            if due(pe_ho, prev - 1):
                                dve.wait_ge(pe_ho.sem, pe_ho.at(prev - 1))
                            v.tensor_copy(out, tiles(ps[:, A, :]))
                            v.tensor_copy(hsT[:, 0:P], ps[:, BB, 0:P]).then_inc(h_sT.sem, 1)
                        else:
                            dve.wait_ge(h_sT.sem, placed)
                            v.copy_predicated(out, mask(level).unsqueeze(1).broadcast_to([P, TILES - 1, P]), tiles(ps[:, A, :]))
                            v.copy_predicated(hsT[:, 0:P], mask(level), ps[:, BB, 0:P]).then_inc(h_sT.sem, 1)
                    if n == 12:
                        dve.wait_ge(h_rms.sem, h_rms.at(prev, 2))
                        v.scalar_tensor_tensor(out=hr[:, P:T], in0=ps[:, C, :], scalar=hnw, in1=hr[:, P:T], op0=ALU.mult, op1=ALU.mult)
                        v.scalar_tensor_tensor(out=hr[:, 0:P], in0=ps[:, DD, 0:P], scalar=hnw, in1=hr[:, 0:P],
                                               op0=ALU.mult, op1=ALU.mult).then_inc(h_out.sem, 1)
                        dve.wait_ge(h_out.sem, h_out.at(prev, 1))
                        v.tensor_tensor(hr, hr, hsg, ALU.mult).then_inc(h_out.sem, 1)
                if h is None:
                    return
                if n == 8:
                    dve.wait_ge(r_eg.sem, r_eg.at(h))
                    v.tensor_scalar(rsg, rsg, 1.0, None, ALU.add).then_inc(r_silu.sem, 1)
                    dve.wait_ge(r_silu.sem, r_silu.at(h, 1))
                    reciprocal_half(rsg, 0, r_silu)
                if n == 9:
                    reciprocal_half(rsg, 1, r_silu)
                    dve.wait_ge(r_silu.sem, r_silu.at(h, 3))
                    v.tensor_tensor(halves(rsg), halves(rsg), proj(3), ALU.mult).then_inc(r_silu.sem, 1)
                if n == 12:
                    tmp = sT[:, 0:REL]
                    if due(r_sT, h - 1):
                        dve.wait_ge(r_sT.sem, r_sT.at(h - 1))
                    if due(pe_rss, h - 1):
                        dve.wait_ge(pe_rss.sem, pe_rss.at(h - 1))
                    v.tensor_scalar(strip, rel, 0.0, lg[:, bass.ds(h, 1)], ALU.max, ALU.mult).then_inc(strip_x.sem, 1)
                    v.tensor_scalar(tmp, rel, 0.0, nlg[:, bass.ds(h + HEADS, 1)], ALU.min, ALU.mult).then_inc(strip_x.sem, 1)
                    dve.wait_ge(strip_x.sem, strip_x.at(h, 2))
                    v.tensor_tensor(strip, strip, tmp, ALU.add).then_inc(strip_x.sem, 1)
                if n == 13:
                    dve.wait_ge(pe_rswap.sem, pe_rswap.at(h))
                    if due(r_stored, h - 1):
                        dve.wait_ge(r_stored.sem, r_stored.at(h - 1))
                    v.tensor_tensor(rope_q, ps[:, A, :], sin, ALU.mult)
                    v.tensor_tensor(rope_k, ps[:, BB, :], sin, ALU.mult).then_inc(rope_sin.sem, 1)
                    dve.wait_ge(rope_sin.sem, rope_sin.at(h))
                    dve.wait_ge(rope_cos.sem, rope_cos.at(h))
                    v.tensor_tensor(rq[:, P:T], rq[:, P:T], rope_q, ALU.add)
                    v.tensor_tensor(rk[:, P:T], rk[:, P:T], rope_k, ALU.add).then_inc(roped.sem, 1)
                    dve.wait_ge(strip_e.sem, strip_e.at(h))
                    diag = strip[:, REL - LAT:REL - LAT + P]
                    v.tensor_tensor(diag, diag, ident, ALU.add).then_inc(strip_i.sem, 1)
                if 12 <= n <= 15:
                    s, odd = (n - 12) // 2, n % 2
                    buf, at = F[:, s, :], 5 * s
                    col = bass.ds(s * HEADS + h, 1)
                    if odd == 0:
                        dve.wait_ge(h_ez.sem, h_ez.at(h, s + 1))
                        v.tensor_scalar(buf, buf, 1.0, None, ALU.add).then_inc(h_gate.sem, 1)
                        dve.wait_ge(h_gate.sem, h_gate.at(h, at + 1))
                        reciprocal_half(buf, 0, h_gate)
                    else:
                        reciprocal_half(buf, 1, h_gate)
                        dve.wait_ge(h_gate.sem, h_gate.at(h, at + 3))
                        v.tensor_scalar(buf, buf, oml[:, col], lb[:, col], ALU.mult, ALU.add).then_inc(h_gate.sem, 1)
                        dve.wait_ge(h_gate.sem, h_gate.at(h, at + 4))
                        if due(la, h - 1):
                            dve.wait_ge(la.sem, la.at(h - 1))
                        v.tensor_scalar(K[:, s, :], buf, -1.0, 1.0, ALU.mult, ALU.add).then_inc(h_gate.sem, 1)
                if n == 15 or n == 16:
                    if n == 15:
                        dve.wait_ge(strip_i.sem, strip_i.at(h))
                        dve.wait_ge(roped.sem, roped.at(h))
                    for jt in range(2 * (n - 15), 2 * (n - 15) + 2):
                        dve.wait_ge(pe_rs.sem, pe_rs.at(h, jt + 1))
                        off = REL - LAT - jt * P
                        v.tensor_tensor(sT[:, jt * LAT:(jt + 1) * LAT], ps[:, A + jt % 2, :], strip[:, off:off + LAT],
                                        ALU.mult).then_inc(r_sT.sem, 1)
                    if n == 16:
                        dve.wait_ge(pe_rs.sem, pe_rs.at(h, 5))
                        v.tensor_tensor(sT[:, 4 * LAT:4 * LAT + P], ps[:, C, 0:P], strip[:, REL - LAT:REL - LAT + P],
                                        ALU.mult).then_inc(r_sT.sem, 1)
                if n == 15:
                    dve.wait_ge(h_log.sem, h_log.at(h, 1))
                    v.tensor_tensor_scan(B[:, 0, :], reset, F[:, 0, :], 0.0, ALU.mult, ALU.add).then_inc(h_scan.sem, 1)
                if n == 17:
                    dve.wait_ge(h_log.sem, h_log.at(h, 2))
                    v.tensor_tensor_scan(B[:, 1, ::-1], reset, F[:, 1, ::-1], 0.0, ALU.mult, ALU.add).then_inc(h_scan.sem, 1)
                    dve.wait_ge(h_scan.sem, h_scan.at(h))
                    if due(h_stored, h - 1):
                        dve.wait_ge(h_stored.sem, h_stored.at(h - 1))
                    bf, bb = tiles(B[:, 0, :]), tiles(B[:, 1, :])
                    v.tensor_tensor(tiles(KL[:, 0, :]), bf[:, :, P - 1:P].broadcast_to([P, TILES, P]), bf, ALU.subtract)
                    v.tensor_tensor(tiles(KL[:, 1, :]), bb[:, :, 0:1].broadcast_to([P, TILES, P]), bb, ALU.subtract).then_inc(h_klx.sem, 1)

            def head(h, prev):
                for n in range(CHUNKS):
                    split(h, n)
                    if n == 0:
                        if prev is not None:
                            items(CHUNKS - 1, prev, None)
                    else:
                        items(n - 1, h, prev)

            head(0, None)
            head(1, 0)
            with dve.Fori(2, HEADS) as h:
                head(h, h - 1)
            last = HEADS - 1
            items(CHUNKS - 1, last, None)

            def split_o(kt):
                dve.wait_ge(o_hi.sem, o_hi.at(kt))
                v.tensor_tensor(hT_lo[:, kt, :], o_raw[:, kt % STAGES, :], hT_hi[:, kt, :].bitcast(F32),
                                ALU.subtract).then_inc(o_lo.sem, 1)

            for n in range(13):
                items(n, None, last)
                if n >= 2:
                    split_o(n - 2)
            for kt in range(11, 2 * HEADS):
                split_o(kt)

            def gate_part(m):
                nb, t = m // TILES, evac_order(m // TILES)[m % TILES]
                dve.wait_ge(d_used.sem, d_used.at(nb))
                if m == 0:
                    dve.wait_ge(gates_in.sem, gates_in.at(2))
                    dve.wait_ge(res_in.sem, res_in.at(1))
                if m >= 2:
                    if due(d_ev, 0, m - 1):
                        dve.wait_ge(d_ev.sem, d_ev.at(0, m - 1))
                v.tensor_tensor(gated[:, m % 2, :], ps[:, out_bank(nb, t), :],
                                gates[:, 0 if t == 0 else 1, nb * WIDE:(nb + 1) * WIDE], ALU.mult).then_inc(d_gated.sem, 1)

            def add_part(m):
                nb, t = m // TILES, evac_order(m // TILES)[m % TILES]
                dve.wait_ge(d_gated.sem, d_gated.at(0, m + 1))
                x = x_res[:, t, nb * WIDE:(nb + 1) * WIDE]
                v.tensor_tensor(x, x, gated[:, m % 2, :], ALU.add).then_inc(d_ev.sem, 1)

            def finish_block(nb):
                for m in range(nb * TILES, (nb + 1) * TILES):
                    gate_part(m)
                    if m > nb * TILES:
                        add_part(m - 1)
                add_part((nb + 1) * TILES - 1)

            for m in range(OUT_BLOCKS * WCHUNKS):
                nb, j = m // WCHUNKS, m % WCHUNKS
                dve.wait_ge(d_hi.sem, d_hi.at(0, m + 1))
                v.tensor_tensor(w_lo[:, m % 2, :], raw[:, m % 2, :], w_hi[:, m % 2, :].bitcast(F32), ALU.subtract).then_inc(d_lo.sem, 1)
                if nb and j == 1:
                    finish_block(nb - 1)
            finish_block(OUT_BLOCKS - 1)

            def fin_step(i, count=[0]):
                count[0] += 1
                i.then_inc(fin_steps.sem, 1)
                dve.wait_ge(fin_steps.sem, fin_steps.at(0, count[0]))

            dve.wait_ge(d_sq.sem, d_sq.at(OUT_BLOCKS - 1))
            fin_step(v.reduce_sum(ssq_out, ssq4, AX_X))
            fin_step(v.tensor_scalar(var_o, ssq_out, 1.0 / D_MODEL, EPS, ALU.mult, ALU.add))
            dve.wait_ge(fin_act.sem, fin_act.at(1))
            newton(rstd_o, var_o, newt_o, fin_step)
            for t in range(TILES):
                v.scalar_tensor_tensor(out=x_res[:, t, :], in0=x_res[:, t, :], scalar=rstd_o[:, t:t + 1], in1=fnw,
                                       op0=ALU.mult, op1=ALU.mult).then_inc(y_ready.sem, 1)

        @block.gpsimd
        def _(pool):
            g = nc.gpsimd

            def items(n, h, prev):
                if prev is not None:
                    if n == 0:
                        pool.wait_ge(h_ekl.sem, h_ekl.at(prev))
                        g.tensor_tensor(KL, KL, K, ALU.mult).then_inc(h_kl.sem, 1)
                    if 1 <= n <= LEVELS:
                        level = n - 1
                        half = P >> (level + 1)
                        buf = XE[:, level % 2, 1, :]
                        bf, bb, x = blocks(B[:, 0, :], level), blocks(B[:, 1, :], level), blocks(buf, level)
                        kf, kb = blocks(K[:, 0, :], level), blocks(K[:, 1, :], level)
                        nblk = T // (2 * half)
                        left, right = slice(0, half), slice(half, 2 * half)
                        pool.wait_ge(h_scan.sem, h_scan.at(prev))
                        if due(pe_level, prev, level - 1):
                            pool.wait_ge(pe_level.sem, pe_level.at(prev, level - 1))
                        g.tensor_tensor(x[:, :, left], bf[:, :, half - 1:half].broadcast_to([P, nblk, half]), bf[:, :, left], ALU.subtract)
                        g.tensor_tensor(x[:, :, right], bb[:, :, half:half + 1].broadcast_to([P, nblk, half]), bb[:, :, right],
                                        ALU.subtract).then_inc(xa.sem, 1)
                        pool.wait_ge(xe.sem, xe.at(prev, level + 1))
                        g.tensor_tensor(x[:, :, left], x[:, :, left], kf[:, :, left], ALU.mult)
                        g.tensor_tensor(x[:, :, right], x[:, :, right], kb[:, :, right], ALU.mult).then_inc(la.sem, 1)
                    if n == LEVELS + 1:
                        if due(pe_level, prev, LEVELS - 1):
                            pool.wait_ge(pe_level.sem, pe_level.at(prev, LEVELS - 1))
                        g.tensor_tensor(XE[:, 1, 1, :], K[:, 0, :], K[:, 1, :], ALU.add).then_inc(la.sem, 1)
                if h is None:
                    return
                if n == 13:
                    pool.wait_ge(pe_rswap.sem, pe_rswap.at(h))
                    g.tensor_tensor(rq[:, P:T], rq[:, P:T], cos, ALU.mult)
                    g.tensor_tensor(rk[:, P:T], rk[:, P:T], cos, ALU.mult).then_inc(rope_cos.sem, 1)
                if n == 15:
                    pool.wait_ge(r_dec.sem, r_dec.at(h))
                    pool.wait_ge(roped.sem, roped.at(h))
                    for s in range(2):
                        i = g.tensor_tensor(rqd[:, s, :], rqd[:, s, :], rq[:, P:T], ALU.mult)
                    i.then_inc(r_qdec.sem, 1)

            def head(h, prev):
                for n in range(CHUNKS):
                    items(n, h, prev)

            head(0, None)
            head(1, 0)
            with pool.Fori(2, HEADS) as h:
                head(h, h - 1)
            for n in range(LEVELS + 2):
                items(n, None, HEADS - 1)

        @block.tensor
        def _(pe):
            mm = nc.tensor.matmul
            pe.wait_ge(con_in.sem, con_in.at(0))
            pe.wait_ge(small_in.sem, small_in.at(5))
            nc.tensor.transpose(ps[:, A, 0:4 * HEADS], lb_in, con[0:4 * HEADS, C_IDENT:C_IDENT + 4 * HEADS]).then_inc(lb_pe.sem, 1)
            pe.wait_ge(cs_ready.sem, cs_ready.at(0))

            def ada_block(pair, b, first):
                nb = 2 * pair + b
                for j in range(WCHUNKS):
                    pe.wait_ge(a_lo.sem, a_lo.at(nb, j + 1))
                    if j == 0:
                        if due(a_row, nb - 2):
                            pe.wait_ge(a_row.sem, a_row.at(nb - 2))
                    for kk in range(WK):
                        k = j * WK + kk
                        w = slice(kk * WIDE, (kk + 1) * WIDE)
                        cs_hi, cs_lo = hT_hi[:, k, 0:P], hT_lo[:, k, 0:P]
                        mm(ps[:, b, :], cs_hi, w_hi[:, j % 2, w], start=k == 0, stop=False)
                        mm(ps[:, b, :], cs_hi, w_lo[:, j % 2, w], start=False, stop=False)
                        i = mm(ps[:, b, :], cs_lo, w_hi[:, j % 2, w], start=False, stop=k == KT - 1)
                    i.then_inc(a_used.sem, 1)

            ada_block(0, 0, True)
            ada_block(0, 1, False)
            with pe.Fori(1, ADA_BLOCKS // 2) as pair:
                for b in range(2):
                    ada_block(pair, b, False)

            pe.wait_ge(x_scaled.sem, x_scaled.at(TILES - 1))
            for k in range(KT):
                bank = 4 + 2 * (k % 2)
                if k >= 2:
                    if due(h_mod, k - 2):
                        pe.wait_ge(h_mod.sem, h_mod.at(k - 2))
                for t in range(1, TILES):
                    nc.tensor.transpose(ps[:, bank, tile_cols(t - 1)], x_in[:, t, k::KT], ident)
                nc.tensor.transpose(ps[:, bank + 1, 0:P], x_in[:, 0, k::KT], ident).then_inc(x_tr.sem, 1)
            pe.wait_ge(h_lo.sem, h_lo.at(KT - 1))

            freed = {0: (h_graw, 1, None), 1: (h_v, 1, None), 2: (r_q, 0, None), 3: (r_k, 0, None), 4: (r_v, 0, None),
                     5: (r_silu, 0, 4), 6: (h_q, 0, None), 7: (h_ez, 0, 1), 8: (h_ez, 0, 2)}

            def chunk(h, n):
                i, half = n // 2, n % 2
                pe.wait_ge(wt_lo.sem, wt_lo.at(h, n + 1))
                if half == 0:
                    signal, back, k = freed[i]
                    if due(signal, h - back, k):
                        pe.wait_ge(signal.sem, signal.at(h - back, k))
                out = [ps[:, 2 * (i % 2) + s, 0:HALF] for s in range(2)]
                for kk in range(KC):
                    k = half * KC + kk
                    w = slice(kk * P, (kk + 1) * P)
                    for step, (wt, x) in enumerate(((w_hi, hT_hi), (w_hi, hT_lo), (w_lo, hT_hi))):
                        for s in range(2):
                            ins = mm(out[s], wt[:, n % 2, w], x[:, k, s * HALF:(s + 1) * HALF],
                                     start=k == 0 and step == 0, stop=k == KT - 1 and step == 2)
                ins.then_inc(wt_used.sem, 1)

            def stage(n, h, prev):
                if prev is not None:
                    if n == 0:
                        pe.wait_ge(h_v.sem, h_v.at(prev))
                        pe.wait_ge(r_out.sem, r_out.at(prev, 1))
                        for t in range(1, TILES):
                            nc.tensor.transpose(ps[:, A, tile_cols(t - 1)], hvT[:, tile_cols(t)], ident)
                        nc.tensor.transpose(ps[:, BB, 0:P], hvT[:, 0:P], ident).then_inc(pe_htok.sem, 1)
                    if n == 1:
                        pe.wait_ge(h_kl.sem, h_kl.at(prev))
                        for i, t in enumerate((0, 1, 2, 3)):
                            nc.tensor.transpose(ps[:, C, tile_cols(i)], KL[:, 0, tile_cols(t)], ident)
                        for i, t in enumerate((0, 2, 3, 4)):
                            ins = nc.tensor.transpose(ps[:, DD, tile_cols(i)], KL[:, 1, tile_cols(t)], ident)
                        ins.then_inc(pe_hkl.sem, 1)
                    if n == 2:
                        pe.wait_ge(h_kltok.sem, h_kltok.at(prev))
                        pe.wait_ge(h_tok.sem, h_tok.at(prev))
                        for i, t in enumerate((0, 1, 2, 3)):
                            mm(ps[:, C, tile_cols(i)], kltok[:, i, :], htok[:, t, :], start=True, stop=True)
                        for i, t in enumerate((0, 2, 3, 4)):
                            ins = mm(ps[:, DD, tile_cols(i)], kltok[:, 4 + i, :], htok[:, t, :], start=True, stop=True)
                        ins.then_inc(pe_hu.sem, 1)
                    if 2 <= n < 2 + PRODUCTS:
                        level = n - 2
                        b = level % 2
                        pe.wait_ge(la.sem, la.at(prev, level + 1))
                        if level < LEVELS:
                            pe.wait_ge(lq.sem, lq.at(prev, level + 1))
                            q = XE[:, b, 0, :]
                        else:
                            q = hq
                        if level:
                            if due(h_sT, prev, level):
                                pe.wait_ge(h_sT.sem, h_sT.at(prev, level))
                        for t in range(1, TILES):
                            mm(ps[:, A, tile_cols(t - 1)], XE[:, b, 1, tile_cols(t)], q[:, tile_cols(t)], start=True, stop=True)
                        mm(ps[:, BB, 0:P], XE[:, b, 1, 0:P], q[:, 0:P], start=True, stop=True).then_inc(pe_level.sem, 1)
                    if n == 10:
                        pe.wait_ge(h_sT.sem, h_sT.at(prev))
                        pe.wait_ge(h_S.sem, h_S.at(prev))
                        pe.wait_ge(h_qr.sem, h_qr.at(prev))
                        pe.wait_ge(h_state.sem, h_state.at(prev))
                        for t in range(1, TILES):
                            out = ps[:, C, tile_cols(t - 1)]
                            mm(out, htok[:, t, :], hsT[:, tile_cols(t)], start=True, stop=False)
                            mm(out, S[:, 0, t - 1, :], F[:, 0, tile_cols(t)], start=False, stop=False)
                            mm(out, S[:, 1, t - 1, :], F[:, 1, tile_cols(t)], start=False, stop=True)
                        mm(ps[:, DD, 0:P], htok[:, 0, :], hsT[:, 0:P], start=True, stop=True).then_inc(pe_ho.sem, 1)
                    if n == 11:
                        pe.wait_ge(h_sq.sem, h_sq.at(prev))
                        mm(ps[:, A, :], ones, hsq[:, P:T], start=True, stop=True)
                        mm(ps[:, BB, 0:P], ones, hsq[:, 0:P], start=True, stop=True).then_inc(pe_hss.sem, 1)
                if h is None:
                    return
                if n == 12:
                    pe.wait_ge(r_q.sem, r_q.at(h))
                    pe.wait_ge(r_k.sem, r_k.at(h))
                    if due(h_rms, h - 1, 1):
                        pe.wait_ge(h_rms.sem, h_rms.at(h - 1, 1))
                    mm(ps[:, A, :], swap, rq[:, P:T], start=True, stop=True)
                    mm(ps[:, BB, :], swap, rk[:, P:T], start=True, stop=True).then_inc(pe_rswap.sem, 1)
                if n == 13:
                    pe.wait_ge(r_v.sem, r_v.at(h))
                    if due(h_out, h - 1, 1):
                        pe.wait_ge(h_out.sem, h_out.at(h - 1, 1))
                    for t in range(1, TILES):
                        nc.tensor.transpose(ps[:, C, tile_cols(t - 1)], rvT[:, tile_cols(t)], ident)
                    nc.tensor.transpose(ps[:, DD, 0:P], rvT[:, 0:P], ident)
                    nc.tensor.transpose(ps[:, DD, P:2 * P], rk[:, 0:P], ident).then_inc(pe_rtok.sem, 1)
                if n == 14 or n == 15:
                    pe.wait_ge(roped.sem, roped.at(h))
                    for jt in range(2 * (n - 14), 2 * (n - 14) + 2):
                        if jt >= 2:
                            if due(r_sT, h, jt - 1):
                                pe.wait_ge(r_sT.sem, r_sT.at(h, jt - 1))
                        mm(ps[:, A + jt % 2, :], rk[:, tile_cols(1 + jt)], rq[:, P:T], start=True, stop=True).then_inc(pe_rs.sem, 1)
                    if n == 15:
                        pe.wait_ge(r_tok.sem, r_tok.at(h))
                        mm(ps[:, C, 0:P], rk[:, 0:P], rq[:, 0:P], start=True, stop=True).then_inc(pe_rs.sem, 1)
                if n == 16:
                    pe.wait_ge(r_sT.sem, r_sT.at(h))
                    pe.wait_ge(r_qdec.sem, r_qdec.at(h))
                    pe.wait_ge(r_S0.sem, r_S0.at(h))
                    for jt in range(4):
                        mm(ps[:, A, :], rtok[:, 1 + jt, :], sT[:, jt * LAT:(jt + 1) * LAT], start=jt == 0, stop=False)
                    for s in range(2):
                        mm(ps[:, A, :], rS0[:, s, :], rqd[:, s, :], start=False, stop=s == 1)
                    mm(ps[:, BB, 0:P], rtok[:, 0, :], sT[:, 4 * LAT:4 * LAT + P], start=True, stop=True)
                    for s in range(2):
                        ins = mm(ps[:, DD, tile_cols(s)], kts[:, s, :], rtok[:, 0, :], start=True, stop=True)
                    ins.then_inc(pe_ro.sem, 1)
                if n == 17:
                    pe.wait_ge(r_sq.sem, r_sq.at(h))
                    pe.wait_ge(r_state.sem, r_state.at(h))
                    mm(ps[:, C, :], ones, rsq[:, P:T], start=True, stop=True)
                    mm(ps[:, DD, 0:P], ones, rsq[:, 0:P], start=True, stop=True).then_inc(pe_rss.sem, 1)

            def head(h, prev):
                for n in range(CHUNKS):
                    chunk(h, n)
                    stage(n, h, prev)

            head(0, None)
            head(1, 0)
            with pe.Fori(2, HEADS) as h:
                head(h, h - 1)
            for n in range(12):
                stage(n, None, HEADS - 1)

            for nb in range(OUT_BLOCKS):
                for j in range(WCHUNKS):
                    m = nb * WCHUNKS + j
                    pe.wait_ge(d_lo.sem, d_lo.at(0, m + 1))
                    if nb == 0:
                        if due(o_lo, WK * (j + 1) - 1):
                            pe.wait_ge(o_lo.sem, o_lo.at(WK * (j + 1) - 1))
                    for t in range(TILES):
                        if j == 0 and nb % 2 == 0 and nb and t < 2:
                            if due(d_ev, nb - 1, t + 1):
                                pe.wait_ge(d_ev.sem, d_ev.at(nb - 1, t + 1))
                        if j == 0 and nb % 2 == 1:
                            if t == 0:
                                if due(d_ev, nb - 2):
                                    pe.wait_ge(d_ev.sem, d_ev.at(nb - 2))
                            if t >= 3:
                                if due(d_ev, nb - 1, t - 2):
                                    pe.wait_ge(d_ev.sem, d_ev.at(nb - 1, t - 2))
                        for kk in range(WK):
                            k = j * WK + kk
                            w = slice(kk * WIDE, (kk + 1) * WIDE)
                            out = ps[:, out_bank(nb, t), :]
                            mm(out, hT_hi[:, k, tile_cols(t)], w_hi[:, m % 2, w], start=k == 0, stop=False)
                            mm(out, hT_hi[:, k, tile_cols(t)], w_lo[:, m % 2, w], start=False, stop=False)
                            i = mm(out, hT_lo[:, k, tile_cols(t)], w_hi[:, m % 2, w], start=False, stop=k == KT - 1)
                    i.then_inc(d_used.sem, 1)


_INS = ["x_prompt", "x_sample", "state_ret_fwd", "state_ret_bwd", "state_hgrn_fwd", "state_hgrn_bwd", "c", "c_ctx",
        "norm_w", "w_ada", "b_ada", "w_in", "ret_decay", "hg_lower_bounds", "hg_norm_w", "w_out", "final_norm_w"]
_STATE = (1, 1, HEADS, P, P)
_OUTS = [(1, CTX, D_MODEL), (1, LAT, D_MODEL), _STATE, _STATE, _STATE, _STATE]


def _constants():
    import numpy as np

    con = np.zeros((P, NCONST), np.float32)
    p = np.arange(P)
    con[:, C_IDENT:C_IDENT + P] = np.eye(P)
    con[p ^ 32, C_SWAP + p] = 1.0
    con[:, C_ONES:C_ONES + P] = 1.0
    quarter = P // 4
    freqs = (np.float32(ROPE_BASE) ** (-np.arange(quarter, dtype=np.float32) / np.float32(quarter))).astype(np.float32)
    tok = np.arange(LAT)
    pos = np.stack([tok // GRID_W, tok % GRID_W]).astype(np.float32)
    ang = (pos[p // (2 * quarter)] * freqs[p % quarter][:, None]).astype(np.float32)
    sign = np.where((p // quarter) % 2 == 0, -1.0, 1.0)[:, None]
    con[:, C_COS:C_COS + LAT] = np.cos(ang)
    con[:, C_SIN:C_SIN + LAT] = sign * np.sin(ang)
    con[:, C_REL:C_REL + REL] = np.arange(REL)[None, :] - (REL - LAT) - p[:, None]
    for level in range(1, PRODUCTS):
        size = P >> level
        con[:, C_MASK + (level - 1) * P:C_MASK + level * P] = p[:, None] // size == p[None, :] // size
    con[:, C_RESET:C_RESET + T] = np.arange(T) % P != 0
    con[:, C_POS:C_POS + 4] = np.stack([p + 1, LAT - p, P - 1 - p, p], 1)
    return con


def kernel(**inputs):
    import numpy as np
    import concourse.bacc as bacc
    from concourse.bass_utils import run_bass_kernel_spmd

    nc = bacc.Bacc("TRN2", target_bir_lowering=False, num_devices=1)
    arrays, args = {}, []
    for name in _INS:
        a = np.ascontiguousarray(inputs[name])
        arrays[f"in_{name}"] = a
        args.append(nc.dram_tensor(f"in_{name}", a.shape, F32, kind="ExternalInput").ap())
    con = _constants()
    arrays["in_constants"] = con
    args.append(nc.dram_tensor("in_constants", con.shape, F32, kind="ExternalInput").ap())
    for i, shape in enumerate(_OUTS):
        args.append(nc.dram_tensor(f"out_{i}", shape, F32, kind="ExternalOutput").ap())
    layer(nc, *args)
    r = run_bass_kernel_spmd(nc, [arrays], core_ids=[0])
    return tuple(r.results[0][f"out_{i}"] for i in range(len(_OUTS)))
```

```python
from contextlib import ExitStack

import concourse.bass as bass
from concourse import mybir

P = 128
D_MODEL = 2048
KT = D_MODEL // P
CTX, LAT = 128, 512
T = CTX + LAT
TILES = T // P
HALF = T // 2
HEADS = 8
PARTS = 9
HEAD_COLS = HEADS * P
CHUNKS = 2 * PARTS
KC = KT // 2
CHUNK_COLS = KC * P
WIDE = 512
WK = CHUNK_COLS // WIDE
WCHUNKS = KT // WK
ADA_BLOCKS = 3 * D_MODEL // WIDE
ADA_INPUT = 2 * D_MODEL // WIDE
GROUPS = 4
GROUP = P // GROUPS
OUT_BLOCKS = D_MODEL // WIDE
LEVELS = 7
PRODUCTS = LEVELS + 1
DK_SCALE = float(P) ** -0.5
EPS = 1e-6
GRID_W = 64
ROPE_BASE = 10000.0

F32 = mybir.dt.float32
F32R = mybir.dt.float32r
I32 = mybir.dt.int32
ALU = mybir.AluOpType
ACT = mybir.ActivationFunctionType
AX_X = mybir.AxisListType.X

C_IDENT, C_SWAP, C_ONES = 0, P, 2 * P
C_COS = 3 * P
C_SIN = C_COS + LAT
C_REL = C_SIN + LAT
REL = LAT + LAT - P
C_MASK = C_REL + REL
C_RESET = C_MASK + LEVELS * P
C_POS = C_RESET + T
NCONST = C_POS + 4


def layer(nc, x_prompt, x_sample, s_ret_f, s_ret_b, s_hg_f, s_hg_b, c, c_ctx, norm_w, w_ada, b_ada,
          w_in, ret_decay, hg_lower, hg_norm_w, w_out, final_norm_w, consts,
          y_prompt, y_sample, n_ret_f, n_ret_b, n_hg_f, n_hg_b):
    ctx = ExitStack()
    with ctx:
        def sb(name, shape, dt=F32):
            return ctx.enter_context(nc.sbuf_tensor(name, shape, dt))

        class Signal:

            def __init__(self, name, each=1):
                self.sem, self.each = ctx.enter_context(nc.semaphore(name)), each

            def at(self, h, k=None):
                return self.each * h + (self.each if k is None else k)

        def due(signal, h, k=None):
            value = signal.at(h, k)
            return not isinstance(value, int) or value > 0

        con = sb("con", [P, NCONST])
        hT_hi = sb("hT_hi", [P, KT, T], F32R)
        hT_lo = sb("hT_lo", [P, KT, T], F32R)
        w_hi = sb("w_hi", [P, 2, CHUNK_COLS], F32R)
        w_lo = sb("w_lo", [P, 2, CHUNK_COLS], F32R)
        small = sb("small", [P, 448])
        AREA = 24320
        area = sb("area", [P, AREA])
        ps = ctx.enter_context(nc.psum_tensor("ps", [P, 8, 512], F32))

        mod_dram = nc.dram_tensor("mod_scratch", (GROUPS, 3 * D_MODEL), F32).ap()
        gate_dram = nc.dram_tensor("gate_scratch", (2, D_MODEL), F32).ap()
        o_dram = nc.dram_tensor("o_scratch", (2 * HEADS, P, T), F32).ap()

        ident = con[:, C_IDENT:C_IDENT + P]
        swap = con[:, C_SWAP:C_SWAP + P]
        ones = con[:, C_ONES:C_ONES + P]
        cos, sin = con[:, C_COS:C_COS + LAT], con[:, C_SIN:C_SIN + LAT]
        rel = con[:, C_REL:C_REL + REL]
        reset = con[:, C_RESET:C_RESET + T]

        def mask(level):
            return con[:, C_MASK + (level - 1) * P:C_MASK + level * P].bitcast(I32)

        used = [0]

        def cols(n):
            used[0] += n
            assert used[0] <= AREA, used[0]
            return area[:, used[0] - n:used[0]]

        scols = [0]

        def sc(n):
            scols[0] += n
            assert scols[0] <= 448
            return small[:, scols[0] - n:scols[0]]

        raw = cols(3 * CHUNK_COLS).rearrange("p (s n) -> p s n", s=3)
        RET0 = used[0]
        rq, rk, rvT = cols(T), cols(T), cols(T)
        rtok = cols(T).rearrange("p (t d) -> p t d", d=P)
        rsg = cols(T)
        strip = cols(REL)
        sT = cols(4 * LAT + P)
        rsq, rr = sT[:, 0:T], sT[:, 2 * LAT:2 * LAT + T]
        rope_q, rope_k = sT[:, 2 * LAT:3 * LAT], sT[:, 3 * LAT:4 * LAT]
        RET1 = used[0]
        rqd = cols(2 * LAT).rearrange("p (s n) -> p s n", s=2)
        graw = area[:, used[0] - 2 * LAT:used[0] - 2 * LAT + T]
        kts = cols(2 * P).rearrange("p (s n) -> p s n", s=2)
        rS0 = cols(2 * P).rearrange("p (s n) -> p s n", s=2)
        rst = cols(2 * P).rearrange("p (s n) -> p s n", s=2)
        HG0 = used[0]
        hq = cols(T)
        F = cols(2 * T).rearrange("p (s n) -> p s n", s=2)
        K = cols(2 * T).rearrange("p (s n) -> p s n", s=2)
        B = cols(2 * T).rearrange("p (s n) -> p s n", s=2)
        KL = cols(2 * T).rearrange("p (s n) -> p s n", s=2)
        hsq, hr = KL[:, 0, :], KL[:, 1, :]
        kltok = cols(8 * P).rearrange("p (t d) -> p t d", d=P)
        XE = cols(4 * T).rearrange("p (b s n) -> p b s n", b=2, s=2)
        S = cols(8 * P).rearrange("p (s t d) -> p s t d", s=2, t=4)
        hst = cols(2 * P).rearrange("p (s n) -> p s n", s=2)
        htok = cols(T).rearrange("p (t d) -> p t d", d=P)
        hsT = cols(T)
        hsg = cols(T)
        hvT = cols(T)

        ada_raw = area[:, 0:WCHUNKS * CHUNK_COLS].rearrange("p (s n) -> p s n", s=WCHUNKS)
        X0 = WCHUNKS * CHUNK_COLS
        x_in = area[:, X0:X0 + TILES * D_MODEL].rearrange("p (t n) -> p t n", t=TILES)
        J0 = X0 + TILES * D_MODEL
        junk_in = area[:, J0:J0 + D_MODEL]
        mod_row = area[:, J0 + D_MODEL:J0 + D_MODEL + 2 * WIDE].rearrange("p (s n) -> p s n", s=2)
        C0 = J0 + D_MODEL + 2 * WIDE
        lb_in = area[0:4 * HEADS, C0:C0 + P]
        mod_cols = area[:, C0 + P:C0 + P + 3 * GROUPS * KT].rearrange("p (g s k) -> p g s k", g=GROUPS, s=3)
        bias_cols = area[:, C0 + 2 * P + P:C0 + 3 * P + 3 * KT].rearrange("p (s k) -> p s k", s=3)
        gate_cols = area[:, C0 + 4 * P:C0 + 4 * P + 2 * KT].rearrange("p (w k) -> p w k", w=2)
        assert P + 3 * GROUPS * KT <= 3 * P and C0 + 5 * P <= AREA
        cs = hT_hi[:, :, 0:P]
        STAGES = 9
        o_raw = area[:, RET0:RET0 + STAGES * T].rearrange("p (s n) -> p s n", s=STAGES)
        gates = area[:, RET0:RET0 + 2 * D_MODEL].rearrange("p (s n) -> p s n", s=2)
        fnw = area[:, RET0 + 2 * D_MODEL:RET0 + 3 * D_MODEL]
        assert RET0 + 3 * D_MODEL <= RET1 and RET0 + STAGES * T <= RET1
        x_res = area[:, HG0:HG0 + TILES * D_MODEL].rearrange("p (t n) -> p t n", t=TILES)
        junk_out = area[:, HG0 + TILES * D_MODEL:HG0 + TILES * D_MODEL + WIDE]
        assert HG0 + TILES * D_MODEL + WIDE <= used[0]
        gated = rqd

        c_raw = sc(2 * KT).rearrange("p (w k) -> p w k", w=2)
        c_sig = sc(2 * KT).rearrange("p (w k) -> p w k", w=2)
        nw = sc(KT)
        mods = sc(4 * KT).rearrange("p (w s k) -> p w s k", w=2, s=2)
        lgr = sc(2 * HEADS)
        lgu, lgt = sc(2 * HEADS), sc(2 * HEADS)
        lg, nlg = sc(2 * HEADS), sc(2 * HEADS)
        dbias = sc(2 * HEADS)
        kdec = sc(2 * HEADS)
        lbT = sc(4 * HEADS)
        lb, oml = sc(2 * HEADS), sc(2 * HEADS)
        lbm = sc(2 * HEADS)
        hnw = sc(1)
        ssq = sc(TILES)
        var, rstd, newt = sc(TILES), sc(TILES), sc(TILES)
        ssq4 = sc(TILES * OUT_BLOCKS).rearrange("p (t n) -> p t n", t=TILES)
        ssq_out, var_o, rstd_o, newt_o = sc(TILES), sc(TILES), sc(TILES), sc(TILES)
        dec = sc(2 * TILES).rearrange("p (s t) -> p s t", s=2)
        eps_col = sc(1)
        lgu2 = sc(2 * HEADS)

        c_in, small_in = Signal("c_in", 16), Signal("small_in", 16)
        x_landed = Signal("x_landed", 16)
        c_steps, c_exp = Signal("c_steps"), Signal("c_exp")
        lg_steps, lg_act = Signal("lg_steps"), Signal("lg_act")
        lb_pe = Signal("lb_pe")
        cs_ready = Signal("cs_ready")
        x_sq = Signal("x_sq")
        rstd_act, rstd_steps = Signal("rstd_act"), Signal("rstd_steps")
        x_scaled = Signal("x_scaled")
        a_landed = [Signal(f"a_landed{j}", 16) for j in range(WCHUNKS)]
        a_hi, a_lo, a_used = Signal("a_hi", KT), Signal("a_lo", KT), Signal("a_used", KT)
        a_row, a_store = Signal("a_row"), [Signal(f"a_store{j}", 16) for j in range(2)]
        mods_in, mod_steps = Signal("mods_in", 16), Signal("mod_steps")
        gate_in, gate_steps, gate_stored = Signal("gate_in", 16), Signal("gate_steps"), Signal("gate_stored", 16)
        x_tr, x_evac = Signal("x_tr"), Signal("x_evac")
        h_mod, h_hi, h_lo = Signal("h_mod"), Signal("h_hi"), Signal("h_lo")
        ctx_hi, ctx_lo = Signal("ctx_hi", 2), Signal("ctx_lo", 2)
        landed = [Signal(f"landed{j}", 16 * CHUNKS // 3) for j in range(3)]
        wt_hi, wt_lo, wt_used = Signal("wt_hi", CHUNKS), Signal("wt_lo", CHUNKS), Signal("wt_used", CHUNKS)
        r_q, r_k, r_v, r_eg = Signal("r_q"), Signal("r_k"), Signal("r_v"), Signal("r_eg")
        r_silu = Signal("r_silu", 4)
        strip_x, strip_e, strip_i = Signal("strip_x", 3), Signal("strip_e"), Signal("strip_i")
        r_dec, r_qdec = Signal("r_dec"), Signal("r_qdec")
        rope_cos, rope_sin, roped = Signal("rope_cos"), Signal("rope_sin"), Signal("roped")
        r_tok = Signal("r_tok", 2)
        r_sT = Signal("r_sT", 5)
        r_sq, r_state, r_rms, r_out = Signal("r_sq"), Signal("r_state"), Signal("r_rms", 2), Signal("r_out", 2)
        pe_rswap, pe_rtok, pe_rs = Signal("pe_rswap"), Signal("pe_rtok"), Signal("pe_rs", 5)
        pe_ro, pe_rss = Signal("pe_ro"), Signal("pe_rss")
        r_S0, r_stored, r_state_stored = Signal("r_S0", 32), Signal("r_stored", 16), Signal("r_state_stored", 32)
        h_q, h_ez, h_v = Signal("h_q"), Signal("h_ez", 2), Signal("h_v")
        h_graw, h_eg, h_silu = Signal("h_graw"), Signal("h_eg"), Signal("h_silu", 4)
        h_gate, h_log, h_scan = Signal("h_gate", 10), Signal("h_log", 2), Signal("h_scan", 2)
        h_klx, h_eb, h_ekl = Signal("h_klx"), Signal("h_eb"), Signal("h_ekl")
        h_dec, h_qr, h_kl = Signal("h_dec"), Signal("h_qr"), Signal("h_kl")
        h_tok, h_kltok, h_state = Signal("h_tok"), Signal("h_kltok"), Signal("h_state")
        h_S = Signal("h_S", 3)
        xq, xa, xe = Signal("xq", LEVELS), Signal("xa", LEVELS), Signal("xe", LEVELS)
        lq, la = Signal("lq", LEVELS), Signal("la", PRODUCTS)
        h_sT = Signal("h_sT", PRODUCTS)
        h_sq, h_rms, h_out = Signal("h_sq"), Signal("h_rms", 2), Signal("h_out", 2)
        pe_htok, pe_hkl, pe_hu, pe_level = Signal("pe_htok"), Signal("pe_hkl"), Signal("pe_hu"), Signal("pe_level", PRODUCTS)
        pe_ho, pe_hss = Signal("pe_ho"), Signal("pe_hss")
        h_S0, h_stored, h_state_stored = Signal("h_S0", 32), Signal("h_stored", 16), Signal("h_state_stored", 32)
        o_landed = [Signal(f"o_landed{j}", 16) for j in range(STAGES)]
        o_hi, o_lo = Signal("o_hi"), Signal("o_lo")
        d_landed = [Signal(f"d_landed{j}", 16) for j in range(2)]
        d_hi, d_lo, d_used = Signal("d_hi", WCHUNKS), Signal("d_lo", WCHUNKS), Signal("d_used", WCHUNKS)
        gates_in, res_in = Signal("gates_in", 16), Signal("res_in", 16)
        d_gated, d_ev, d_sq = Signal("d_gated", TILES), Signal("d_ev", TILES), Signal("d_sq", TILES)
        fin_steps, fin_act, y_ready, y_stored = Signal("fin_steps"), Signal("fin_act"), Signal("y_ready"), Signal("y_stored", 16)
        con_in = Signal("con_in", 16)

        A, BB, C, DD = 4, 5, 6, 7

        w_ada_v = w_ada[0].rearrange("(p k) n -> p k n", k=KT)
        w_in_v = w_in[0].rearrange("(p k) n -> p k n", k=KT)
        w_out_v = w_out[0].rearrange("(k p) n -> p k n", p=P)

        def tile_cols(t):
            return slice(t * P, (t + 1) * P)

        def proj(i):
            return ps[:, 2 * (i % 2):2 * (i % 2) + 2, 0:HALF]

        def halves(ap):
            return ap.rearrange("p (s n) -> p s n", s=2)

        def tiles(ap):
            return ap.rearrange("p (t n) -> p t n", n=P)

        def blocks(ap, level):
            return ap.rearrange("p (b n) -> p b n", n=P >> level)

        def evac_order(nb):
            return [0, 1, 2, 3, 4] if nb % 2 == 0 else [3, 4, 0, 1, 2]

        def out_bank(nb, t):
            return ((0, 1, 2, 3, BB), (A, C, DD, 0, 1))[nb % 2][t]

        def ctx_scores(h, level):
            return ps[:, BB if h is not None or level == 0 else DD, 0:P]

        def ctx_sums(h):
            return ps[:, BB, 0:P] if h is not None else ps[:, DD, P:2 * P]

        block = ctx.enter_context(nc.Block())

        @block.sync
        def _(sp):
            def load_ada(nb, j, gate):
                if gate:
                    if due(a_lo, nb - 1, WK * (j + 1)):
                        sp.wait_ge(a_lo.sem, a_lo.at(nb - 1, WK * (j + 1)))
                sp.dma_start(ada_raw[:, j, :].rearrange("p (k n) -> p k n", k=WK),
                             w_ada_v[:, j * WK:(j + 1) * WK, bass.ds(nb * WIDE, WIDE)]).then_inc(a_landed[j].sem, 16)

            def ada_block(nb):
                for j in range(WCHUNKS):
                    load_ada(nb, j, not isinstance(nb, int) or nb > 0)

            sp.dma_start(c_raw[:, 0, :], c_ctx.rearrange("(p k) -> p k", k=KT)).then_inc(c_in.sem, 16)
            sp.dma_start(c_raw[:, 1, :], c[0].rearrange("(p k) -> p k", k=KT)).then_inc(c_in.sem, 16)
            ada_block(0)
            sp.dma_start(lgr, ret_decay.rearrange("l s h -> l (s h)").broadcast_to([P, 2 * HEADS])).then_inc(small_in.sem, 16)
            sp.dma_start(lb_in, hg_lower.rearrange("s l (h d) -> (s l h) d", d=P)).then_inc(small_in.sem, 16)
            sp.dma_start(nw, norm_w[0].rearrange("(p k) -> p k", k=KT)).then_inc(small_in.sem, 16)
            sp.dma_start(hnw, hg_norm_w.rearrange("l p -> p l")).then_inc(small_in.sem, 16)
            sp.dma_start(bias_cols, b_ada[0].rearrange("(s p k) -> p s k", s=3, k=KT)).then_inc(small_in.sem, 16)
            sp.dma_start(con[:, :], consts).then_inc(con_in.sem, 16)
            sp.dma_start(x_in[:, 0, :], x_prompt[0]).then_inc(x_landed.sem, 16)
            sp.dma_start(x_in[:, 1:TILES, :], x_sample[0].rearrange("(t p) n -> p t n", p=P)).then_inc(x_landed.sem, 16)
            for nb in range(1, 4):
                ada_block(nb)
            with sp.Fori(4, ADA_BLOCKS) as nb:
                ada_block(nb)

            def load(h, n):
                if n < 3:
                    if isinstance(h, int) and h == 0:
                        sp.wait_ge(a_lo.sem, a_lo.at(ADA_BLOCKS - 1, WK * (n + 1)))
                    else:
                        if due(wt_lo, h - 1, CHUNKS + n - 2):
                            sp.wait_ge(wt_lo.sem, wt_lo.at(h - 1, CHUNKS + n - 2))
                else:
                    if due(wt_lo, h, n - 2):
                        sp.wait_ge(wt_lo.sem, wt_lo.at(h, n - 2))
                i, half = n // 2, n % 2
                sp.dma_start(raw[:, n % 3, :].rearrange("p (k n) -> p k n", k=KC),
                             w_in_v[:, half * KC:(half + 1) * KC, bass.ds(i * HEAD_COLS + h * P, P)]
                             ).then_inc(landed[n % 3].sem, 16)

            def store_states(h, new_f, new_b, buf, ready, stored):
                sp.wait_ge(ready.sem, ready.at(h))
                for s, new in enumerate((new_f, new_b)):
                    sp.dma_start(new[0, 0, bass.ds(h, 1)].rearrange("h d v -> (h d) v"), buf[:, s, :]).then_inc(stored.sem, 16)

            def items(n, h, prev):
                if n == 3 and prev is None:
                    for b in range(2):
                        sp.wait_ge(a_store[b].sem, a_store[b].at(ADA_BLOCKS // 2 - 1))
                    sp.dma_start(mod_cols[:, :, 2, :], mod_dram[:, 2 * D_MODEL:3 * D_MODEL].rearrange("g (p k) -> p g k", k=KT)
                                 ).then_inc(gate_in.sem, 16)
                if n == 10 and prev is None:
                    sp.wait_ge(gate_steps.sem, gate_steps.at(1))
                    sp.dma_start(gate_dram.rearrange("w (p k) -> p w k", k=KT), gate_cols).then_inc(gate_stored.sem, 16)
                if n == 4 and prev is not None:
                    store_states(prev, n_ret_f, n_ret_b, rst, r_state, r_state_stored)
                if n == 6 and prev is not None:
                    sp.wait_ge(r_out.sem, r_out.at(prev))
                    sp.dma_start(o_dram[bass.ds(prev, 1)].rearrange("h d t -> (h d) t"), rr).then_inc(r_stored.sem, 16)
                if n == 6 and h is not None:
                    if due(pe_ro, h - 1):
                        sp.wait_ge(pe_ro.sem, pe_ro.at(h - 1))
                    for s, old in enumerate((s_ret_f, s_ret_b)):
                        sp.dma_start(rS0[:, s, :], old[0, 0, bass.ds(h, 1)].rearrange("h d v -> (h d) v")).then_inc(r_S0.sem, 16)
                if n == 8 and prev is not None:
                    store_states(prev, n_hg_f, n_hg_b, hst, h_state, h_state_stored)
                if n == 17 and prev is not None:
                    sp.wait_ge(h_out.sem, h_out.at(prev))
                    sp.dma_start(o_dram[bass.ds(prev + HEADS, 1)].rearrange("h d t -> (h d) t"), hr).then_inc(h_stored.sem, 16)
                if n == 17 and h is not None:
                    if due(pe_ho, h - 1):
                        sp.wait_ge(pe_ho.sem, pe_ho.at(h - 1))
                    for s, old, at in ((0, s_hg_f, 0), (1, s_hg_b, 3)):
                        sp.dma_start(S[:, s, at, :], old[0, 0, bass.ds(h, 1)].rearrange("h d v -> (h d) v")).then_inc(h_S0.sem, 16)

            def head(h, prev):
                for n in range(CHUNKS):
                    load(h, n)
                    items(n, h, prev)

            head(0, None)
            head(1, 0)
            with sp.Fori(2, HEADS) as h:
                head(h, h - 1)
            last = HEADS - 1
            items(4, None, last)
            items(6, None, last)

            def load_o(kt):
                if kt >= STAGES:
                    if due(o_lo, kt - STAGES):
                        sp.wait_ge(o_lo.sem, o_lo.at(kt - STAGES))
                if kt < HEADS:
                    sp.wait_ge(r_stored.sem, r_stored.at(kt))
                else:
                    if due(h_stored, kt - HEADS):
                        sp.wait_ge(h_stored.sem, h_stored.at(kt - HEADS))
                sp.dma_start(o_raw[:, kt % STAGES, :], o_dram[kt]).then_inc(o_landed[kt % STAGES].sem, 16)

            def load_w_out(m):
                nb, j = m // WCHUNKS, m % WCHUNKS
                if m < 2:
                    sp.wait_ge(wt_lo.sem, wt_lo.at(last))
                else:
                    if due(d_lo, 0, m - 1):
                        sp.wait_ge(d_lo.sem, d_lo.at(0, m - 1))
                sp.dma_start(raw[:, m % 2, :].rearrange("p (k n) -> p k n", k=WK),
                             w_out_v[:, j * WK:(j + 1) * WK, nb * WIDE:(nb + 1) * WIDE]).then_inc(d_landed[m % 2].sem, 16)

            load_w_out(0)
            load_w_out(1)
            sp.wait_ge(r_stored.sem, r_stored.at(last))
            for kt in range(STAGES):
                load_o(kt)
            load_w_out(2)
            items(8, None, last)
            for m in range(3, 3 + (2 * HEADS - 1 - STAGES) // 2):
                load_o(STAGES + 2 * (m - 3))
                load_o(STAGES + 2 * (m - 3) + 1)
                load_w_out(m)
            for m in range(m + 1, WCHUNKS + 2):
                load_w_out(m)
            sp.wait_ge(h_state_stored.sem, h_state_stored.at(last))

            for m in range(WCHUNKS + 2, OUT_BLOCKS * WCHUNKS):
                load_w_out(m)
                if m == WCHUNKS + 2:
                    sp.wait_ge(o_lo.sem, o_lo.at(2 * HEADS - 1))
                    sp.dma_start(x_res[:, 0, :], x_prompt[0]).then_inc(res_in.sem, 16)
                    sp.dma_start(x_res[:, 1:TILES, :], x_sample[0].rearrange("(t p) n -> p t n", p=P)).then_inc(res_in.sem, 16)
                    sp.wait_ge(gate_stored.sem, gate_stored.at(0))
                    for w in range(2):
                        sp.dma_start(gates[:, w, :], gate_dram[w:w + 1, :].broadcast_to([P, D_MODEL])
                                     ).then_inc(gates_in.sem, 16)
                    sp.dma_start(fnw, final_norm_w.rearrange("(l n) -> l n", l=1).broadcast_to([P, D_MODEL])).then_inc(gates_in.sem, 16)
            for t in range(TILES):
                sp.wait_ge(y_ready.sem, y_ready.at(t))
                out = y_prompt[0] if t == 0 else y_sample[0, (t - 1) * P:t * P, :]
                sp.dma_start(out, x_res[:, t, :]).then_inc(y_stored.sem, 16)
            sp.wait_ge(y_stored.sem, y_stored.at(TILES - 1))
            sp.wait_ge(r_state_stored.sem, r_state_stored.at(last))
            sp.wait_ge(h_state_stored.sem, h_state_stored.at(last))

        @block.scalar
        def _(act):
            act.preload_act_table_set("natural_log_exp_and_others")
            act.wait_ge(c_in.sem, c_in.at(1))
            act.activation(c_sig, c_raw, ACT.Exp, scale=-1.0).then_inc(c_exp.sem, 1)

            def ada_block(nb, extra=None):
                for j in range(WCHUNKS):
                    act.wait_ge(a_landed[j].sem, a_landed[j].at(nb))
                    for kk in range(WK):
                        if not (isinstance(nb, int) and nb == 0 and j < 2):
                            if due(a_used, nb, WK * (j - 2) + kk + 1):
                                act.wait_ge(a_used.sem, a_used.at(nb, WK * (j - 2) + kk + 1))
                        w = slice(kk * WIDE, (kk + 1) * WIDE)
                        act.activation(w_hi[:, j % 2, w], ada_raw[:, j, w], ACT.Copy).then_inc(a_hi.sem, 1)
                    if extra is not None:
                        extra(j)

            def store_row(nb, b):
                act.wait_ge(a_row.sem, a_row.at(nb))
                act.dma_start(mod_dram[:, bass.ds(nb * WIDE, WIDE)], mod_row[0:P:GROUP, b, :]).then_inc(a_store[b].sem, 16)

            def stores(nb):
                def extra(j):
                    if j == 4:
                        store_row(nb - 1, (nb - 1) % 2)
                return extra

            ada_block(0)
            act.wait_ge(small_in.sem, small_in.at(4))
            act.activation(lgt, lgr, ACT.Exp).then_inc(lg_act.sem, 1)
            act.wait_ge(lg_steps.sem, lg_steps.at(0, 1))
            act.activation(lg, lgu, ACT.Ln).then_inc(lg_act.sem, 1)
            act.wait_ge(lg_steps.sem, lg_steps.at(0, 10))
            act.activation(lbT, lbT, ACT.Exp).then_inc(lg_act.sem, 1)
            act.wait_ge(lg_steps.sem, lg_steps.at(0, 15))
            act.activation(kdec, kdec, ACT.Exp).then_inc(lg_act.sem, 1)
            act.wait_ge(x_landed.sem, x_landed.at(1))
            for t in range(TILES):
                if t:
                    if due(x_sq, t - 1):
                        act.wait_ge(x_sq.sem, x_sq.at(t - 1))
                act.activation(junk_in, x_in[:, t, :], ACT.Square, accum_out=ssq[:, t:t + 1]).then_inc(x_sq.sem, 1)

            def with_rstd(j):
                stores(1)(j)
                if j == 1:
                    act.wait_ge(rstd_steps.sem, rstd_steps.at(0, 1))
                    act.activation(rstd, var, ACT.Ln).then_inc(rstd_act.sem, 1)
                    act.wait_ge(rstd_act.sem, rstd_act.at(0))
                    act.activation(rstd, rstd, ACT.Exp, scale=-0.5).then_inc(rstd_act.sem, 1)

            def with_transposes(nb):
                def extra(j):
                    stores(nb)(j)
                    k = (nb - 2) * WCHUNKS + j - 1
                    if k >= 0:
                        evacuate_x(k)
                return extra

            def evacuate_x(k):
                bank = 4 + 2 * (k % 2)
                act.wait_ge(x_tr.sem, x_tr.at(k))
                act.activation(x_in[:, 1:TILES, k::KT], tiles(ps[:, bank, :]), ACT.Copy)
                act.activation(x_in[:, 0, k::KT], ps[:, bank + 1, 0:P], ACT.Copy).then_inc(x_evac.sem, 1)

            def high_input(k):
                act.wait_ge(h_mod.sem, h_mod.at(k))
                act.activation(tiles(hT_hi[:, k, P:T]), x_in[:, 1:TILES, k::KT], ACT.Copy).then_inc(h_hi.sem, 1)

            def with_modulation(nb):
                def extra(j):
                    stores(nb)(j)
                    if nb == ADA_INPUT and j == 7:
                        for b in range(2):
                            if due(a_store[b], ADA_INPUT // 2 - 1):
                                act.wait_ge(a_store[b].sem, a_store[b].at(ADA_INPUT // 2 - 1))
                        for s in range(2):
                            act.dma_start(mod_cols[:, :, s, :], mod_dram[:, s * D_MODEL:(s + 1) * D_MODEL].rearrange(
                                "g (p k) -> p g k", k=KT)).then_inc(mods_in.sem, 16)
                    k = (nb - ADA_INPUT - 1) * WCHUNKS + j - 3
                    if 0 <= k < KT:
                        high_input(k)
                return extra

            ada_block(1, with_rstd)
            for nb in range(2, 4):
                ada_block(nb, with_transposes(nb))
            evacuate_x(KT - 1)
            with act.Fori(2, ADA_INPUT // 2) as pair:
                for b in range(2):
                    nb = 2 * pair + b
                    def extra(j):
                        if j == 4:
                            store_row(nb - 1, 1 - b)
                    ada_block(nb, extra)
            for nb in range(ADA_INPUT, ADA_BLOCKS):
                ada_block(nb, with_modulation(nb))
            store_row(ADA_BLOCKS - 1, 1)

            def high_context(half):
                ks = slice(half * KC, (half + 1) * KC)
                act.wait_ge(a_used.sem, a_used.at(ADA_BLOCKS - 1))
                act.activation(hT_hi[:, ks, 0:P], x_in[:, 0, :].rearrange("p (n k) -> p k n", k=KT)[:, ks, :],
                               ACT.Copy).then_inc(ctx_hi.sem, 1)

            def split(h, n):
                act.wait_ge(landed[n % 3].sem, landed[n % 3].at(h, 16 * (n // 3 + 1)))
                if n >= 2:
                    if due(wt_used, h, n - 1):
                        act.wait_ge(wt_used.sem, wt_used.at(h, n - 1))
                elif isinstance(h, int) and h == 0:
                    act.wait_ge(a_used.sem, a_used.at(ADA_BLOCKS - 1))
                else:
                    if due(wt_used, h - 1, CHUNKS + n - 1):
                        act.wait_ge(wt_used.sem, wt_used.at(h - 1, CHUNKS + n - 1))
                act.activation(w_hi[:, n % 2, :], raw[:, n % 3, :], ACT.Copy).then_inc(wt_hi.sem, 1)

            def projected(h, i):
                act.wait_ge(wt_used.sem, wt_used.at(h, 2 * i + 2))

            def items(n, h, prev):
                if prev is not None:
                    if n == 0:
                        projected(prev, 8)
                        act.wait_ge(pe_ro.sem, pe_ro.at(prev))
                        act.activation(halves(graw), proj(8), ACT.Copy).then_inc(h_graw.sem, 1)
                        act.wait_ge(pe_rss.sem, pe_rss.at(prev))
                        act.activation(rr[:, P:T], ps[:, C, :], ACT.Ln, scale=1.0 / P, bias=eps_col)
                        act.activation(rr[:, 0:P], ps[:, DD, 0:P], ACT.Ln, scale=1.0 / P, bias=eps_col).then_inc(r_rms.sem, 1)
                        act.wait_ge(r_rms.sem, r_rms.at(prev, 1))
                        act.activation(rr, rr, ACT.Exp, scale=-0.5).then_inc(r_rms.sem, 1)
                        act.wait_ge(h_graw.sem, h_graw.at(prev))
                        if due(h_out, prev - 1):
                            act.wait_ge(h_out.sem, h_out.at(prev - 1))
                        act.activation(hsg, graw, ACT.Exp, scale=-1.0).then_inc(h_eg.sem, 1)
                    if n == 1:
                        act.wait_ge(pe_htok.sem, pe_htok.at(prev))
                        if due(pe_ho, prev - 1):
                            act.wait_ge(pe_ho.sem, pe_ho.at(prev - 1))
                        act.activation(htok[:, 1:TILES, :], tiles(ps[:, A, :]), ACT.Copy)
                        act.activation(htok[:, 0, :], ps[:, BB, 0:P], ACT.Copy).then_inc(h_tok.sem, 1)
                    if n == 2:
                        act.wait_ge(pe_hkl.sem, pe_hkl.at(prev))
                        act.activation(kltok[:, 0:4, :], tiles(ps[:, C, :]), ACT.Copy)
                        act.activation(kltok[:, 4:8, :], tiles(ps[:, DD, :]), ACT.Copy).then_inc(h_kltok.sem, 1)
                    if n == 3:
                        act.wait_ge(pe_hu.sem, pe_hu.at(prev))
                        if due(h_state_stored, prev - 1):
                            act.wait_ge(h_state_stored.sem, h_state_stored.at(prev - 1))
                        act.activation(hst[:, 0, :], ps[:, C, 0:P], ACT.Copy)
                        act.activation(hst[:, 1, :], ps[:, DD, 0:P], ACT.Copy).then_inc(h_state.sem, 1)
                    if 1 <= n <= LEVELS:
                        level = n - 1
                        act.wait_ge(xq.sem, xq.at(prev, level + 1))
                        act.wait_ge(xa.sem, xa.at(prev, level + 1))
                        x = XE[:, level % 2]
                        act.activation(x, x, ACT.Exp).then_inc(xe.sem, 1)
                    if n == 11:
                        act.wait_ge(pe_ho.sem, pe_ho.at(prev))
                        act.activation(hsq[:, P:T], ps[:, C, :], ACT.Square)
                        act.activation(hsq[:, 0:P], ps[:, DD, 0:P], ACT.Square).then_inc(h_sq.sem, 1)
                    if n == 12:
                        act.wait_ge(pe_hss.sem, pe_hss.at(prev))
                        act.activation(hr[:, P:T], ps[:, A, :], ACT.Ln, scale=1.0 / P, bias=eps_col)
                        act.activation(hr[:, 0:P], ctx_sums(h), ACT.Ln, scale=1.0 / P, bias=eps_col).then_inc(h_rms.sem, 1)
                        act.wait_ge(h_rms.sem, h_rms.at(prev, 1))
                        act.activation(hr, hr, ACT.Exp, scale=-0.5).then_inc(h_rms.sem, 1)
                if h is None:
                    return
                if n == 2:
                    projected(h, 0)
                    if due(pe_ro, h - 1):
                        act.wait_ge(pe_ro.sem, pe_ro.at(h - 1))
                    act.activation(halves(rq), proj(0), ACT.Copy).then_inc(r_q.sem, 1)
                if n == 4:
                    projected(h, 1)
                    act.activation(halves(rk), proj(1), ACT.Copy, scale=DK_SCALE).then_inc(r_k.sem, 1)
                if n == 6:
                    projected(h, 2)
                    act.activation(halves(rvT), proj(2), ACT.Copy).then_inc(r_v.sem, 1)
                if n == 8:
                    projected(h, 3)
                    if due(r_out, h - 1):
                        act.wait_ge(r_out.sem, r_out.at(h - 1))
                    act.activation(halves(rsg), proj(3), ACT.Exp, scale=-1.0).then_inc(r_eg.sem, 1)
                if n == 10:
                    projected(h, 4)
                    if due(pe_level, h - 1):
                        act.wait_ge(pe_level.sem, pe_level.at(h - 1))
                    act.activation(halves(hq), proj(4), ACT.Copy).then_inc(h_q.sem, 1)
                if n == 12 or n == 14:
                    s = (n - 12) // 2
                    projected(h, 5 + s)
                    if due(pe_ho, h - 1):
                        act.wait_ge(pe_ho.sem, pe_ho.at(h - 1))
                    act.activation(halves(F[:, s, :]), proj(5 + s), ACT.Exp, scale=-1.0).then_inc(h_ez.sem, 1)
                if n == 16:
                    projected(h, 7)
                    if due(pe_htok, h - 1):
                        act.wait_ge(pe_htok.sem, pe_htok.at(h - 1))
                    act.activation(halves(hvT), proj(7), ACT.Copy).then_inc(h_v.sem, 1)
                if n == 13:
                    act.wait_ge(strip_x.sem, strip_x.at(h, 3))
                    act.activation(strip, strip, ACT.Exp).then_inc(strip_e.sem, 1)
                    if due(h_silu, h - 1):
                        act.wait_ge(h_silu.sem, h_silu.at(h - 1))
                    for s in range(2):
                        col = bass.ds(s * HEADS + h, 1)
                        i = act.activation(rqd[:, s, :], rel[:, REL - LAT:REL], ACT.Exp, bias=dbias[:, col],
                                           scale=(lg if s == 0 else nlg)[:, col])
                    i.then_inc(r_dec.sem, 1)
                if n == 14:
                    act.wait_ge(pe_rtok.sem, pe_rtok.at(h))
                    act.activation(rtok[:, 1:TILES, :], tiles(ps[:, C, :]), ACT.Copy)
                    act.activation(rtok[:, 0, :], ps[:, DD, 0:P], ACT.Copy).then_inc(r_tok.sem, 1)
                    for s in range(2):
                        i = act.activation(kts[:, s, :], ps[:, DD, P:2 * P], ACT.Copy, scale=kdec[:, bass.ds(s * HEADS + h, 1)])
                    i.then_inc(r_tok.sem, 1)
                if n == 14 or n == 16:
                    s = (n - 14) // 2
                    act.wait_ge(h_gate.sem, h_gate.at(h, 5 * s + 5))
                    act.activation(F[:, s, :], F[:, s, :], ACT.Ln).then_inc(h_log.sem, 1)
                if n == 17:
                    act.wait_ge(pe_ro.sem, pe_ro.at(h))
                    act.activation(rsq[:, P:T], ps[:, A, :], ACT.Square)
                    act.activation(rsq[:, 0:P], ps[:, BB, 0:P], ACT.Square).then_inc(r_sq.sem, 1)
                    if due(r_state_stored, h - 1):
                        act.wait_ge(r_state_stored.sem, r_state_stored.at(h - 1))
                    act.activation(rst, ps[:, DD, 0:2 * P].rearrange("p (s n) -> p s n", s=2), ACT.Copy).then_inc(r_state.sem, 1)
                    act.wait_ge(h_scan.sem, h_scan.at(h))
                    act.activation(F, B, ACT.Exp).then_inc(h_eb.sem, 1)
                    act.wait_ge(h_klx.sem, h_klx.at(h))
                    act.activation(KL, KL, ACT.Exp).then_inc(h_ekl.sem, 1)

            def head(h, prev):
                for n in range(CHUNKS):
                    if prev is None and n < 2:
                        high_context(n)
                    split(h, n)
                    if n == 0:
                        if prev is not None:
                            items(CHUNKS - 1, prev, None)
                    else:
                        items(n - 1, h, prev)

            head(0, None)
            head(1, 0)
            with act.Fori(2, HEADS) as h:
                head(h, h - 1)
            last = HEADS - 1
            items(CHUNKS - 1, last, None)

            def split_o(kt):
                if kt == 2 * HEADS - 1:
                    act.wait_ge(h_out.sem, h_out.at(last))
                    src = hr
                else:
                    act.wait_ge(o_landed[kt % STAGES].sem, o_landed[kt % STAGES].at(kt // STAGES))
                    src = o_raw[:, kt % STAGES, :]
                if kt == 0:
                    act.wait_ge(wt_used.sem, wt_used.at(last))
                act.activation(hT_hi[:, kt, :], src, ACT.Copy).then_inc(o_hi.sem, 1)

            def split_w(m):
                act.wait_ge(d_landed[m % 2].sem, d_landed[m % 2].at(m // 2))
                if m >= 2:
                    if due(d_used, 0, m - 1):
                        act.wait_ge(d_used.sem, d_used.at(0, m - 1))
                act.activation(w_hi[:, m % 2, :], raw[:, m % 2, :], ACT.Copy).then_inc(d_hi.sem, 1)

            for n in range(13):
                items(n, None, last)
                j = n - 2
                if 0 <= j < WCHUNKS:
                    for kt in range(WK * j, min(WK * j + WK, 2 * HEADS - 1)):
                        split_o(kt)
                    split_w(j)
            split_o(2 * HEADS - 1)

            def square(m):
                nb, t = m // TILES, evac_order(m // TILES)[m % TILES]
                act.wait_ge(d_ev.sem, d_ev.at(0, m + 1))
                if m:
                    act.wait_ge(d_sq.sem, d_sq.at(0, m))
                act.activation(junk_out, x_res[:, t, nb * WIDE:(nb + 1) * WIDE], ACT.Square,
                               accum_out=ssq4[:, t, nb:nb + 1]).then_inc(d_sq.sem, 1)

            for m in range(WCHUNKS, OUT_BLOCKS * WCHUNKS):
                nb, j = m // WCHUNKS, m % WCHUNKS
                split_w(m)
                if nb and 2 <= j < 2 + TILES:
                    square((nb - 1) * TILES + j - 2)
            for t in range(TILES):
                square((OUT_BLOCKS - 1) * TILES + t)
            act.wait_ge(fin_steps.sem, fin_steps.at(0, 2))
            act.activation(rstd_o, var_o, ACT.Ln).then_inc(fin_act.sem, 1)
            act.wait_ge(fin_act.sem, fin_act.at(0))
            act.activation(rstd_o, rstd_o, ACT.Exp, scale=-0.5).then_inc(fin_act.sem, 1)

        @block.vector
        def _(dve):
            v = nc.vector
            v.memset(eps_col, EPS)

            def newton(out, x, tmp, step):
                step(v.tensor_tensor(tmp, out, out, ALU.mult))
                step(v.tensor_tensor(tmp, tmp, x, ALU.mult))
                step(v.tensor_scalar(tmp, tmp, -0.5, 1.5, ALU.mult, ALU.add))
                step(v.tensor_tensor(out, out, tmp, ALU.mult))

            def c_step(i, count=[0]):
                count[0] += 1
                i.then_inc(c_steps.sem, 1)
                dve.wait_ge(c_steps.sem, c_steps.at(0, count[0]))

            dve.wait_ge(c_exp.sem, c_exp.at(0))
            c_step(v.tensor_scalar(c_sig, c_sig, 1.0, None, ALU.add))
            c_step(v.reciprocal(c_sig, c_sig))
            c_step(v.tensor_tensor(c_sig, c_sig, c_raw, ALU.mult))
            for w in range(2):
                i = v.tensor_copy(cs[:, :, w * GROUP:(w + 1) * GROUP], c_sig[:, w, :].unsqueeze(2).broadcast_to([P, KT, GROUP]))
            c_step(i)
            for w in range(2):
                i = v.tensor_tensor(cs[:, :, (2 + w) * GROUP:(3 + w) * GROUP], c_sig[:, w, :].unsqueeze(2).broadcast_to([P, KT, GROUP]),
                                    cs[:, :, w * GROUP:(w + 1) * GROUP].bitcast(F32), ALU.subtract)
            i.then_inc(cs_ready.sem, 1)

            def ada_block(nb, extra=None):
                for j in range(WCHUNKS):
                    for kk in range(WK):
                        dve.wait_ge(a_hi.sem, a_hi.at(nb, WK * j + kk + 1))
                        w = slice(kk * WIDE, (kk + 1) * WIDE)
                        v.tensor_tensor(w_lo[:, j % 2, w], ada_raw[:, j, w], w_hi[:, j % 2, w].bitcast(F32),
                                        ALU.subtract).then_inc(a_lo.sem, 1)
                    if extra is not None:
                        extra(j)

            def mod_block(pair, b):
                dve.wait_ge(a_used.sem, a_used.at(2 * pair + b))
                if due(a_store[b], pair - 1):
                    dve.wait_ge(a_store[b].sem, a_store[b].at(pair - 1))
                v.tensor_copy(mod_row[:, b, :], ps[:, b, :]).then_inc(a_row.sem, 1)

            ada_block(0)

            def lg_step(i, count=[0]):
                count[0] += 1
                i.then_inc(lg_steps.sem, 1)
                dve.wait_ge(lg_steps.sem, lg_steps.at(0, count[0]))

            dve.wait_ge(lg_act.sem, lg_act.at(0))
            lg_step(v.tensor_scalar(lgu, lgt, -1.0, 1.0, ALU.mult, ALU.add))
            lg_step(v.tensor_scalar(nlg, lgu, -1.0, 1.0, ALU.mult, ALU.add))
            lg_step(v.tensor_tensor(nlg, nlg, lgt, ALU.subtract))
            lg_step(v.reciprocal(lgu2, lgu))
            lg_step(v.tensor_tensor(nlg, nlg, lgu2, ALU.mult))
            dve.wait_ge(lg_act.sem, lg_act.at(1))
            lg_step(v.tensor_tensor(lg, lg, nlg, ALU.add))
            lg_step(v.tensor_scalar(nlg, lg, -1.0, None, ALU.mult))
            dve.wait_ge(lb_pe.sem, lb_pe.at(0))
            lbp = ps[:, A, 0:4 * HEADS].rearrange("p (s l h) -> p s l h", s=2, l=2)
            lbv = lbT.rearrange("p (s l h) -> p s l h", s=2, l=2)
            lbm3 = lbm.rearrange("p (s h) -> p s h", s=2)
            lg_step(v.tensor_copy(lbT, ps[:, A, 0:4 * HEADS]))
            lg_step(v.tensor_tensor(lbm3, lbv[:, :, 0, :], lbv[:, :, 1, :], ALU.max))
            for l in range(2):
                i = v.tensor_tensor(lbv[:, :, l, :], lbv[:, :, l, :], lbm3, ALU.subtract)
            lg_step(i)
            dve.wait_ge(lg_act.sem, lg_act.at(2))
            lg_step(v.tensor_tensor(lbm3, lbv[:, :, 0, :], lbv[:, :, 1, :], ALU.add))
            lg_step(v.reciprocal(lbm, lbm))
            lg_step(v.tensor_tensor(lb.rearrange("p (s h) -> p s h", s=2), lbv[:, :, 0, :], lbm3, ALU.mult))
            lg_step(v.tensor_scalar(oml, lb, -1.0, 1.0, ALU.mult, ALU.add))
            for s in range(2):
                g = slice(s * HEADS, (s + 1) * HEADS)
                v.tensor_scalar(dbias[:, g], lg[:, g], con[:, C_POS + s:C_POS + s + 1], None, ALU.mult)
                i = v.tensor_scalar(kdec[:, g], lg[:, g], con[:, C_POS + 2 + s:C_POS + 3 + s], None, ALU.mult)
            lg_step(i)

            def rstd_step(i, count=[0]):
                count[0] += 1
                i.then_inc(rstd_steps.sem, 1)
                dve.wait_ge(rstd_steps.sem, rstd_steps.at(0, count[0]))

            def block_1(j):
                if j == 0:
                    dve.wait_ge(x_sq.sem, x_sq.at(TILES - 1))
                    rstd_step(v.tensor_scalar(var, ssq, 1.0 / D_MODEL, EPS, ALU.mult, ALU.add))
                if j == 1:
                    mod_block(0, 0)
                if j == 2:
                    dve.wait_ge(rstd_act.sem, rstd_act.at(1))
                    newton(rstd, var, newt, rstd_step)
                if 3 <= j < 3 + TILES:
                    t = j - 3
                    v.tensor_scalar(x_in[:, t, :], x_in[:, t, :], rstd[:, t:t + 1], None, ALU.mult).then_inc(x_scaled.sem, 1)

            def rows(nb):
                def extra(j):
                    if j == 1:
                        mod_block((nb - 1) // 2, (nb - 1) % 2)
                return extra

            def mod_step(i, count=[0]):
                count[0] += 1
                i.then_inc(mod_steps.sem, 1)
                dve.wait_ge(mod_steps.sem, mod_steps.at(0, count[0]))

            def modulate(k):
                dve.wait_ge(x_evac.sem, x_evac.at(k))
                for w, x in ((0, x_in[:, 0, k::KT]), (1, x_in[:, 1:TILES, k::KT])):
                    i = v.tensor_scalar(x, x, mods[:, w, 1, k:k + 1], mods[:, w, 0, k:k + 1], ALU.mult, ALU.add)
                i.then_inc(h_mod.sem, 1)

            def low_context(half):
                ks = slice(half * KC, (half + 1) * KC)
                dve.wait_ge(ctx_hi.sem, ctx_hi.at(0, half + 1))
                v.tensor_tensor(hT_lo[:, ks, 0:P], x_in[:, 0, :].rearrange("p (n k) -> p k n", k=KT)[:, ks, :],
                                hT_hi[:, ks, 0:P].bitcast(F32), ALU.subtract).then_inc(ctx_lo.sem, 1)

            def with_modulation(nb):
                def extra(j):
                    rows(nb)(j)
                    if nb == ADA_INPUT + 1 and j == 1:
                        dve.wait_ge(mods_in.sem, mods_in.at(1))
                        mod_step(v.tensor_tensor(mods, mod_cols[:, 0:2, 0:2, :], mod_cols[:, 2:4, 0:2, :], ALU.add))
                        mod_step(v.tensor_tensor(mods, mods, bias_cols[:, 0:2, :].unsqueeze(1).broadcast_to([P, 2, 2, KT]), ALU.add))
                        for w in range(2):
                            i = v.scalar_tensor_tensor(out=mods[:, w, 1, :], in0=mods[:, w, 1, :], scalar=1.0, in1=nw,
                                                       op0=ALU.add, op1=ALU.mult)
                        mod_step(i)
                    k = (nb - ADA_INPUT - 1) * WCHUNKS + j - 2
                    if 0 <= k < KT:
                        modulate(k)
                return extra

            ada_block(1, block_1)
            for nb in range(2, 4):
                ada_block(nb, rows(nb))
            with dve.Fori(2, ADA_INPUT // 2) as pair:
                for b in range(2):
                    nb = 2 * pair + b
                    def extra(j):
                        if j == 1:
                            mod_block(pair - 1 + b, 1 - b)
                    ada_block(nb, extra)
            for nb in range(ADA_INPUT, ADA_BLOCKS):
                ada_block(nb, with_modulation(nb))
            mod_block(ADA_BLOCKS // 2 - 1, 1)

            def split(h, n):
                dve.wait_ge(wt_hi.sem, wt_hi.at(h, n + 1))
                v.tensor_tensor(w_lo[:, n % 2, :], raw[:, n % 3, :], w_hi[:, n % 2, :].bitcast(F32),
                                ALU.subtract).then_inc(wt_lo.sem, 1)

            def reciprocal_half(buf, half, signal):
                part = buf[:, half * HALF:(half + 1) * HALF]
                v.reciprocal(part, part).then_inc(signal.sem, 1)

            def items(n, h, prev):
                if prev is not None:
                    if n == 0:
                        dve.wait_ge(r_rms.sem, r_rms.at(prev, 2))
                        v.tensor_tensor(rr[:, P:T], ps[:, A, :], rr[:, P:T], ALU.mult)
                        v.tensor_tensor(rr[:, 0:P], ps[:, BB, 0:P], rr[:, 0:P], ALU.mult).then_inc(r_out.sem, 1)
                        dve.wait_ge(r_out.sem, r_out.at(prev, 1))
                        dve.wait_ge(r_silu.sem, r_silu.at(prev))
                        v.tensor_tensor(rr, rr, rsg, ALU.mult).then_inc(r_out.sem, 1)
                        dve.wait_ge(h_eb.sem, h_eb.at(prev))
                        v.tensor_copy(dec[:, 0, :], tiles(F[:, 0, :])[:, :, P - 1])
                        v.tensor_copy(dec[:, 1, :], tiles(F[:, 1, :])[:, :, 0]).then_inc(h_dec.sem, 1)
                        dve.wait_ge(h_dec.sem, h_dec.at(prev))
                        for s in range(2):
                            i = v.tensor_tensor(F[:, s, :], F[:, s, :], hq, ALU.mult)
                        i.then_inc(h_qr.sem, 1)
                    if n == 1:
                        dve.wait_ge(h_eg.sem, h_eg.at(prev))
                        v.tensor_scalar(hsg, hsg, 1.0, None, ALU.add).then_inc(h_silu.sem, 1)
                        dve.wait_ge(h_silu.sem, h_silu.at(prev, 1))
                        reciprocal_half(hsg, 0, h_silu)
                    if n == 2:
                        reciprocal_half(hsg, 1, h_silu)
                        dve.wait_ge(h_silu.sem, h_silu.at(prev, 3))
                        v.tensor_tensor(hsg, hsg, graw, ALU.mult).then_inc(h_silu.sem, 1)
                    if 1 <= n <= LEVELS:
                        level = n - 1
                        half = P >> (level + 1)
                        buf = XE[:, level % 2, 0, :]
                        bf, bb, x = blocks(B[:, 0, :], level), blocks(B[:, 1, :], level), blocks(buf, level)
                        nblk = T // (2 * half)
                        if due(pe_level, prev, level - 1):
                            dve.wait_ge(pe_level.sem, pe_level.at(prev, level - 1))
                        v.tensor_tensor(x[:, :, half:2 * half], bf[:, :, half:2 * half],
                                        bf[:, :, half - 1:half].broadcast_to([P, nblk, half]), ALU.subtract)
                        v.tensor_tensor(x[:, :, 0:half], bb[:, :, 0:half],
                                        bb[:, :, half:half + 1].broadcast_to([P, nblk, half]), ALU.subtract).then_inc(xq.sem, 1)
                        dve.wait_ge(xe.sem, xe.at(prev, level + 1))
                        v.tensor_tensor(buf, buf, hq, ALU.mult).then_inc(lq.sem, 1)
                    if n == 3:
                        dve.wait_ge(pe_hu.sem, pe_hu.at(prev))
                        dve.wait_ge(h_S0.sem, h_S0.at(prev))
                        if due(pe_ho, prev - 1):
                            dve.wait_ge(pe_ho.sem, pe_ho.at(prev - 1))
                        for i in range(3):
                            v.scalar_tensor_tensor(out=S[:, 0, i + 1, :], in0=S[:, 0, i, :], scalar=dec[:, 0, i + 1:i + 2],
                                                   in1=ps[:, C, tile_cols(i + 1)], op0=ALU.mult, op1=ALU.add)
                            v.scalar_tensor_tensor(out=S[:, 1, 2 - i, :], in0=S[:, 1, 3 - i, :], scalar=dec[:, 1, 4 - i:5 - i],
                                                   in1=ps[:, DD, tile_cols(3 - i)], op0=ALU.mult, op1=ALU.add).then_inc(h_S.sem, 1)
                            dve.wait_ge(h_S.sem, h_S.at(prev, i + 1))
                    if 3 <= n < 3 + PRODUCTS:
                        level = n - 3
                        scored, placed = pe_level.at(prev, level + 1), h_sT.at(prev, level)
                        if not isinstance(prev, int):
                            scored, placed = dve.to_reg(scored), dve.to_reg(placed)
                        if level:
                            dve.wait_ge(con_in.sem, con_in.at(0))
                        dve.wait_ge(pe_level.sem, scored)
                        out = tiles(hsT[:, P:T])
                        if level == 0:
                            if due(pe_ho, prev - 1):
                                dve.wait_ge(pe_ho.sem, pe_ho.at(prev - 1))
                            v.tensor_copy(out, tiles(ps[:, A, :]))
                            v.tensor_copy(hsT[:, 0:P], ctx_scores(h, level)).then_inc(h_sT.sem, 1)
                        else:
                            dve.wait_ge(h_sT.sem, placed)
                            v.copy_predicated(out, mask(level).unsqueeze(1).broadcast_to([P, TILES - 1, P]), tiles(ps[:, A, :]))
                            v.copy_predicated(hsT[:, 0:P], mask(level), ctx_scores(h, level)).then_inc(h_sT.sem, 1)
                    if n == 12:
                        dve.wait_ge(h_rms.sem, h_rms.at(prev, 2))
                        v.scalar_tensor_tensor(out=hr[:, P:T], in0=ps[:, C, :], scalar=hnw, in1=hr[:, P:T], op0=ALU.mult, op1=ALU.mult)
                        v.scalar_tensor_tensor(out=hr[:, 0:P], in0=ps[:, DD, 0:P], scalar=hnw, in1=hr[:, 0:P],
                                               op0=ALU.mult, op1=ALU.mult).then_inc(h_out.sem, 1)
                        dve.wait_ge(h_out.sem, h_out.at(prev, 1))
                        v.tensor_tensor(hr, hr, hsg, ALU.mult).then_inc(h_out.sem, 1)
                if h is None:
                    return
                if n == 4 and prev is None:
                    dve.wait_ge(gate_in.sem, gate_in.at(0))
                    v.tensor_tensor(gate_cols, mod_cols[:, 0:2, 2, :], mod_cols[:, 2:4, 2, :], ALU.add).then_inc(gate_steps.sem, 1)
                    dve.wait_ge(gate_steps.sem, gate_steps.at(0))
                    v.tensor_tensor(gate_cols, gate_cols, bias_cols[:, 2, :].unsqueeze(1).broadcast_to([P, 2, KT]), ALU.add).then_inc(gate_steps.sem, 1)
                if n == 8:
                    dve.wait_ge(r_eg.sem, r_eg.at(h))
                    v.tensor_scalar(rsg, rsg, 1.0, None, ALU.add).then_inc(r_silu.sem, 1)
                    dve.wait_ge(r_silu.sem, r_silu.at(h, 1))
                    reciprocal_half(rsg, 0, r_silu)
                if n == 9:
                    reciprocal_half(rsg, 1, r_silu)
                    dve.wait_ge(r_silu.sem, r_silu.at(h, 3))
                    v.tensor_tensor(halves(rsg), halves(rsg), proj(3), ALU.mult).then_inc(r_silu.sem, 1)
                if n == 12:
                    tmp = sT[:, 0:REL]
                    if due(r_sT, h - 1):
                        dve.wait_ge(r_sT.sem, r_sT.at(h - 1))
                    if due(pe_rss, h - 1):
                        dve.wait_ge(pe_rss.sem, pe_rss.at(h - 1))
                    v.tensor_scalar(strip, rel, 0.0, lg[:, bass.ds(h, 1)], ALU.max, ALU.mult).then_inc(strip_x.sem, 1)
                    v.tensor_scalar(tmp, rel, 0.0, nlg[:, bass.ds(h + HEADS, 1)], ALU.min, ALU.mult).then_inc(strip_x.sem, 1)
                    dve.wait_ge(strip_x.sem, strip_x.at(h, 2))
                    v.tensor_tensor(strip, strip, tmp, ALU.add).then_inc(strip_x.sem, 1)
                if n == 13:
                    dve.wait_ge(pe_rswap.sem, pe_rswap.at(h))
                    if due(r_stored, h - 1):
                        dve.wait_ge(r_stored.sem, r_stored.at(h - 1))
                    v.tensor_tensor(rope_q, ps[:, A, :], sin, ALU.mult)
                    v.tensor_tensor(rope_k, ps[:, BB, :], sin, ALU.mult).then_inc(rope_sin.sem, 1)
                    dve.wait_ge(rope_sin.sem, rope_sin.at(h))
                    dve.wait_ge(rope_cos.sem, rope_cos.at(h))
                    v.tensor_tensor(rq[:, P:T], rq[:, P:T], rope_q, ALU.add)
                    v.tensor_tensor(rk[:, P:T], rk[:, P:T], rope_k, ALU.add).then_inc(roped.sem, 1)
                    dve.wait_ge(strip_e.sem, strip_e.at(h))
                    diag = strip[:, REL - LAT:REL - LAT + P]
                    v.tensor_tensor(diag, diag, ident, ALU.add).then_inc(strip_i.sem, 1)
                if 12 <= n <= 15:
                    s, odd = (n - 12) // 2, n % 2
                    buf, at = F[:, s, :], 5 * s
                    col = bass.ds(s * HEADS + h, 1)
                    if odd == 0:
                        dve.wait_ge(h_ez.sem, h_ez.at(h, s + 1))
                        v.tensor_scalar(buf, buf, 1.0, None, ALU.add).then_inc(h_gate.sem, 1)
                        dve.wait_ge(h_gate.sem, h_gate.at(h, at + 1))
                        reciprocal_half(buf, 0, h_gate)
                    else:
                        reciprocal_half(buf, 1, h_gate)
                        dve.wait_ge(h_gate.sem, h_gate.at(h, at + 3))
                        v.tensor_scalar(buf, buf, oml[:, col], lb[:, col], ALU.mult, ALU.add).then_inc(h_gate.sem, 1)
                        dve.wait_ge(h_gate.sem, h_gate.at(h, at + 4))
                        if due(la, h - 1):
                            dve.wait_ge(la.sem, la.at(h - 1))
                        v.tensor_scalar(K[:, s, :], buf, -1.0, 1.0, ALU.mult, ALU.add).then_inc(h_gate.sem, 1)
                if n == 15 or n == 16:
                    if n == 15:
                        dve.wait_ge(strip_i.sem, strip_i.at(h))
                        dve.wait_ge(roped.sem, roped.at(h))
                    for jt in range(2 * (n - 15), 2 * (n - 15) + 2):
                        dve.wait_ge(pe_rs.sem, pe_rs.at(h, jt + 1))
                        off = REL - LAT - jt * P
                        v.tensor_tensor(sT[:, jt * LAT:(jt + 1) * LAT], ps[:, A + jt % 2, :], strip[:, off:off + LAT],
                                        ALU.mult).then_inc(r_sT.sem, 1)
                    if n == 16:
                        dve.wait_ge(pe_rs.sem, pe_rs.at(h, 5))
                        v.tensor_tensor(sT[:, 4 * LAT:4 * LAT + P], ps[:, C, 0:P], strip[:, REL - LAT:REL - LAT + P],
                                        ALU.mult).then_inc(r_sT.sem, 1)
                if n == 15:
                    dve.wait_ge(h_log.sem, h_log.at(h, 1))
                    v.tensor_tensor_scan(B[:, 0, :], reset, F[:, 0, :], 0.0, ALU.mult, ALU.add).then_inc(h_scan.sem, 1)
                if n == 17:
                    dve.wait_ge(h_log.sem, h_log.at(h, 2))
                    v.tensor_tensor_scan(B[:, 1, ::-1], reset, F[:, 1, ::-1], 0.0, ALU.mult, ALU.add).then_inc(h_scan.sem, 1)
                    dve.wait_ge(h_scan.sem, h_scan.at(h))
                    if due(h_stored, h - 1):
                        dve.wait_ge(h_stored.sem, h_stored.at(h - 1))
                    bf, bb = tiles(B[:, 0, :]), tiles(B[:, 1, :])
                    v.tensor_tensor(tiles(KL[:, 0, :]), bf[:, :, P - 1:P].broadcast_to([P, TILES, P]), bf, ALU.subtract)
                    v.tensor_tensor(tiles(KL[:, 1, :]), bb[:, :, 0:1].broadcast_to([P, TILES, P]), bb, ALU.subtract).then_inc(h_klx.sem, 1)

            def head(h, prev):
                for n in range(CHUNKS):
                    if prev is None and n < 2:
                        low_context(n)
                    split(h, n)
                    if n == 0:
                        if prev is not None:
                            items(CHUNKS - 1, prev, None)
                    else:
                        items(n - 1, h, prev)

            head(0, None)
            head(1, 0)
            with dve.Fori(2, HEADS) as h:
                head(h, h - 1)
            last = HEADS - 1
            items(CHUNKS - 1, last, None)

            def split_o(kt):
                dve.wait_ge(o_hi.sem, o_hi.at(kt))
                src = hr if kt == 2 * HEADS - 1 else o_raw[:, kt % STAGES, :]
                v.tensor_tensor(hT_lo[:, kt, :], src, hT_hi[:, kt, :].bitcast(F32), ALU.subtract).then_inc(o_lo.sem, 1)

            def split_w(m):
                dve.wait_ge(d_hi.sem, d_hi.at(0, m + 1))
                v.tensor_tensor(w_lo[:, m % 2, :], raw[:, m % 2, :], w_hi[:, m % 2, :].bitcast(F32), ALU.subtract).then_inc(d_lo.sem, 1)

            for n in range(13):
                items(n, None, last)
                j = n - 2
                if 0 <= j < WCHUNKS:
                    for kt in range(WK * j, min(WK * j + WK, 2 * HEADS - 1)):
                        split_o(kt)
                    split_w(j)
            split_o(2 * HEADS - 1)

            def gate_part(m):
                nb, t = m // TILES, evac_order(m // TILES)[m % TILES]
                dve.wait_ge(d_used.sem, d_used.at(nb))
                if m == 0:
                    dve.wait_ge(gates_in.sem, gates_in.at(2))
                    dve.wait_ge(res_in.sem, res_in.at(1))
                if m >= 2:
                    if due(d_ev, 0, m - 1):
                        dve.wait_ge(d_ev.sem, d_ev.at(0, m - 1))
                v.tensor_tensor(gated[:, m % 2, :], ps[:, out_bank(nb, t), :],
                                gates[:, 0 if t == 0 else 1, nb * WIDE:(nb + 1) * WIDE], ALU.mult).then_inc(d_gated.sem, 1)

            def add_part(m):
                nb, t = m // TILES, evac_order(m // TILES)[m % TILES]
                dve.wait_ge(d_gated.sem, d_gated.at(0, m + 1))
                x = x_res[:, t, nb * WIDE:(nb + 1) * WIDE]
                v.tensor_tensor(x, x, gated[:, m % 2, :], ALU.add).then_inc(d_ev.sem, 1)

            def finish_block(nb):
                for m in range(nb * TILES, (nb + 1) * TILES):
                    gate_part(m)
                    if m > nb * TILES:
                        add_part(m - 1)
                add_part((nb + 1) * TILES - 1)

            for m in range(WCHUNKS, OUT_BLOCKS * WCHUNKS):
                nb, j = m // WCHUNKS, m % WCHUNKS
                split_w(m)
                if nb and j == 1:
                    finish_block(nb - 1)
            finish_block(OUT_BLOCKS - 1)

            def fin_step(i, count=[0]):
                count[0] += 1
                i.then_inc(fin_steps.sem, 1)
                dve.wait_ge(fin_steps.sem, fin_steps.at(0, count[0]))

            dve.wait_ge(d_sq.sem, d_sq.at(OUT_BLOCKS - 1))
            fin_step(v.reduce_sum(ssq_out, ssq4, AX_X))
            fin_step(v.tensor_scalar(var_o, ssq_out, 1.0 / D_MODEL, EPS, ALU.mult, ALU.add))
            dve.wait_ge(fin_act.sem, fin_act.at(1))
            newton(rstd_o, var_o, newt_o, fin_step)
            for t in range(TILES):
                v.scalar_tensor_tensor(out=x_res[:, t, :], in0=x_res[:, t, :], scalar=rstd_o[:, t:t + 1], in1=fnw,
                                       op0=ALU.mult, op1=ALU.mult).then_inc(y_ready.sem, 1)

        @block.gpsimd
        def _(pool):
            g = nc.gpsimd

            def items(n, h, prev):
                if prev is not None:
                    if n == 0:
                        pool.wait_ge(h_ekl.sem, h_ekl.at(prev))
                        g.tensor_tensor(KL, KL, K, ALU.mult).then_inc(h_kl.sem, 1)
                    if 1 <= n <= LEVELS:
                        level = n - 1
                        half = P >> (level + 1)
                        buf = XE[:, level % 2, 1, :]
                        bf, bb, x = blocks(B[:, 0, :], level), blocks(B[:, 1, :], level), blocks(buf, level)
                        kf, kb = blocks(K[:, 0, :], level), blocks(K[:, 1, :], level)
                        nblk = T // (2 * half)
                        left, right = slice(0, half), slice(half, 2 * half)
                        pool.wait_ge(h_scan.sem, h_scan.at(prev))
                        if due(pe_level, prev, level - 1):
                            pool.wait_ge(pe_level.sem, pe_level.at(prev, level - 1))
                        g.tensor_tensor(x[:, :, left], bf[:, :, half - 1:half].broadcast_to([P, nblk, half]), bf[:, :, left], ALU.subtract)
                        g.tensor_tensor(x[:, :, right], bb[:, :, half:half + 1].broadcast_to([P, nblk, half]), bb[:, :, right],
                                        ALU.subtract).then_inc(xa.sem, 1)
                        pool.wait_ge(xe.sem, xe.at(prev, level + 1))
                        g.tensor_tensor(x[:, :, left], x[:, :, left], kf[:, :, left], ALU.mult)
                        g.tensor_tensor(x[:, :, right], x[:, :, right], kb[:, :, right], ALU.mult).then_inc(la.sem, 1)
                    if n == LEVELS + 1:
                        if due(pe_level, prev, LEVELS - 1):
                            pool.wait_ge(pe_level.sem, pe_level.at(prev, LEVELS - 1))
                        g.tensor_tensor(XE[:, 1, 1, :], K[:, 0, :], K[:, 1, :], ALU.add).then_inc(la.sem, 1)
                if h is None:
                    return
                if n == 13:
                    pool.wait_ge(pe_rswap.sem, pe_rswap.at(h))
                    g.tensor_tensor(rq[:, P:T], rq[:, P:T], cos, ALU.mult)
                    g.tensor_tensor(rk[:, P:T], rk[:, P:T], cos, ALU.mult).then_inc(rope_cos.sem, 1)
                if n == 15:
                    pool.wait_ge(r_dec.sem, r_dec.at(h))
                    pool.wait_ge(roped.sem, roped.at(h))
                    for s in range(2):
                        i = g.tensor_tensor(rqd[:, s, :], rqd[:, s, :], rq[:, P:T], ALU.mult)
                    i.then_inc(r_qdec.sem, 1)

            def head(h, prev):
                for n in range(CHUNKS):
                    items(n, h, prev)

            for k in range(KT):
                pool.wait_ge(h_hi.sem, h_hi.at(k))
                g.tensor_tensor(tiles(hT_lo[:, k, P:T]), x_in[:, 1:TILES, k::KT], tiles(hT_hi[:, k, P:T].bitcast(F32)),
                                ALU.subtract).then_inc(h_lo.sem, 1)

            head(0, None)
            head(1, 0)
            with pool.Fori(2, HEADS) as h:
                head(h, h - 1)
            for n in range(LEVELS + 2):
                items(n, None, HEADS - 1)

        @block.tensor
        def _(pe):
            mm = nc.tensor.matmul
            pe.wait_ge(cs_ready.sem, cs_ready.at(0))

            def ada_block(nb, b, extra=None):
                for j in range(WCHUNKS):
                    if j == 0:
                        if due(a_row, nb - 2):
                            pe.wait_ge(a_row.sem, a_row.at(nb - 2))
                    for kk in range(WK):
                        k = j * WK + kk
                        pe.wait_ge(a_lo.sem, a_lo.at(nb, k + 1))
                        w = slice(kk * WIDE, (kk + 1) * WIDE)
                        mm(ps[:, b, :], cs[:, k, :], w_hi[:, j % 2, w], start=k == 0, stop=False)
                        mm(ps[:, b, :], cs[:, k, :], w_lo[:, j % 2, w], start=False, stop=k == KT - 1).then_inc(a_used.sem, 1)
                    if extra is not None:
                        extra(j)

            def transposes(nb):
                def extra(j):
                    k = (nb - 2) * WCHUNKS + j
                    bank = 4 + 2 * (k % 2)
                    if k == 0:
                        pe.wait_ge(x_scaled.sem, x_scaled.at(TILES - 1))
                    if k >= 2:
                        if due(x_evac, k - 2):
                            pe.wait_ge(x_evac.sem, x_evac.at(k - 2))
                    for t in range(1, TILES):
                        nc.tensor.transpose(ps[:, bank, tile_cols(t - 1)], x_in[:, t, k::KT], ident)
                    nc.tensor.transpose(ps[:, bank + 1, 0:P], x_in[:, 0, k::KT], ident).then_inc(x_tr.sem, 1)
                return extra

            ada_block(0, 0)
            pe.wait_ge(con_in.sem, con_in.at(0))
            pe.wait_ge(small_in.sem, small_in.at(4))
            nc.tensor.transpose(ps[:, A, 0:4 * HEADS], lb_in, con[0:4 * HEADS, C_IDENT:C_IDENT + 4 * HEADS]).then_inc(lb_pe.sem, 1)
            ada_block(1, 1)
            for nb in range(2, 4):
                ada_block(nb, nb % 2, transposes(nb))
            with pe.Fori(2, ADA_BLOCKS // 2) as pair:
                for b in range(2):
                    ada_block(2 * pair + b, b)
            pe.wait_ge(h_lo.sem, h_lo.at(KT - 1))

            freed = {0: (h_graw, 1, None), 1: (h_v, 1, None), 2: (r_q, 0, None), 3: (r_k, 0, None), 4: (r_v, 0, None),
                     5: (r_silu, 0, 4), 6: (h_q, 0, None), 7: (h_ez, 0, 1), 8: (h_ez, 0, 2)}

            def chunk(h, n):
                i, half = n // 2, n % 2
                if isinstance(h, int) and h == 0 and n < 2:
                    pe.wait_ge(ctx_lo.sem, ctx_lo.at(0, n + 1))
                pe.wait_ge(wt_lo.sem, wt_lo.at(h, n + 1))
                if half == 0:
                    signal, back, k = freed[i]
                    if due(signal, h - back, k):
                        pe.wait_ge(signal.sem, signal.at(h - back, k))
                out = [ps[:, 2 * (i % 2) + s, 0:HALF] for s in range(2)]
                for kk in range(KC):
                    k = half * KC + kk
                    w = slice(kk * P, (kk + 1) * P)
                    for step, (wt, x) in enumerate(((w_hi, hT_hi), (w_hi, hT_lo), (w_lo, hT_hi))):
                        for s in range(2):
                            ins = mm(out[s], wt[:, n % 2, w], x[:, k, s * HALF:(s + 1) * HALF],
                                     start=k == 0 and step == 0, stop=k == KT - 1 and step == 2)
                ins.then_inc(wt_used.sem, 1)

            def stage(n, h, prev):
                if prev is not None:
                    if n == 0:
                        pe.wait_ge(h_v.sem, h_v.at(prev))
                        pe.wait_ge(r_out.sem, r_out.at(prev, 1))
                        for t in range(1, TILES):
                            nc.tensor.transpose(ps[:, A, tile_cols(t - 1)], hvT[:, tile_cols(t)], ident)
                        nc.tensor.transpose(ps[:, BB, 0:P], hvT[:, 0:P], ident).then_inc(pe_htok.sem, 1)
                    if n == 1:
                        pe.wait_ge(h_kl.sem, h_kl.at(prev))
                        for i, t in enumerate((0, 1, 2, 3)):
                            nc.tensor.transpose(ps[:, C, tile_cols(i)], KL[:, 0, tile_cols(t)], ident)
                        for i, t in enumerate((0, 2, 3, 4)):
                            ins = nc.tensor.transpose(ps[:, DD, tile_cols(i)], KL[:, 1, tile_cols(t)], ident)
                        ins.then_inc(pe_hkl.sem, 1)
                    if n == 2:
                        pe.wait_ge(h_kltok.sem, h_kltok.at(prev))
                        pe.wait_ge(h_tok.sem, h_tok.at(prev))
                        for i, t in enumerate((0, 1, 2, 3)):
                            mm(ps[:, C, tile_cols(i)], kltok[:, i, :], htok[:, t, :], start=True, stop=True)
                        for i, t in enumerate((0, 2, 3, 4)):
                            ins = mm(ps[:, DD, tile_cols(i)], kltok[:, 4 + i, :], htok[:, t, :], start=True, stop=True)
                        ins.then_inc(pe_hu.sem, 1)
                    if 2 <= n < 2 + PRODUCTS:
                        level = n - 2
                        b = level % 2
                        pe.wait_ge(la.sem, la.at(prev, level + 1))
                        if level < LEVELS:
                            pe.wait_ge(lq.sem, lq.at(prev, level + 1))
                            q = XE[:, b, 0, :]
                        else:
                            q = hq
                        if level:
                            if due(h_sT, prev, level):
                                pe.wait_ge(h_sT.sem, h_sT.at(prev, level))
                        for t in range(1, TILES):
                            mm(ps[:, A, tile_cols(t - 1)], XE[:, b, 1, tile_cols(t)], q[:, tile_cols(t)], start=True, stop=True)
                        if h is None and level == 1:
                            pe.wait_ge(h_S.sem, h_S.at(prev))
                            pe.wait_ge(h_state.sem, h_state.at(prev))
                        mm(ctx_scores(h, level), XE[:, b, 1, 0:P], q[:, 0:P], start=True, stop=True).then_inc(pe_level.sem, 1)
                    if n == 10:
                        pe.wait_ge(h_sT.sem, h_sT.at(prev))
                        pe.wait_ge(h_S.sem, h_S.at(prev))
                        pe.wait_ge(h_qr.sem, h_qr.at(prev))
                        pe.wait_ge(h_state.sem, h_state.at(prev))
                        for t in range(1, TILES):
                            out = ps[:, C, tile_cols(t - 1)]
                            mm(out, htok[:, t, :], hsT[:, tile_cols(t)], start=True, stop=False)
                            mm(out, S[:, 0, t - 1, :], F[:, 0, tile_cols(t)], start=False, stop=False)
                            mm(out, S[:, 1, t - 1, :], F[:, 1, tile_cols(t)], start=False, stop=True)
                        mm(ps[:, DD, 0:P], htok[:, 0, :], hsT[:, 0:P], start=True, stop=True).then_inc(pe_ho.sem, 1)
                    if n == 11:
                        pe.wait_ge(h_sq.sem, h_sq.at(prev))
                        mm(ps[:, A, :], ones, hsq[:, P:T], start=True, stop=True)
                        mm(ctx_sums(h), ones, hsq[:, 0:P], start=True, stop=True).then_inc(pe_hss.sem, 1)
                if h is None:
                    return
                if n == 12:
                    pe.wait_ge(r_q.sem, r_q.at(h))
                    pe.wait_ge(r_k.sem, r_k.at(h))
                    if due(h_rms, h - 1, 1):
                        pe.wait_ge(h_rms.sem, h_rms.at(h - 1, 1))
                    mm(ps[:, A, :], swap, rq[:, P:T], start=True, stop=True)
                    mm(ps[:, BB, :], swap, rk[:, P:T], start=True, stop=True).then_inc(pe_rswap.sem, 1)
                if n == 13:
                    pe.wait_ge(r_v.sem, r_v.at(h))
                    if due(h_out, h - 1, 1):
                        pe.wait_ge(h_out.sem, h_out.at(h - 1, 1))
                    for t in range(1, TILES):
                        nc.tensor.transpose(ps[:, C, tile_cols(t - 1)], rvT[:, tile_cols(t)], ident)
                    nc.tensor.transpose(ps[:, DD, 0:P], rvT[:, 0:P], ident)
                    nc.tensor.transpose(ps[:, DD, P:2 * P], rk[:, 0:P], ident).then_inc(pe_rtok.sem, 1)
                if n == 14 or n == 15:
                    pe.wait_ge(roped.sem, roped.at(h))
                    for jt in range(2 * (n - 14), 2 * (n - 14) + 2):
                        if jt >= 2:
                            if due(r_sT, h, jt - 1):
                                pe.wait_ge(r_sT.sem, r_sT.at(h, jt - 1))
                        mm(ps[:, A + jt % 2, :], rk[:, tile_cols(1 + jt)], rq[:, P:T], start=True, stop=True).then_inc(pe_rs.sem, 1)
                    if n == 15:
                        pe.wait_ge(r_tok.sem, r_tok.at(h))
                        mm(ps[:, C, 0:P], rk[:, 0:P], rq[:, 0:P], start=True, stop=True).then_inc(pe_rs.sem, 1)
                if n == 16:
                    pe.wait_ge(r_sT.sem, r_sT.at(h))
                    pe.wait_ge(r_qdec.sem, r_qdec.at(h))
                    pe.wait_ge(r_S0.sem, r_S0.at(h))
                    for jt in range(4):
                        mm(ps[:, A, :], rtok[:, 1 + jt, :], sT[:, jt * LAT:(jt + 1) * LAT], start=jt == 0, stop=False)
                    for s in range(2):
                        mm(ps[:, A, :], rS0[:, s, :], rqd[:, s, :], start=False, stop=s == 1)
                    mm(ps[:, BB, 0:P], rtok[:, 0, :], sT[:, 4 * LAT:4 * LAT + P], start=True, stop=True)
                    for s in range(2):
                        ins = mm(ps[:, DD, tile_cols(s)], kts[:, s, :], rtok[:, 0, :], start=True, stop=True)
                    ins.then_inc(pe_ro.sem, 1)
                if n == 17:
                    pe.wait_ge(r_sq.sem, r_sq.at(h))
                    pe.wait_ge(r_state.sem, r_state.at(h))
                    mm(ps[:, C, :], ones, rsq[:, P:T], start=True, stop=True)
                    mm(ps[:, DD, 0:P], ones, rsq[:, 0:P], start=True, stop=True).then_inc(pe_rss.sem, 1)

            def head(h, prev):
                for n in range(CHUNKS):
                    chunk(h, n)
                    stage(n, h, prev)

            head(0, None)
            head(1, 0)
            with pe.Fori(2, HEADS) as h:
                head(h, h - 1)
            last = HEADS - 1

            def out_tile(nb, j, kk, t):
                m, k = nb * WCHUNKS + j, j * WK + kk
                w = slice(kk * WIDE, (kk + 1) * WIDE)
                out = ps[:, out_bank(nb, t), :]
                mm(out, hT_hi[:, k, tile_cols(t)], w_hi[:, m % 2, w], start=k == 0, stop=False)
                mm(out, hT_hi[:, k, tile_cols(t)], w_lo[:, m % 2, w], start=False, stop=False)
                return mm(out, hT_lo[:, k, tile_cols(t)], w_hi[:, m % 2, w], start=False, stop=k == KT - 1)

            def first_block(j, kk):
                pe.wait_ge(d_lo.sem, d_lo.at(0, j + 1))
                pe.wait_ge(o_lo.sem, o_lo.at(WK * j + kk))
                if j == 0 and kk == 0:
                    pe.wait_ge(h_graw.sem, h_graw.at(last))
                    pe.wait_ge(h_v.sem, h_v.at(last))
                for t in range(TILES):
                    i = out_tile(0, j, kk, t)
                if kk == WK - 1:
                    i.then_inc(d_used.sem, 1)

            for n in range(12):
                stage(n, None, last)
                if 3 <= n < 10:
                    for kk in range(WK):
                        first_block(n - 3, kk)
                if n == 10:
                    first_block(WCHUNKS - 1, 0)
            first_block(WCHUNKS - 1, 1)

            for nb in range(1, OUT_BLOCKS):
                for j in range(WCHUNKS):
                    m = nb * WCHUNKS + j
                    pe.wait_ge(d_lo.sem, d_lo.at(0, m + 1))
                    for t in range(TILES):
                        if j == 0 and nb % 2 == 0 and t < 2:
                            if due(d_ev, nb - 1, t + 1):
                                pe.wait_ge(d_ev.sem, d_ev.at(nb - 1, t + 1))
                        if j == 0 and nb % 2 == 1:
                            if t == 0:
                                if due(d_ev, nb - 2):
                                    pe.wait_ge(d_ev.sem, d_ev.at(nb - 2))
                            if t >= 3:
                                if due(d_ev, nb - 1, t - 2):
                                    pe.wait_ge(d_ev.sem, d_ev.at(nb - 1, t - 2))
                        for kk in range(WK):
                            i = out_tile(nb, j, kk, t)
                    i.then_inc(d_used.sem, 1)


_INS = ["x_prompt", "x_sample", "state_ret_fwd", "state_ret_bwd", "state_hgrn_fwd", "state_hgrn_bwd", "c", "c_ctx",
        "norm_w", "w_ada", "b_ada", "w_in", "ret_decay", "hg_lower_bounds", "hg_norm_w", "w_out", "final_norm_w"]
_STATE = (1, 1, HEADS, P, P)
_OUTS = [(1, CTX, D_MODEL), (1, LAT, D_MODEL), _STATE, _STATE, _STATE, _STATE]


def _constants():
    import numpy as np

    con = np.zeros((P, NCONST), np.float32)
    p = np.arange(P)
    con[:, C_IDENT:C_IDENT + P] = np.eye(P)
    con[p ^ 32, C_SWAP + p] = 1.0
    con[:, C_ONES:C_ONES + P] = 1.0
    quarter = P // 4
    freqs = (np.float32(ROPE_BASE) ** (-np.arange(quarter, dtype=np.float32) / np.float32(quarter))).astype(np.float32)
    tok = np.arange(LAT)
    pos = np.stack([tok // GRID_W, tok % GRID_W]).astype(np.float32)
    ang = (pos[p // (2 * quarter)] * freqs[p % quarter][:, None]).astype(np.float32)
    sign = np.where((p // quarter) % 2 == 0, -1.0, 1.0)[:, None]
    con[:, C_COS:C_COS + LAT] = np.cos(ang)
    con[:, C_SIN:C_SIN + LAT] = sign * np.sin(ang)
    con[:, C_REL:C_REL + REL] = np.arange(REL)[None, :] - (REL - LAT) - p[:, None]
    for level in range(1, PRODUCTS):
        size = P >> level
        con[:, C_MASK + (level - 1) * P:C_MASK + level * P] = p[:, None] // size == p[None, :] // size
    con[:, C_RESET:C_RESET + T] = np.arange(T) % P != 0
    con[:, C_POS:C_POS + 4] = np.stack([p + 1, LAT - p, P - 1 - p, p], 1)
    return con


def kernel(**inputs):
    import numpy as np
    import concourse.bacc as bacc
    from concourse.bass_utils import run_bass_kernel_spmd

    nc = bacc.Bacc("TRN2", target_bir_lowering=False, num_devices=1)
    arrays, args = {}, []
    for name in _INS:
        a = np.ascontiguousarray(inputs[name])
        arrays[f"in_{name}"] = a
        args.append(nc.dram_tensor(f"in_{name}", a.shape, F32, kind="ExternalInput").ap())
    con = _constants()
    arrays["in_constants"] = con
    args.append(nc.dram_tensor("in_constants", con.shape, F32, kind="ExternalInput").ap())
    for i, shape in enumerate(_OUTS):
        args.append(nc.dram_tensor(f"out_{i}", shape, F32, kind="ExternalOutput").ap())
    layer(nc, *args)
    r = run_bass_kernel_spmd(nc, [arrays], core_ids=[0])
    return tuple(r.results[0][f"out_{i}"] for i in range(len(_OUTS)))
```

```python
from contextlib import ExitStack

import concourse.bass as bass
from concourse import mybir

P = 128
D_MODEL = 2048
KT = D_MODEL // P
CTX, LAT = 128, 512
T = CTX + LAT
TILES = T // P
HALF = T // 2
HEADS = 8
PARTS = 9
HEAD_COLS = HEADS * P
CHUNKS = 2 * PARTS
KC = KT // 2
CHUNK_COLS = KC * P
WIDE = 512
WK = CHUNK_COLS // WIDE
WCHUNKS = KT // WK
POOL_SHARE = 4
EARLY = 3
ADA_BLOCKS = 3 * D_MODEL // WIDE
ADA_INPUT = 2 * D_MODEL // WIDE
GROUPS = 4
GROUP = P // GROUPS
OUT_BLOCKS = D_MODEL // WIDE
OUT_CHUNKS = (OUT_BLOCKS + 1) * WCHUNKS
LEVELS = 7
PRODUCTS = LEVELS + 1
DK_SCALE = float(P) ** -0.5
EPS = 1e-6
GRID_W = 64
ROTARY = P // 4
ROPE_BASE = 10000.0

F32 = mybir.dt.float32
F32R = mybir.dt.float32r
I32 = mybir.dt.int32
ALU = mybir.AluOpType
ACT = mybir.ActivationFunctionType
AX_X = mybir.AxisListType.X

C_IDENT, C_POS = 0, P
NSTART = P + 4
C_ONES = NSTART
C_COS = C_ONES + P
C_SIN = C_COS + LAT
C_REL = C_SIN + LAT
REL = LAT + LAT - P
C_MASK = C_REL + REL
C_RESET = C_MASK + LEVELS * P
NCONST = C_RESET + T


def layer(nc, x_prompt, x_sample, s_ret_f, s_ret_b, s_hg_f, s_hg_b, c, c_ctx, norm_w, w_ada, b_ada,
          w_in, ret_decay, hg_lower, hg_norm_w, w_out, final_norm_w, consts,
          y_prompt, y_sample, n_ret_f, n_ret_b, n_hg_f, n_hg_b):
    ctx = ExitStack()
    with ctx:
        def sb(name, shape, dt=F32):
            return ctx.enter_context(nc.sbuf_tensor(name, shape, dt))

        class Signal:

            def __init__(self, name, each=1):
                self.sem, self.each = ctx.enter_context(nc.semaphore(name)), each

            def at(self, h, k=None):
                return self.each * h + (self.each if k is None else k)

        def due(signal, h, k=None):
            value = signal.at(h, k)
            return not isinstance(value, int) or value > 0

        con = sb("con", [P, NCONST])
        hT_hi = sb("hT_hi", [P, KT, T], F32R)
        hT_lo = sb("hT_lo", [P, KT, T], F32R)
        w_hi = sb("w_hi", [P, 2, CHUNK_COLS], F32R)
        w_lo = sb("w_lo", [P, 2, CHUNK_COLS], F32R)
        small = sb("small", [P, 448])
        AREA = 24320
        area = sb("area", [P, AREA])
        ps = ctx.enter_context(nc.psum_tensor("ps", [P, 8, 512], F32))

        mod_dram = nc.dram_tensor("mod_scratch", (GROUPS, 3 * D_MODEL), F32).ap()
        gate_dram = nc.dram_tensor("gate_scratch", (2, D_MODEL), F32).ap()
        o_dram = nc.dram_tensor("o_scratch", (2 * HEADS, P, T), F32).ap()

        ident = con[:, C_IDENT:C_IDENT + P]
        ones = con[:, C_ONES:C_ONES + P]
        cos, sin = con[:, C_COS:C_COS + LAT], con[:, C_SIN:C_SIN + LAT]
        rel = con[:, C_REL:C_REL + REL]
        reset = con[:, C_RESET:C_RESET + T]

        def mask(level):
            return con[:, C_MASK + (level - 1) * P:C_MASK + level * P].bitcast(I32)

        used = [0]

        def cols(n):
            used[0] += n
            assert used[0] <= AREA, used[0]
            return area[:, used[0] - n:used[0]]

        scols = [0]

        def sc(n):
            scols[0] += n
            assert scols[0] <= 448
            return small[:, scols[0] - n:scols[0]]

        raw = cols(3 * CHUNK_COLS).rearrange("p (s n) -> p s n", s=3)
        RET0 = used[0]
        rq, rk, rvT = cols(T), cols(T), cols(T)
        rtok = cols(T).rearrange("p (t d) -> p t d", d=P)
        rsg = cols(T)
        strip = cols(REL)
        sT = cols(4 * LAT + P)
        rsq, rr = sT[:, 0:T], sT[:, 2 * LAT:2 * LAT + T]
        rope_q, rope_k = sT[:, 2 * LAT:3 * LAT], sT[:, 3 * LAT:4 * LAT]
        RET1 = used[0]
        rqd = cols(2 * LAT).rearrange("p (s n) -> p s n", s=2)
        graw = area[:, used[0] - 2 * LAT:used[0] - 2 * LAT + T]
        kts = cols(2 * P).rearrange("p (s n) -> p s n", s=2)
        rS0 = cols(2 * P).rearrange("p (s n) -> p s n", s=2)
        rst = cols(2 * P).rearrange("p (s n) -> p s n", s=2)
        HG0 = used[0]
        hq = cols(T)
        F = cols(2 * T).rearrange("p (s n) -> p s n", s=2)
        K = cols(2 * T).rearrange("p (s n) -> p s n", s=2)
        B = cols(2 * T).rearrange("p (s n) -> p s n", s=2)
        KL = cols(2 * T).rearrange("p (s n) -> p s n", s=2)
        hsq, hr = KL[:, 0, :], KL[:, 1, :]
        kltok = cols(8 * P).rearrange("p (t d) -> p t d", d=P)
        XE = cols(4 * T).rearrange("p (b s n) -> p b s n", b=2, s=2)
        S = cols(8 * P).rearrange("p (s t d) -> p s t d", s=2, t=4)
        hst = cols(2 * P).rearrange("p (s n) -> p s n", s=2)
        htok = cols(T).rearrange("p (t d) -> p t d", d=P)
        hsT = cols(T)
        hsg = cols(T)
        hvT = cols(T)

        ada_raw = area[:, 0:WCHUNKS * CHUNK_COLS].rearrange("p (s n) -> p s n", s=WCHUNKS)
        X0 = WCHUNKS * CHUNK_COLS
        x_in = area[:, X0:X0 + TILES * D_MODEL].rearrange("p (t n) -> p t n", t=TILES)
        J0 = X0 + TILES * D_MODEL
        junk_in = area[:, J0:J0 + D_MODEL]
        mod_row = area[:, J0 + D_MODEL:J0 + D_MODEL + 2 * WIDE].rearrange("p (s n) -> p s n", s=2)
        C0 = J0 + D_MODEL + 2 * WIDE
        lb_in = area[0:4 * HEADS, C0:C0 + P]
        mod_cols = area[:, C0 + P:C0 + P + 3 * GROUPS * KT].rearrange("p (g s k) -> p g s k", g=GROUPS, s=3)
        bias_cols = area[:, C0 + 2 * P + P:C0 + 3 * P + 3 * KT].rearrange("p (s k) -> p s k", s=3)
        gate_cols = area[:, C0 + 4 * P:C0 + 4 * P + 2 * KT].rearrange("p (w k) -> p w k", w=2)
        assert P + 3 * GROUPS * KT <= 3 * P and C0 + 5 * P <= AREA
        cs = hT_hi[:, :, 0:P]
        STAGES = 9
        o_raw = area[:, RET0:RET0 + STAGES * T].rearrange("p (s n) -> p s n", s=STAGES)
        gates = area[:, RET0:RET0 + 2 * D_MODEL].rearrange("p (s n) -> p s n", s=2)
        fnw = area[:, RET0 + 2 * D_MODEL:RET0 + 3 * D_MODEL]
        assert RET0 + 3 * D_MODEL <= RET1 and RET0 + STAGES * T <= RET1
        x_res = area[:, HG0:HG0 + TILES * D_MODEL].rearrange("p (t n) -> p t n", t=TILES)
        junk_out = area[:, HG0 + TILES * D_MODEL:HG0 + TILES * D_MODEL + WIDE]
        assert HG0 + TILES * D_MODEL + WIDE <= used[0]
        gated = rqd

        c_raw = sc(2 * KT).rearrange("p (w k) -> p w k", w=2)
        c_sig = sc(2 * KT).rearrange("p (w k) -> p w k", w=2)
        nw = sc(KT)
        mods = sc(4 * KT).rearrange("p (w s k) -> p w s k", w=2, s=2)
        lgr = sc(2 * HEADS)
        lgu, lgt = sc(2 * HEADS), sc(2 * HEADS)
        lg, nlg = sc(2 * HEADS), sc(2 * HEADS)
        dbias = sc(2 * HEADS)
        kdec = sc(2 * HEADS)
        lbT = sc(4 * HEADS)
        lb, oml = sc(2 * HEADS), sc(2 * HEADS)
        lbm = sc(2 * HEADS)
        hnw = sc(1)
        ssq = sc(TILES)
        var, rstd, newt = sc(TILES), sc(TILES), sc(TILES)
        ssq4 = sc(TILES * OUT_BLOCKS).rearrange("p (t n) -> p t n", t=TILES)
        ssq_out, var_o, rstd_o, newt_o = sc(TILES), sc(TILES), sc(TILES), sc(TILES)
        dec = sc(2 * TILES).rearrange("p (s t) -> p s t", s=2)
        eps_col = sc(1)
        lgu2 = sc(2 * HEADS)

        c_in, small_in = Signal("c_in", 16), Signal("small_in", 16)
        con_start, x_landed = Signal("con_start", 16), [Signal(f"x_landed{t}", 16) for t in range(TILES)]
        c_steps, c_exp = Signal("c_steps"), Signal("c_exp")
        lg_steps, lg_act = Signal("lg_steps"), Signal("lg_act")
        lb_pe = Signal("lb_pe")
        cs_ready = Signal("cs_ready")
        x_sq = Signal("x_sq")
        rstd_act, rstd_steps = Signal("rstd_act"), Signal("rstd_steps")
        x_scaled = Signal("x_scaled")
        a_landed = [Signal(f"a_landed{j}", 16) for j in range(WCHUNKS)]
        a_hi, a_used = Signal("a_hi", KT), Signal("a_used", KT)
        a_lo, a_lo_pool = Signal("a_lo", KT - KT // POOL_SHARE), Signal("a_lo_pool", KT // POOL_SHARE)
        a_row, a_store = Signal("a_row"), [Signal(f"a_store{j}", 16) for j in range(2)]
        mods_in, mod_steps = Signal("mods_in", 16), Signal("mod_steps")
        gate_in, gate_steps, gate_stored = Signal("gate_in", 16), Signal("gate_steps"), Signal("gate_stored", 16)
        x_tr, x_evac = Signal("x_tr"), [Signal("x_evac_act"), Signal("x_evac_dve")]
        h_mod, h_hi, h_lo = Signal("h_mod"), Signal("h_hi"), Signal("h_lo")
        ctx_hi, ctx_lo = Signal("ctx_hi", 2), Signal("ctx_lo", 2)
        landed = [Signal(f"landed{j}", 16 * CHUNKS // 3) for j in range(3)]
        wt_hi, wt_lo, wt_used = Signal("wt_hi", CHUNKS), Signal("wt_lo", CHUNKS), Signal("wt_used", CHUNKS)
        r_q, r_k, r_v, r_eg = Signal("r_q"), Signal("r_k"), Signal("r_v"), Signal("r_eg")
        r_silu = Signal("r_silu", 4)
        strip_x, strip_e, strip_i = Signal("strip_x", 3), Signal("strip_e"), Signal("strip_i")
        r_dec, r_qdec = Signal("r_dec"), Signal("r_qdec")
        rope_cos, rope_sin, roped = Signal("rope_cos"), Signal("rope_sin"), Signal("roped")
        r_tok = Signal("r_tok", 2)
        r_sT = Signal("r_sT", 5)
        r_sq, r_state, r_rms, r_out = Signal("r_sq"), Signal("r_state"), Signal("r_rms", 2), Signal("r_out", 2)
        swapped, pe_rtok, pe_rs = Signal("swapped", 2 * P // ROTARY * 16), Signal("pe_rtok"), Signal("pe_rs", 5)
        pe_ro, pe_rss = Signal("pe_ro"), Signal("pe_rss")
        r_S0, r_stored, r_state_stored = Signal("r_S0", 32), Signal("r_stored", 16), Signal("r_state_stored", 32)
        h_q, h_ez, h_v = Signal("h_q"), Signal("h_ez", 2), Signal("h_v")
        h_graw, h_eg, h_silu = Signal("h_graw"), Signal("h_eg"), Signal("h_silu", 4)
        h_gate, h_log, h_scan = Signal("h_gate", 10), Signal("h_log", 2), Signal("h_scan", 2)
        h_klx, h_eb, h_ekl = Signal("h_klx"), Signal("h_eb"), Signal("h_ekl")
        h_dec, h_qr, h_kl = Signal("h_dec"), Signal("h_qr"), Signal("h_kl")
        h_tok, h_kltok, h_state = Signal("h_tok"), Signal("h_kltok"), Signal("h_state")
        h_S = Signal("h_S", 3)
        xq, xa, xe = Signal("xq", LEVELS), Signal("xa", LEVELS), Signal("xe", LEVELS)
        lq, la = Signal("lq", LEVELS), Signal("la", PRODUCTS)
        h_sT = Signal("h_sT", PRODUCTS)
        h_sq, h_rms, h_out = Signal("h_sq"), Signal("h_rms", 2), Signal("h_out", 2)
        pe_htok, pe_hkl, pe_hu, pe_level = Signal("pe_htok"), Signal("pe_hkl"), Signal("pe_hu"), Signal("pe_level", PRODUCTS)
        pe_ho, pe_hss = Signal("pe_ho"), Signal("pe_hss")
        h_S0, h_stored, h_state_stored = Signal("h_S0", 32), Signal("h_stored", 16), Signal("h_state_stored", 32)
        o_landed = [Signal(f"o_landed{j}", 16) for j in range(STAGES)]
        o_hi, o_lo = Signal("o_hi"), Signal("o_lo")
        d_landed = [Signal(f"d_landed{j}", 16) for j in range(2)]
        d_hi, d_lo, d_used = Signal("d_hi", WCHUNKS), Signal("d_lo", WCHUNKS), Signal("d_used", WCHUNKS)
        res_in = [Signal(f"res_in{nb}", 4 * 16) for nb in range(OUT_BLOCKS)]
        fnw_in, weighted = Signal("fnw_in", 16), Signal("weighted", (OUT_BLOCKS - 1) * TILES)
        d_gated, d_ev, d_sq = Signal("d_gated", TILES), Signal("d_ev", TILES), Signal("d_sq", TILES)
        d_tile = Signal("d_tile")
        fin_steps, fin_act = Signal("fin_steps", 6), Signal("fin_act", 2)
        y_left, y_right, y_stored = [Signal("y_left_dve"), Signal("y_left_act")], Signal("y_right"), Signal("y_stored", 16)
        con_in = Signal("con_in", 16)

        A, BB, C, DD = 4, 5, 6, 7

        w_ada_v = w_ada[0].rearrange("(p k) n -> p k n", k=KT)
        w_in_v = w_in[0].rearrange("(p k) n -> p k n", k=KT)
        w_out_v = w_out[0].rearrange("(k p) n -> p k n", p=P)

        def tile_cols(t):
            return slice(t * P, (t + 1) * P)

        def proj(i):
            return ps[:, 2 * (i % 2):2 * (i % 2) + 2, 0:HALF]

        def halves(ap):
            return ap.rearrange("p (s n) -> p s n", s=2)

        def tiles(ap):
            return ap.rearrange("p (t n) -> p t n", n=P)

        def blocks(ap, level):
            return ap.rearrange("p (b n) -> p b n", n=P >> level)

        def evac_order(nb):
            return [3, 4, 0, 1, 2] if nb == 1 else [0, 1, 2, 3, 4]

        def out_bank(nb, t):
            return ((0, 1, 2, 3, BB), (A, C, DD, 0, 1))[nb % 2][t]

        def ctx_scores(h, level):
            return ps[:, BB if h is not None or level == 0 else DD, 0:P]

        def ctx_sums(h):
            return ps[:, BB, 0:P] if h is not None else ps[:, DD, P:2 * P]

        def on_pool(k):
            return k % POOL_SHARE == POOL_SHARE - 1

        def lows(k):
            return k + 1 - (k + 1) // POOL_SHARE, (k + 1) // POOL_SHARE

        def split_at(n):
            return (n - 2,) if 2 <= n < 2 + WCHUNKS else ()

        def modulated_at(chunk):
            first, last = (2 * (chunk - 1)) // 3, (2 * chunk) // 3
            return range(max(first, 0), min(last, KT)) if chunk >= 2 else range(0)

        block = ctx.enter_context(nc.Block())

        @block.sync
        def _(sp):
            def load_ada(nb, j, gate):
                if gate:
                    by_dve, by_pool = lows(WK * j + WK - 1)
                    by_dve, by_pool = a_lo.at(nb - 1, by_dve), a_lo_pool.at(nb - 1, by_pool)
                    if not isinstance(nb, int):
                        by_dve, by_pool = sp.to_reg(by_dve), sp.to_reg(by_pool)
                    if on_pool(WK * j + WK - 1):
                        sp.wait_ge(a_lo_pool.sem, by_pool)
                    sp.wait_ge(a_lo.sem, by_dve)
                sp.dma_start(ada_raw[:, j, :].rearrange("p (k n) -> p k n", k=WK),
                             w_ada_v[:, j * WK:(j + 1) * WK, bass.ds(nb * WIDE, WIDE)]).then_inc(a_landed[j].sem, 16)

            def ada_block(nb, extra=None):
                for j in range(WCHUNKS):
                    load_ada(nb, j, not isinstance(nb, int) or nb > 0)
                    if extra is not None:
                        extra(nb * WCHUNKS + j)

            def start(chunk):
                if chunk == 0:
                    sp.dma_start(lgr, ret_decay.rearrange("l s h -> l (s h)").broadcast_to([P, 2 * HEADS])).then_inc(small_in.sem, 16)
                    sp.dma_start(lb_in, hg_lower.rearrange("s l (h d) -> (s l h) d", d=P)).then_inc(small_in.sem, 16)
                    sp.dma_start(nw, norm_w[0].rearrange("(p k) -> p k", k=KT)).then_inc(small_in.sem, 16)
                    sp.dma_start(hnw, hg_norm_w.rearrange("l p -> p l")).then_inc(small_in.sem, 16)
                    sp.dma_start(bias_cols, b_ada[0].rearrange("(s p k) -> p s k", s=3, k=KT)).then_inc(small_in.sem, 16)
                    sp.dma_start(con[:, 0:NSTART], consts[:, 0:NSTART]).then_inc(con_start.sem, 16)
                if chunk % 2 == 0 and chunk // 2 < TILES:
                    t = chunk // 2
                    src = x_prompt[0] if t == 0 else x_sample[0, (t - 1) * P:t * P, :]
                    sp.dma_start(x_in[:, t, :], src).then_inc(x_landed[t].sem, 16)

            sp.dma_start(c_raw[:, 0, :], c_ctx.rearrange("(p k) -> p k", k=KT)).then_inc(c_in.sem, 16)
            sp.dma_start(c_raw[:, 1, :], c[0].rearrange("(p k) -> p k", k=KT)).then_inc(c_in.sem, 16)
            for nb in range(4):
                ada_block(nb, start)
            with sp.Fori(4, ADA_BLOCKS) as nb:
                ada_block(nb)

            def load(h, n):
                if n < 3:
                    if isinstance(h, int) and h == 0:
                        sp.wait_ge(a_lo.sem, a_lo.at(ADA_BLOCKS - 1, lows(WK * n + WK - 1)[0]))
                        sp.wait_ge(a_lo_pool.sem, a_lo_pool.at(ADA_BLOCKS - 1, lows(WK * n + WK)[1]))
                    else:
                        if due(wt_lo, h - 1, CHUNKS + n - 2):
                            sp.wait_ge(wt_lo.sem, wt_lo.at(h - 1, CHUNKS + n - 2))
                else:
                    if due(wt_lo, h, n - 2):
                        sp.wait_ge(wt_lo.sem, wt_lo.at(h, n - 2))
                i, half = n // 2, n % 2
                sp.dma_start(raw[:, n % 3, :].rearrange("p (k n) -> p k n", k=KC),
                             w_in_v[:, half * KC:(half + 1) * KC, bass.ds(i * HEAD_COLS + h * P, P)]
                             ).then_inc(landed[n % 3].sem, 16)

            def store_states(h, new_f, new_b, buf, ready, stored):
                sp.wait_ge(ready.sem, ready.at(h))
                for s, new in enumerate((new_f, new_b)):
                    sp.dma_start(new[0, 0, bass.ds(h, 1)].rearrange("h d v -> (h d) v"), buf[:, s, :]).then_inc(stored.sem, 16)

            def items(n, h, prev):
                if n == 2 and prev is None:
                    sp.dma_start(con[:, NSTART:NCONST], consts[:, NSTART:NCONST]).then_inc(con_in.sem, 16)
                if n == 3 and prev is None:
                    for b in range(2):
                        sp.wait_ge(a_store[b].sem, a_store[b].at(ADA_BLOCKS // 2 - 1))
                    sp.dma_start(mod_cols[:, :, 2, :], mod_dram[:, 2 * D_MODEL:3 * D_MODEL].rearrange("g (p k) -> p g k", k=KT)
                                 ).then_inc(gate_in.sem, 16)
                if n == 10 and prev is None:
                    sp.wait_ge(gate_steps.sem, gate_steps.at(1))
                    sp.dma_start(gate_dram.rearrange("w (p k) -> p w k", k=KT), gate_cols).then_inc(gate_stored.sem, 16)
                if n == 4 and prev is not None:
                    store_states(prev, n_ret_f, n_ret_b, rst, r_state, r_state_stored)
                if n == 6 and prev is not None:
                    sp.wait_ge(r_out.sem, r_out.at(prev))
                    sp.dma_start(o_dram[bass.ds(prev, 1)].rearrange("h d t -> (h d) t"), rr).then_inc(r_stored.sem, 16)
                if n == 6 and h is not None:
                    if due(pe_ro, h - 1):
                        sp.wait_ge(pe_ro.sem, pe_ro.at(h - 1))
                    for s, old in enumerate((s_ret_f, s_ret_b)):
                        sp.dma_start(rS0[:, s, :], old[0, 0, bass.ds(h, 1)].rearrange("h d v -> (h d) v")).then_inc(r_S0.sem, 16)
                if n == 8 and prev is not None:
                    store_states(prev, n_hg_f, n_hg_b, hst, h_state, h_state_stored)
                if n == 9 and h is not None:
                    sp.wait_ge(r_k.sem, r_k.at(h))
                    if prev is not None:
                        sp.wait_ge(r_stored.sem, r_stored.at(prev))
                    for src, dst in ((rq, rope_q), (rk, rope_k)):
                        for p in range(0, P, ROTARY):
                            q = p ^ ROTARY
                            sp.dma_start(dst[p:p + ROTARY, :], src[q:q + ROTARY, P:T]).then_inc(swapped.sem, 16)
                if n == 17 and prev is not None:
                    sp.wait_ge(h_out.sem, h_out.at(prev))
                    sp.dma_start(o_dram[bass.ds(prev + HEADS, 1)].rearrange("h d t -> (h d) t"), hr).then_inc(h_stored.sem, 16)
                if n == 17 and h is not None:
                    if due(pe_ho, h - 1):
                        sp.wait_ge(pe_ho.sem, pe_ho.at(h - 1))
                    for s, old, at in ((0, s_hg_f, 0), (1, s_hg_b, 3)):
                        sp.dma_start(S[:, s, at, :], old[0, 0, bass.ds(h, 1)].rearrange("h d v -> (h d) v")).then_inc(h_S0.sem, 16)

            def head(h, prev):
                for n in range(CHUNKS):
                    load(h, n)
                    items(n, h, prev)

            head(0, None)
            head(1, 0)
            with sp.Fori(2, HEADS) as h:
                head(h, h - 1)
            last = HEADS - 1
            items(4, None, last)
            items(6, None, last)

            def load_o(kt):
                if kt >= STAGES:
                    if due(o_lo, kt - STAGES):
                        sp.wait_ge(o_lo.sem, o_lo.at(kt - STAGES))
                if kt < HEADS:
                    sp.wait_ge(r_stored.sem, r_stored.at(kt))
                else:
                    if due(h_stored, kt - HEADS):
                        sp.wait_ge(h_stored.sem, h_stored.at(kt - HEADS))
                sp.dma_start(o_raw[:, kt % STAGES, :], o_dram[kt]).then_inc(o_landed[kt % STAGES].sem, 16)

            def load_w_out(m):
                nb, j = min(m // WCHUNKS, OUT_BLOCKS - 1), m % WCHUNKS
                if m < 2:
                    sp.wait_ge(wt_lo.sem, wt_lo.at(last))
                else:
                    if due(d_lo, 0, m - 1):
                        sp.wait_ge(d_lo.sem, d_lo.at(0, m - 1))
                sp.dma_start(raw[:, m % 2, :].rearrange("p (k n) -> p k n", k=WK),
                             w_out_v[:, j * WK:(j + 1) * WK, nb * WIDE:(nb + 1) * WIDE]).then_inc(d_landed[m % 2].sem, 16)

            load_w_out(0)
            load_w_out(1)
            for kt in range(STAGES):
                if kt == 0:
                    sp.wait_ge(r_out.sem, r_out.at(last))
                if kt == STAGES - 1:
                    sp.wait_ge(r_stored.sem, r_stored.at(last))
                load_o(kt)
            load_w_out(2)
            items(8, None, last)
            for m in range(3, 3 + (2 * HEADS - 1 - STAGES) // 2):
                load_o(STAGES + 2 * (m - 3))
                load_o(STAGES + 2 * (m - 3) + 1)
                load_w_out(m)
            for m in range(m + 1, WCHUNKS + 2):
                load_w_out(m)
            sp.wait_ge(h_state_stored.sem, h_state_stored.at(last))

            def load_residual(nb):
                at = slice(nb * WIDE, (nb + 1) * WIDE)
                sp.dma_start(x_res[:, 0, at], x_prompt[0, :, at]).then_inc(res_in[nb].sem, 16)
                sp.dma_start(x_res[:, 1:TILES, at], x_sample[0, :, at].rearrange("(t p) n -> p t n", p=P)).then_inc(res_in[nb].sem, 16)
                for w in range(2):
                    sp.dma_start(gates[:, w, at], gate_dram[w:w + 1, at].broadcast_to([P, WIDE])).then_inc(res_in[nb].sem, 16)

            sp.wait_ge(gate_stored.sem, gate_stored.at(0))
            sp.wait_ge(o_lo.sem, o_lo.at(2 * HEADS - 1))
            for m in range(WCHUNKS + 2, OUT_CHUNKS):
                i = m - WCHUNKS - 2
                if i % 2 == 0 and i // 2 < OUT_BLOCKS:
                    load_residual(i // 2)
                if i == 2 * OUT_BLOCKS:
                    sp.dma_start(fnw, final_norm_w.rearrange("(l n) -> l n", l=1).broadcast_to([P, D_MODEL])).then_inc(fnw_in.sem, 16)
                load_w_out(m)
            for t in range(TILES):
                sp.wait_ge(y_right.sem, y_right.at(t))
                sp.wait_ge(y_left[t % 2].sem, y_left[t % 2].at(t // 2))
                out = y_prompt[0] if t == 0 else y_sample[0, (t - 1) * P:t * P, :]
                sp.dma_start(out, x_res[:, t, :]).then_inc(y_stored.sem, 16)
            sp.wait_ge(y_stored.sem, y_stored.at(TILES - 1))
            sp.wait_ge(r_state_stored.sem, r_state_stored.at(last))
            sp.wait_ge(h_state_stored.sem, h_state_stored.at(last))

        @block.scalar
        def _(act):
            act.preload_act_table_set("natural_log_exp_and_others")
            act.wait_ge(c_in.sem, c_in.at(1))
            act.activation(c_sig, c_raw, ACT.Exp, scale=-1.0).then_inc(c_exp.sem, 1)

            def ada_block(nb, extra=None):
                for j in range(WCHUNKS):
                    act.wait_ge(a_landed[j].sem, a_landed[j].at(nb))
                    for kk in range(WK):
                        if not (isinstance(nb, int) and nb == 0 and j < 2):
                            if due(a_used, nb, WK * (j - 2) + kk + 1):
                                act.wait_ge(a_used.sem, a_used.at(nb, WK * (j - 2) + kk + 1))
                        w = slice(kk * WIDE, (kk + 1) * WIDE)
                        act.activation(w_hi[:, j % 2, w], ada_raw[:, j, w], ACT.Copy).then_inc(a_hi.sem, 1)
                    if extra is not None:
                        extra(j)

            def store_row(nb, b):
                act.wait_ge(a_row.sem, a_row.at(nb))
                act.dma_start(mod_dram[:, bass.ds(nb * WIDE, WIDE)], mod_row[0:P:GROUP, b, :]).then_inc(a_store[b].sem, 16)

            def stores(nb):
                def extra(j):
                    if j == 4:
                        store_row(nb - 1, (nb - 1) % 2)
                return extra

            def square_in(t):
                act.wait_ge(x_landed[t].sem, x_landed[t].at(0))
                if t:
                    if due(x_sq, t - 1):
                        act.wait_ge(x_sq.sem, x_sq.at(t - 1))
                act.activation(junk_in, x_in[:, t, :], ACT.Square, accum_out=ssq[:, t:t + 1]).then_inc(x_sq.sem, 1)

            def block_0(j):
                if j % 2:
                    square_in(j // 2)

            def block_1(j):
                stores(1)(j)
                if j == 0:
                    act.wait_ge(small_in.sem, small_in.at(4))
                    act.activation(lgt, lgr, ACT.Exp).then_inc(lg_act.sem, 1)
                if j == 1:
                    square_in(TILES - 1)
                if j == 2:
                    act.wait_ge(lg_steps.sem, lg_steps.at(0, 1))
                    act.activation(lg, lgu, ACT.Ln).then_inc(lg_act.sem, 1)
                if j == 3:
                    act.wait_ge(rstd_steps.sem, rstd_steps.at(0, 1))
                    act.activation(rstd, var, ACT.Ln).then_inc(rstd_act.sem, 1)
                    act.wait_ge(rstd_act.sem, rstd_act.at(0))
                    act.activation(rstd, rstd, ACT.Exp, scale=-0.5).then_inc(rstd_act.sem, 1)
                if j == 4:
                    act.wait_ge(lg_steps.sem, lg_steps.at(0, 10))
                    act.activation(lbT, lbT, ACT.Exp).then_inc(lg_act.sem, 1)
                if j == 7:
                    act.wait_ge(lg_steps.sem, lg_steps.at(0, 15))
                    act.activation(kdec, kdec, ACT.Exp).then_inc(lg_act.sem, 1)

            def high_input(k):
                act.wait_ge(h_mod.sem, h_mod.at(k))
                act.activation(tiles(hT_hi[:, k, P:T]), x_in[:, 1:TILES, k::KT], ACT.Copy).then_inc(h_hi.sem, 1)

            def with_modulation(nb):
                def extra(j):
                    stores(nb)(j)
                    if nb == ADA_INPUT and j == 7:
                        for b in range(2):
                            if due(a_store[b], ADA_INPUT // 2 - 1):
                                act.wait_ge(a_store[b].sem, a_store[b].at(ADA_INPUT // 2 - 1))
                        for s in range(2):
                            act.dma_start(mod_cols[:, :, s, :], mod_dram[:, s * D_MODEL:(s + 1) * D_MODEL].rearrange(
                                "g (p k) -> p g k", k=KT)).then_inc(mods_in.sem, 16)
                    for k in modulated_at((nb - ADA_INPUT - 1) * WCHUNKS + j - 1):
                        high_input(k)
                return extra

            def with_transposes(nb):
                def extra(j):
                    stores(nb)(j)
                    k = (nb - 2) * WCHUNKS + j - 2
                    if k >= 0 and k % 2 == 0:
                        even_input(k)
                return extra

            def even_input(k):
                bank = 2 + 2 * (k % 3)
                act.wait_ge(x_tr.sem, x_tr.at(k))
                act.activation(x_in[:, 1:TILES, k::KT], tiles(ps[:, bank, :]), ACT.Copy)
                act.activation(x_in[:, 0, k::KT], ps[:, bank + 1, 0:P], ACT.Copy).then_inc(x_evac[0].sem, 1)

            ada_block(0, block_0)
            ada_block(1, block_1)
            for nb in range(2, 4):
                ada_block(nb, with_transposes(nb))
            even_input(KT - 2)
            with act.Fori(2, ADA_INPUT // 2) as pair:
                for b in range(2):
                    nb = 2 * pair + b
                    def extra(j):
                        if j == 4:
                            store_row(nb - 1, 1 - b)
                    ada_block(nb, extra)
            for nb in range(ADA_INPUT, ADA_BLOCKS):
                ada_block(nb, with_modulation(nb))
            def high_context(half):
                ks = slice(half * KC, (half + 1) * KC)
                if half == 1:
                    for chunk in (3 * WCHUNKS - 1, 3 * WCHUNKS):
                        for k in modulated_at(chunk):
                            high_input(k)
                act.wait_ge(a_used.sem, a_used.at(ADA_BLOCKS - 1))
                act.activation(hT_hi[:, ks, 0:P], x_in[:, 0, :].rearrange("p (n k) -> p k n", k=KT)[:, ks, :],
                               ACT.Copy).then_inc(ctx_hi.sem, 1)
                if half == 0:
                    store_row(ADA_BLOCKS - 1, 1)

            def split(h, n):
                act.wait_ge(landed[n % 3].sem, landed[n % 3].at(h, 16 * (n // 3 + 1)))
                if n >= 2:
                    if due(wt_used, h, n - 1):
                        act.wait_ge(wt_used.sem, wt_used.at(h, n - 1))
                elif isinstance(h, int) and h == 0:
                    act.wait_ge(a_used.sem, a_used.at(ADA_BLOCKS - 1, KT - WK * (1 - n)))
                else:
                    if due(wt_used, h - 1, CHUNKS + n - 1):
                        act.wait_ge(wt_used.sem, wt_used.at(h - 1, CHUNKS + n - 1))
                act.activation(w_hi[:, n % 2, :], raw[:, n % 3, :], ACT.Copy).then_inc(wt_hi.sem, 1)

            def projected(h, i):
                act.wait_ge(wt_used.sem, wt_used.at(h, 2 * i + 2))

            def gate_columns(prev):
                projected(prev, 8)
                act.wait_ge(pe_ro.sem, pe_ro.at(prev))
                act.activation(halves(graw), proj(8), ACT.Copy).then_inc(h_graw.sem, 1)

            def items(n, h, prev):
                if prev is not None:
                    if n == 0:
                        act.wait_ge(pe_rss.sem, pe_rss.at(prev))
                        act.activation(rr[:, P:T], ps[:, C, :], ACT.Ln, scale=1.0 / P, bias=eps_col)
                        act.activation(rr[:, 0:P], ps[:, DD, 0:P], ACT.Ln, scale=1.0 / P, bias=eps_col).then_inc(r_rms.sem, 1)
                        act.wait_ge(r_rms.sem, r_rms.at(prev, 1))
                        act.activation(rr, rr, ACT.Exp, scale=-0.5).then_inc(r_rms.sem, 1)
                        act.wait_ge(h_graw.sem, h_graw.at(prev))
                        if due(h_out, prev - 1):
                            act.wait_ge(h_out.sem, h_out.at(prev - 1))
                        act.activation(hsg, graw, ACT.Exp, scale=-1.0).then_inc(h_eg.sem, 1)
                    if n == 1:
                        act.wait_ge(pe_htok.sem, pe_htok.at(prev))
                        if due(pe_ho, prev - 1):
                            act.wait_ge(pe_ho.sem, pe_ho.at(prev - 1))
                        act.activation(htok[:, 1:TILES, :], tiles(ps[:, A, :]), ACT.Copy)
                        act.activation(htok[:, 0, :], ps[:, BB, 0:P], ACT.Copy).then_inc(h_tok.sem, 1)
                    if n == 2:
                        act.wait_ge(pe_hkl.sem, pe_hkl.at(prev))
                        act.activation(kltok[:, 0:4, :], tiles(ps[:, C, :]), ACT.Copy)
                        act.activation(kltok[:, 4:8, :], tiles(ps[:, DD, :]), ACT.Copy).then_inc(h_kltok.sem, 1)
                    if n == 3:
                        act.wait_ge(pe_hu.sem, pe_hu.at(prev))
                        if due(h_state_stored, prev - 1):
                            act.wait_ge(h_state_stored.sem, h_state_stored.at(prev - 1))
                        act.activation(hst[:, 0, :], ps[:, C, 0:P], ACT.Copy)
                        act.activation(hst[:, 1, :], ps[:, DD, 0:P], ACT.Copy).then_inc(h_state.sem, 1)
                    if 1 <= n <= LEVELS:
                        level = n - 1
                        act.wait_ge(xq.sem, xq.at(prev, level + 1))
                        act.wait_ge(xa.sem, xa.at(prev, level + 1))
                        x = XE[:, level % 2]
                        act.activation(x, x, ACT.Exp).then_inc(xe.sem, 1)
                    if n == 11:
                        act.wait_ge(pe_ho.sem, pe_ho.at(prev))
                        act.activation(hsq[:, P:T], ps[:, C, :], ACT.Square)
                        act.activation(hsq[:, 0:P], ps[:, DD, 0:P], ACT.Square).then_inc(h_sq.sem, 1)
                    if n == 12:
                        act.wait_ge(pe_hss.sem, pe_hss.at(prev))
                        act.activation(hr[:, P:T], ps[:, A, :], ACT.Ln, scale=1.0 / P, bias=eps_col)
                        act.activation(hr[:, 0:P], ctx_sums(h), ACT.Ln, scale=1.0 / P, bias=eps_col).then_inc(h_rms.sem, 1)
                        act.wait_ge(h_rms.sem, h_rms.at(prev, 1))
                        act.activation(hr, hr, ACT.Exp, scale=-0.5).then_inc(h_rms.sem, 1)
                if h is None:
                    return
                if n == 2:
                    projected(h, 0)
                    if due(pe_ro, h - 1):
                        act.wait_ge(pe_ro.sem, pe_ro.at(h - 1))
                    act.activation(halves(rq), proj(0), ACT.Copy).then_inc(r_q.sem, 1)
                if n == 4:
                    projected(h, 1)
                    act.activation(halves(rk), proj(1), ACT.Copy, scale=DK_SCALE).then_inc(r_k.sem, 1)
                if n == 6:
                    projected(h, 2)
                    act.activation(halves(rvT), proj(2), ACT.Copy).then_inc(r_v.sem, 1)
                if n == 8:
                    projected(h, 3)
                    if due(r_out, h - 1):
                        act.wait_ge(r_out.sem, r_out.at(h - 1))
                    act.activation(halves(rsg), proj(3), ACT.Exp, scale=-1.0).then_inc(r_eg.sem, 1)
                if n == 10:
                    projected(h, 4)
                    if due(pe_level, h - 1):
                        act.wait_ge(pe_level.sem, pe_level.at(h - 1))
                    act.activation(halves(hq), proj(4), ACT.Copy).then_inc(h_q.sem, 1)
                if n == 12 or n == 14:
                    s = (n - 12) // 2
                    projected(h, 5 + s)
                    if due(pe_ho, h - 1):
                        act.wait_ge(pe_ho.sem, pe_ho.at(h - 1))
                    act.activation(halves(F[:, s, :]), proj(5 + s), ACT.Exp, scale=-1.0).then_inc(h_ez.sem, 1)
                if n == 16:
                    projected(h, 7)
                    if due(pe_htok, h - 1):
                        act.wait_ge(pe_htok.sem, pe_htok.at(h - 1))
                    act.activation(halves(hvT), proj(7), ACT.Copy).then_inc(h_v.sem, 1)
                if n == 13:
                    if prev is None:
                        act.wait_ge(con_in.sem, con_in.at(0))
                    act.wait_ge(strip_x.sem, strip_x.at(h, 3))
                    act.activation(strip, strip, ACT.Exp).then_inc(strip_e.sem, 1)
                    if due(h_silu, h - 1):
                        act.wait_ge(h_silu.sem, h_silu.at(h - 1))
                    for s in range(2):
                        col = bass.ds(s * HEADS + h, 1)
                        i = act.activation(rqd[:, s, :], rel[:, REL - LAT:REL], ACT.Exp, bias=dbias[:, col],
                                           scale=(lg if s == 0 else nlg)[:, col])
                    i.then_inc(r_dec.sem, 1)
                if n == 14:
                    act.wait_ge(pe_rtok.sem, pe_rtok.at(h))
                    act.activation(rtok[:, 1:TILES, :], tiles(ps[:, C, :]), ACT.Copy)
                    act.activation(rtok[:, 0, :], ps[:, DD, 0:P], ACT.Copy).then_inc(r_tok.sem, 1)
                    for s in range(2):
                        i = act.activation(kts[:, s, :], ps[:, DD, P:2 * P], ACT.Copy, scale=kdec[:, bass.ds(s * HEADS + h, 1)])
                    i.then_inc(r_tok.sem, 1)
                if n == 14 or n == 16:
                    s = (n - 14) // 2
                    act.wait_ge(h_gate.sem, h_gate.at(h, 5 * s + 5))
                    act.activation(F[:, s, :], F[:, s, :], ACT.Ln).then_inc(h_log.sem, 1)
                if n == 17:
                    act.wait_ge(pe_ro.sem, pe_ro.at(h))
                    act.activation(rsq[:, P:T], ps[:, A, :], ACT.Square)
                    act.activation(rsq[:, 0:P], ps[:, BB, 0:P], ACT.Square).then_inc(r_sq.sem, 1)
                    if due(r_state_stored, h - 1):
                        act.wait_ge(r_state_stored.sem, r_state_stored.at(h - 1))
                    act.activation(rst, ps[:, DD, 0:2 * P].rearrange("p (s n) -> p s n", s=2), ACT.Copy).then_inc(r_state.sem, 1)
                    act.wait_ge(h_scan.sem, h_scan.at(h))
                    act.activation(F, B, ACT.Exp).then_inc(h_eb.sem, 1)
                    act.wait_ge(h_klx.sem, h_klx.at(h))
                    act.activation(KL, KL, ACT.Exp).then_inc(h_ekl.sem, 1)

            def head(h, prev):
                for n in range(CHUNKS):
                    if prev is not None and n == 1:
                        gate_columns(prev)
                    split(h, n)
                    if prev is None and n < 2:
                        high_context(n)
                    if n == 0:
                        if prev is not None:
                            items(CHUNKS - 1, prev, None)
                    else:
                        items(n - 1, h, prev)

            head(0, None)
            head(1, 0)
            with act.Fori(2, HEADS) as h:
                head(h, h - 1)
            last = HEADS - 1
            items(CHUNKS - 1, last, None)

            def split_o(kt):
                if kt == 2 * HEADS - 1:
                    act.wait_ge(h_out.sem, h_out.at(last))
                    src = hr
                else:
                    act.wait_ge(o_landed[kt % STAGES].sem, o_landed[kt % STAGES].at(kt // STAGES))
                    src = o_raw[:, kt % STAGES, :]
                if kt == 0:
                    act.wait_ge(wt_used.sem, wt_used.at(last))
                act.activation(hT_hi[:, kt, :], src, ACT.Copy).then_inc(o_hi.sem, 1)

            def split_w(m):
                act.wait_ge(d_landed[m % 2].sem, d_landed[m % 2].at(m // 2))
                if m >= 2:
                    if due(d_used, 0, m - 1):
                        act.wait_ge(d_used.sem, d_used.at(0, m - 1))
                act.activation(w_hi[:, m % 2, :], raw[:, m % 2, :], ACT.Copy).then_inc(d_hi.sem, 1)

            gate_columns(last)
            for n in range(13):
                items(n, None, last)
                for j in split_at(n):
                    for kt in range(WK * j, min(WK * j + WK, 2 * HEADS - 1)):
                        split_o(kt)
                    split_w(j)
            split_o(2 * HEADS - 1)

            def square(m):
                nb, t = m // TILES, evac_order(m // TILES)[m % TILES]
                act.wait_ge(d_ev.sem, d_ev.at(0, m + 1))
                if m:
                    act.wait_ge(d_sq.sem, d_sq.at(0, m))
                act.activation(junk_out, x_res[:, t, nb * WIDE:(nb + 1) * WIDE], ACT.Square,
                               accum_out=ssq4[:, t, nb:nb + 1]).then_inc(d_sq.sem, 1)

            def last_norm(group, tokens):
                act.wait_ge(fin_steps.sem, fin_steps.at(group, 2))
                act.activation(rstd_o[:, tokens], var_o[:, tokens], ACT.Ln).then_inc(fin_act.sem, 1)
                act.wait_ge(fin_act.sem, fin_act.at(group, 1))
                act.activation(rstd_o[:, tokens], rstd_o[:, tokens], ACT.Exp, scale=-0.5).then_inc(fin_act.sem, 1)

            def finish_left(t):
                act.wait_ge(fin_steps.sem, fin_steps.at(0 if t < EARLY else 1))
                act.wait_ge(weighted.sem, weighted.at(0))
                x = x_res[:, t, 0:D_MODEL - WIDE]
                act.activation(x, x, ACT.Copy, scale=rstd_o[:, t:t + 1]).then_inc(y_left[1].sem, 1)

            for m in range(WCHUNKS, OUT_CHUNKS):
                nb, j = m // WCHUNKS, m % WCHUNKS
                split_w(m)
                if nb < OUT_BLOCKS and 3 <= j < 3 + TILES:
                    square((nb - 1) * TILES + j - 3)
                if nb == OUT_BLOCKS and 2 <= j < 2 + EARLY:
                    square((OUT_BLOCKS - 1) * TILES + j - 2)
                if nb == OUT_BLOCKS and j == 5:
                    last_norm(0, slice(0, EARLY))
                if nb == OUT_BLOCKS and j == 7:
                    finish_left(1)
            for t in range(EARLY, TILES):
                square((OUT_BLOCKS - 1) * TILES + t)
            last_norm(1, slice(EARLY, TILES))
            finish_left(3)

        @block.vector
        def _(dve):
            v = nc.vector
            v.memset(eps_col, EPS)

            def newton(out, x, tmp, step):
                step(v.tensor_tensor(tmp, out, out, ALU.mult))
                step(v.tensor_tensor(tmp, tmp, x, ALU.mult))
                step(v.tensor_scalar(tmp, tmp, -0.5, 1.5, ALU.mult, ALU.add))
                step(v.tensor_tensor(out, out, tmp, ALU.mult))

            def c_step(i, count=[0]):
                count[0] += 1
                i.then_inc(c_steps.sem, 1)
                dve.wait_ge(c_steps.sem, c_steps.at(0, count[0]))

            dve.wait_ge(c_exp.sem, c_exp.at(0))
            c_step(v.tensor_scalar(c_sig, c_sig, 1.0, None, ALU.add))
            c_step(v.reciprocal(c_sig, c_sig))
            c_step(v.tensor_tensor(c_sig, c_sig, c_raw, ALU.mult))
            for w in range(2):
                i = v.tensor_copy(cs[:, :, w * GROUP:(w + 1) * GROUP], c_sig[:, w, :].unsqueeze(2).broadcast_to([P, KT, GROUP]))
            c_step(i)
            for w in range(2):
                i = v.tensor_tensor(cs[:, :, (2 + w) * GROUP:(3 + w) * GROUP], c_sig[:, w, :].unsqueeze(2).broadcast_to([P, KT, GROUP]),
                                    cs[:, :, w * GROUP:(w + 1) * GROUP].bitcast(F32), ALU.subtract)
            i.then_inc(cs_ready.sem, 1)

            def ada_block(nb, extra=None):
                for j in range(WCHUNKS):
                    for kk in range(WK):
                        if on_pool(WK * j + kk):
                            continue
                        dve.wait_ge(a_hi.sem, a_hi.at(nb, WK * j + kk + 1))
                        w = slice(kk * WIDE, (kk + 1) * WIDE)
                        v.tensor_tensor(w_lo[:, j % 2, w], ada_raw[:, j, w], w_hi[:, j % 2, w].bitcast(F32),
                                        ALU.subtract).then_inc(a_lo.sem, 1)
                    if extra is not None:
                        extra(j)

            def mod_block(pair, b):
                dve.wait_ge(a_used.sem, a_used.at(2 * pair + b))
                if due(a_store[b], pair - 1):
                    dve.wait_ge(a_store[b].sem, a_store[b].at(pair - 1))
                v.tensor_copy(mod_row[:, b, :], ps[:, b, :]).then_inc(a_row.sem, 1)

            ada_block(0)

            def lg_step(i, count=[0]):
                count[0] += 1
                i.then_inc(lg_steps.sem, 1)
                dve.wait_ge(lg_steps.sem, lg_steps.at(0, count[0]))

            lbp = ps[:, A, 0:4 * HEADS].rearrange("p (s l h) -> p s l h", s=2, l=2)
            lbv = lbT.rearrange("p (s l h) -> p s l h", s=2, l=2)
            lbm3 = lbm.rearrange("p (s h) -> p s h", s=2)

            def lg_part_0():
                dve.wait_ge(lg_act.sem, lg_act.at(0))
                lg_step(v.tensor_scalar(lgu, lgt, -1.0, 1.0, ALU.mult, ALU.add))
                lg_step(v.tensor_scalar(nlg, lgu, -1.0, 1.0, ALU.mult, ALU.add))
                lg_step(v.tensor_tensor(nlg, nlg, lgt, ALU.subtract))
                lg_step(v.reciprocal(lgu2, lgu))
                lg_step(v.tensor_tensor(nlg, nlg, lgu2, ALU.mult))

            def lg_part_1():
                dve.wait_ge(lg_act.sem, lg_act.at(1))
                lg_step(v.tensor_tensor(lg, lg, nlg, ALU.add))
                lg_step(v.tensor_scalar(nlg, lg, -1.0, None, ALU.mult))
                dve.wait_ge(lb_pe.sem, lb_pe.at(0))
                lg_step(v.tensor_copy(lbT, ps[:, A, 0:4 * HEADS]))
                lg_step(v.tensor_tensor(lbm3, lbv[:, :, 0, :], lbv[:, :, 1, :], ALU.max))
                for l in range(2):
                    i = v.tensor_tensor(lbv[:, :, l, :], lbv[:, :, l, :], lbm3, ALU.subtract)
                lg_step(i)

            def lg_part_2():
                dve.wait_ge(lg_act.sem, lg_act.at(2))
                lg_step(v.tensor_tensor(lbm3, lbv[:, :, 0, :], lbv[:, :, 1, :], ALU.add))
                lg_step(v.reciprocal(lbm, lbm))
                lg_step(v.tensor_tensor(lb.rearrange("p (s h) -> p s h", s=2), lbv[:, :, 0, :], lbm3, ALU.mult))
                lg_step(v.tensor_scalar(oml, lb, -1.0, 1.0, ALU.mult, ALU.add))
                for s in range(2):
                    g = slice(s * HEADS, (s + 1) * HEADS)
                    v.tensor_scalar(dbias[:, g], lg[:, g], con[:, C_POS + s:C_POS + s + 1], None, ALU.mult)
                    i = v.tensor_scalar(kdec[:, g], lg[:, g], con[:, C_POS + 2 + s:C_POS + 3 + s], None, ALU.mult)
                lg_step(i)

            def rstd_step(i, count=[0]):
                count[0] += 1
                i.then_inc(rstd_steps.sem, 1)
                dve.wait_ge(rstd_steps.sem, rstd_steps.at(0, count[0]))

            def block_1(j):
                if j == 0:
                    lg_part_0()
                if j == 1:
                    mod_block(0, 0)
                if j == 2:
                    dve.wait_ge(x_sq.sem, x_sq.at(TILES - 1))
                    rstd_step(v.tensor_scalar(var, ssq, 1.0 / D_MODEL, EPS, ALU.mult, ALU.add))
                if j == 3:
                    lg_part_1()
                if j == 4:
                    dve.wait_ge(rstd_act.sem, rstd_act.at(1))
                    newton(rstd, var, newt, rstd_step)
                if j == 5:
                    lg_part_2()
                for t in {4: (0,), 5: (1,), 6: (2, 3), 7: (4,)}.get(j, ()):
                    v.tensor_scalar(x_in[:, t, :], x_in[:, t, :], rstd[:, t:t + 1], None, ALU.mult).then_inc(x_scaled.sem, 1)

            def rows(nb):
                def extra(j):
                    if j == 1:
                        mod_block((nb - 1) // 2, (nb - 1) % 2)
                return extra

            def mod_step(i, count=[0]):
                count[0] += 1
                i.then_inc(mod_steps.sem, 1)
                dve.wait_ge(mod_steps.sem, mod_steps.at(0, count[0]))

            def modulate(k):
                dve.wait_ge(x_evac[k % 2].sem, x_evac[k % 2].at(k // 2))
                for w, x in ((0, x_in[:, 0, k::KT]), (1, x_in[:, 1:TILES, k::KT])):
                    i = v.tensor_scalar(x, x, mods[:, w, 1, k:k + 1], mods[:, w, 0, k:k + 1], ALU.mult, ALU.add)
                i.then_inc(h_mod.sem, 1)

            def low_context(half):
                ks = slice(half * KC, (half + 1) * KC)
                if half == 1:
                    for k in modulated_at(3 * WCHUNKS):
                        modulate(k)
                else:
                    mod_block(ADA_BLOCKS // 2 - 1, 1)
                dve.wait_ge(ctx_hi.sem, ctx_hi.at(0, half + 1))
                v.tensor_tensor(hT_lo[:, ks, 0:P], x_in[:, 0, :].rearrange("p (n k) -> p k n", k=KT)[:, ks, :],
                                hT_hi[:, ks, 0:P].bitcast(F32), ALU.subtract).then_inc(ctx_lo.sem, 1)

            def with_modulation(nb):
                def extra(j):
                    rows(nb)(j)
                    if nb == ADA_INPUT + 1 and j == 1:
                        dve.wait_ge(mods_in.sem, mods_in.at(1))
                        mod_step(v.tensor_tensor(mods, mod_cols[:, 0:2, 0:2, :], mod_cols[:, 2:4, 0:2, :], ALU.add))
                        mod_step(v.tensor_tensor(mods, mods, bias_cols[:, 0:2, :].unsqueeze(1).broadcast_to([P, 2, 2, KT]), ALU.add))
                        for w in range(2):
                            i = v.scalar_tensor_tensor(out=mods[:, w, 1, :], in0=mods[:, w, 1, :], scalar=1.0, in1=nw,
                                                       op0=ALU.add, op1=ALU.mult)
                        mod_step(i)
                    for k in modulated_at((nb - ADA_INPUT - 1) * WCHUNKS + j):
                        modulate(k)
                return extra

            def odd_input(k):
                bank = 2 + 2 * (k % 3)
                dve.wait_ge(x_tr.sem, x_tr.at(k))
                v.tensor_copy(x_in[:, 1:TILES, k::KT], tiles(ps[:, bank, :]))
                v.tensor_copy(x_in[:, 0, k::KT], ps[:, bank + 1, 0:P]).then_inc(x_evac[1].sem, 1)

            def with_transposes(nb):
                def extra(j):
                    rows(nb)(j)
                    k = (nb - 2) * WCHUNKS + j - 2
                    if k % 2 == 1 and k > 0:
                        odd_input(k)
                return extra

            ada_block(1, block_1)
            for nb in range(2, 4):
                ada_block(nb, with_transposes(nb))
            odd_input(KT - 1)
            with dve.Fori(2, ADA_INPUT // 2) as pair:
                for b in range(2):
                    nb = 2 * pair + b
                    def extra(j):
                        if j == 1:
                            mod_block(pair - 1 + b, 1 - b)
                    ada_block(nb, extra)
            for nb in range(ADA_INPUT, ADA_BLOCKS):
                ada_block(nb, with_modulation(nb))
            def split(h, n):
                dve.wait_ge(wt_hi.sem, wt_hi.at(h, n + 1))
                v.tensor_tensor(w_lo[:, n % 2, :], raw[:, n % 3, :], w_hi[:, n % 2, :].bitcast(F32),
                                ALU.subtract).then_inc(wt_lo.sem, 1)

            def reciprocal_half(buf, half, signal):
                part = buf[:, half * HALF:(half + 1) * HALF]
                v.reciprocal(part, part).then_inc(signal.sem, 1)

            def items(n, h, prev):
                if prev is not None:
                    if n == 0:
                        dve.wait_ge(r_rms.sem, r_rms.at(prev, 2))
                        v.tensor_tensor(rr[:, P:T], ps[:, A, :], rr[:, P:T], ALU.mult)
                        v.tensor_tensor(rr[:, 0:P], ps[:, BB, 0:P], rr[:, 0:P], ALU.mult).then_inc(r_out.sem, 1)
                        dve.wait_ge(r_out.sem, r_out.at(prev, 1))
                        dve.wait_ge(r_silu.sem, r_silu.at(prev))
                        v.tensor_tensor(rr, rr, rsg, ALU.mult).then_inc(r_out.sem, 1)
                        dve.wait_ge(h_eb.sem, h_eb.at(prev))
                        v.tensor_copy(dec[:, 0, :], tiles(F[:, 0, :])[:, :, P - 1])
                        v.tensor_copy(dec[:, 1, :], tiles(F[:, 1, :])[:, :, 0]).then_inc(h_dec.sem, 1)
                        dve.wait_ge(h_dec.sem, h_dec.at(prev))
                        for s in range(2):
                            i = v.tensor_tensor(F[:, s, :], F[:, s, :], hq, ALU.mult)
                        i.then_inc(h_qr.sem, 1)
                    if n == 10:
                        dve.wait_ge(h_eg.sem, h_eg.at(prev))
                        v.tensor_scalar(hsg, hsg, 1.0, None, ALU.add).then_inc(h_silu.sem, 1)
                        dve.wait_ge(h_silu.sem, h_silu.at(prev, 1))
                        reciprocal_half(hsg, 0, h_silu)
                    if n == 11:
                        reciprocal_half(hsg, 1, h_silu)
                        dve.wait_ge(h_silu.sem, h_silu.at(prev, 3))
                        v.tensor_tensor(hsg, hsg, graw, ALU.mult).then_inc(h_silu.sem, 1)
                    if 1 <= n <= LEVELS:
                        level = n - 1
                        half = P >> (level + 1)
                        buf = XE[:, level % 2, 0, :]
                        bf, bb, x = blocks(B[:, 0, :], level), blocks(B[:, 1, :], level), blocks(buf, level)
                        nblk = T // (2 * half)
                        if due(pe_level, prev, level - 1):
                            dve.wait_ge(pe_level.sem, pe_level.at(prev, level - 1))
                        v.tensor_tensor(x[:, :, half:2 * half], bf[:, :, half:2 * half],
                                        bf[:, :, half - 1:half].broadcast_to([P, nblk, half]), ALU.subtract)
                        v.tensor_tensor(x[:, :, 0:half], bb[:, :, 0:half],
                                        bb[:, :, half:half + 1].broadcast_to([P, nblk, half]), ALU.subtract).then_inc(xq.sem, 1)
                        dve.wait_ge(xe.sem, xe.at(prev, level + 1))
                        v.tensor_tensor(buf, buf, hq, ALU.mult).then_inc(lq.sem, 1)
                    if n == 3:
                        dve.wait_ge(pe_hu.sem, pe_hu.at(prev))
                        dve.wait_ge(h_S0.sem, h_S0.at(prev))
                        if due(pe_ho, prev - 1):
                            dve.wait_ge(pe_ho.sem, pe_ho.at(prev - 1))
                        for i in range(3):
                            v.scalar_tensor_tensor(out=S[:, 0, i + 1, :], in0=S[:, 0, i, :], scalar=dec[:, 0, i + 1:i + 2],
                                                   in1=ps[:, C, tile_cols(i + 1)], op0=ALU.mult, op1=ALU.add)
                            v.scalar_tensor_tensor(out=S[:, 1, 2 - i, :], in0=S[:, 1, 3 - i, :], scalar=dec[:, 1, 4 - i:5 - i],
                                                   in1=ps[:, DD, tile_cols(3 - i)], op0=ALU.mult, op1=ALU.add).then_inc(h_S.sem, 1)
                            dve.wait_ge(h_S.sem, h_S.at(prev, i + 1))
                    if 3 <= n < 3 + PRODUCTS:
                        level = n - 3
                        scored, placed = pe_level.at(prev, level + 1), h_sT.at(prev, level)
                        if not isinstance(prev, int):
                            scored, placed = dve.to_reg(scored), dve.to_reg(placed)
                        if level:
                            dve.wait_ge(con_in.sem, con_in.at(0))
                        dve.wait_ge(pe_level.sem, scored)
                        out = tiles(hsT[:, P:T])
                        if level == 0:
                            if due(pe_ho, prev - 1):
                                dve.wait_ge(pe_ho.sem, pe_ho.at(prev - 1))
                            v.tensor_copy(out, tiles(ps[:, A, :]))
                            v.tensor_copy(hsT[:, 0:P], ctx_scores(h, level)).then_inc(h_sT.sem, 1)
                        else:
                            dve.wait_ge(h_sT.sem, placed)
                            v.copy_predicated(out, mask(level).unsqueeze(1).broadcast_to([P, TILES - 1, P]), tiles(ps[:, A, :]))
                            v.copy_predicated(hsT[:, 0:P], mask(level), ctx_scores(h, level)).then_inc(h_sT.sem, 1)
                    if n == 12:
                        dve.wait_ge(h_rms.sem, h_rms.at(prev, 2))
                        v.scalar_tensor_tensor(out=hr[:, P:T], in0=ps[:, C, :], scalar=hnw, in1=hr[:, P:T], op0=ALU.mult, op1=ALU.mult)
                        v.scalar_tensor_tensor(out=hr[:, 0:P], in0=ps[:, DD, 0:P], scalar=hnw, in1=hr[:, 0:P],
                                               op0=ALU.mult, op1=ALU.mult).then_inc(h_out.sem, 1)
                        dve.wait_ge(h_out.sem, h_out.at(prev, 1))
                        v.tensor_tensor(hr, hr, hsg, ALU.mult).then_inc(h_out.sem, 1)
                if h is None:
                    return
                if n == 4 and prev is None:
                    dve.wait_ge(gate_in.sem, gate_in.at(0))
                    v.tensor_tensor(gate_cols, mod_cols[:, 0:2, 2, :], mod_cols[:, 2:4, 2, :], ALU.add).then_inc(gate_steps.sem, 1)
                    dve.wait_ge(gate_steps.sem, gate_steps.at(0))
                    v.tensor_tensor(gate_cols, gate_cols, bias_cols[:, 2, :].unsqueeze(1).broadcast_to([P, 2, KT]), ALU.add).then_inc(gate_steps.sem, 1)
                if n == 8:
                    dve.wait_ge(r_eg.sem, r_eg.at(h))
                    v.tensor_scalar(rsg, rsg, 1.0, None, ALU.add).then_inc(r_silu.sem, 1)
                    dve.wait_ge(r_silu.sem, r_silu.at(h, 1))
                    reciprocal_half(rsg, 0, r_silu)
                if n == 9:
                    reciprocal_half(rsg, 1, r_silu)
                    dve.wait_ge(r_silu.sem, r_silu.at(h, 3))
                    v.tensor_tensor(halves(rsg), halves(rsg), proj(3), ALU.mult).then_inc(r_silu.sem, 1)
                if n == 12:
                    tmp = sT[:, 0:REL]
                    if prev is None:
                        dve.wait_ge(con_in.sem, con_in.at(0))
                    if due(r_sT, h - 1):
                        dve.wait_ge(r_sT.sem, r_sT.at(h - 1))
                    if due(pe_rss, h - 1):
                        dve.wait_ge(pe_rss.sem, pe_rss.at(h - 1))
                    v.tensor_scalar(strip, rel, 0.0, lg[:, bass.ds(h, 1)], ALU.max, ALU.mult).then_inc(strip_x.sem, 1)
                    v.tensor_scalar(tmp, rel, 0.0, nlg[:, bass.ds(h + HEADS, 1)], ALU.min, ALU.mult).then_inc(strip_x.sem, 1)
                    dve.wait_ge(strip_x.sem, strip_x.at(h, 2))
                    v.tensor_tensor(strip, strip, tmp, ALU.add).then_inc(strip_x.sem, 1)
                if n == 13:
                    dve.wait_ge(swapped.sem, swapped.at(h))
                    v.tensor_tensor(rope_q, rope_q, sin, ALU.mult)
                    v.tensor_tensor(rope_k, rope_k, sin, ALU.mult).then_inc(rope_sin.sem, 1)
                    dve.wait_ge(rope_sin.sem, rope_sin.at(h))
                    dve.wait_ge(rope_cos.sem, rope_cos.at(h))
                    v.tensor_tensor(rq[:, P:T], rq[:, P:T], rope_q, ALU.add)
                    v.tensor_tensor(rk[:, P:T], rk[:, P:T], rope_k, ALU.add).then_inc(roped.sem, 1)
                    dve.wait_ge(strip_e.sem, strip_e.at(h))
                    diag = strip[:, REL - LAT:REL - LAT + P]
                    v.tensor_tensor(diag, diag, ident, ALU.add).then_inc(strip_i.sem, 1)
                if 12 <= n <= 15:
                    s, odd = (n - 12) // 2, n % 2
                    buf, at = F[:, s, :], 5 * s
                    col = bass.ds(s * HEADS + h, 1)
                    if odd == 0:
                        dve.wait_ge(h_ez.sem, h_ez.at(h, s + 1))
                        v.tensor_scalar(buf, buf, 1.0, None, ALU.add).then_inc(h_gate.sem, 1)
                        dve.wait_ge(h_gate.sem, h_gate.at(h, at + 1))
                        reciprocal_half(buf, 0, h_gate)
                    else:
                        reciprocal_half(buf, 1, h_gate)
                        dve.wait_ge(h_gate.sem, h_gate.at(h, at + 3))
                        v.tensor_scalar(buf, buf, oml[:, col], lb[:, col], ALU.mult, ALU.add).then_inc(h_gate.sem, 1)
                        dve.wait_ge(h_gate.sem, h_gate.at(h, at + 4))
                        if due(la, h - 1):
                            dve.wait_ge(la.sem, la.at(h - 1))
                        v.tensor_scalar(K[:, s, :], buf, -1.0, 1.0, ALU.mult, ALU.add).then_inc(h_gate.sem, 1)
                if n == 15 or n == 16:
                    if n == 15:
                        dve.wait_ge(strip_i.sem, strip_i.at(h))
                        dve.wait_ge(roped.sem, roped.at(h))
                    for jt in range(2 * (n - 15), 2 * (n - 15) + 2):
                        dve.wait_ge(pe_rs.sem, pe_rs.at(h, jt + 1))
                        off = REL - LAT - jt * P
                        v.tensor_tensor(sT[:, jt * LAT:(jt + 1) * LAT], ps[:, A + jt % 2, :], strip[:, off:off + LAT],
                                        ALU.mult).then_inc(r_sT.sem, 1)
                    if n == 16:
                        dve.wait_ge(pe_rs.sem, pe_rs.at(h, 5))
                        v.tensor_tensor(sT[:, 4 * LAT:4 * LAT + P], ps[:, C, 0:P], strip[:, REL - LAT:REL - LAT + P],
                                        ALU.mult).then_inc(r_sT.sem, 1)
                if n == 15:
                    dve.wait_ge(h_log.sem, h_log.at(h, 1))
                    v.tensor_tensor_scan(B[:, 0, :], reset, F[:, 0, :], 0.0, ALU.mult, ALU.add).then_inc(h_scan.sem, 1)
                if n == 17:
                    dve.wait_ge(h_log.sem, h_log.at(h, 2))
                    v.tensor_tensor_scan(B[:, 1, ::-1], reset, F[:, 1, ::-1], 0.0, ALU.mult, ALU.add).then_inc(h_scan.sem, 1)
                    dve.wait_ge(h_scan.sem, h_scan.at(h))
                    if due(h_stored, h - 1):
                        dve.wait_ge(h_stored.sem, h_stored.at(h - 1))
                    bf, bb = tiles(B[:, 0, :]), tiles(B[:, 1, :])
                    v.tensor_tensor(tiles(KL[:, 0, :]), bf[:, :, P - 1:P].broadcast_to([P, TILES, P]), bf, ALU.subtract)
                    v.tensor_tensor(tiles(KL[:, 1, :]), bb[:, :, 0:1].broadcast_to([P, TILES, P]), bb, ALU.subtract).then_inc(h_klx.sem, 1)

            def head(h, prev):
                for n in range(CHUNKS):
                    split(h, n)
                    if prev is None and n < 2:
                        low_context(n)
                    if n == 0:
                        if prev is not None:
                            items(CHUNKS - 1, prev, None)
                    else:
                        items(n - 1, h, prev)

            head(0, None)
            head(1, 0)
            with dve.Fori(2, HEADS) as h:
                head(h, h - 1)
            last = HEADS - 1
            items(CHUNKS - 1, last, None)

            def split_o(kt):
                dve.wait_ge(o_hi.sem, o_hi.at(kt))
                src = hr if kt == 2 * HEADS - 1 else o_raw[:, kt % STAGES, :]
                v.tensor_tensor(hT_lo[:, kt, :], src, hT_hi[:, kt, :].bitcast(F32), ALU.subtract).then_inc(o_lo.sem, 1)

            def split_w(m):
                dve.wait_ge(d_hi.sem, d_hi.at(0, m + 1))
                v.tensor_tensor(w_lo[:, m % 2, :], raw[:, m % 2, :], w_hi[:, m % 2, :].bitcast(F32), ALU.subtract).then_inc(d_lo.sem, 1)

            for n in range(13):
                items(n, None, last)
                for j in split_at(n):
                    for kt in range(WK * j, min(WK * j + WK, 2 * HEADS - 1)):
                        split_o(kt)
                    split_w(j)
            split_o(2 * HEADS - 1)

            def gate_part(m):
                nb, t = m // TILES, evac_order(m // TILES)[m % TILES]
                if nb < OUT_BLOCKS - 1:
                    dve.wait_ge(d_used.sem, d_used.at(nb))
                elif t < EARLY:
                    dve.wait_ge(d_used.sem, d_used.at(nb))
                elif t < TILES - 1:
                    if due(d_tile, t - EARLY):
                        dve.wait_ge(d_tile.sem, d_tile.at(t - EARLY))
                else:
                    dve.wait_ge(d_used.sem, d_used.at(nb + 1))
                if m % TILES == 0:
                    dve.wait_ge(res_in[nb].sem, res_in[nb].at(0))
                if m >= 2:
                    if due(d_ev, 0, m - 1):
                        dve.wait_ge(d_ev.sem, d_ev.at(0, m - 1))
                v.tensor_tensor(gated[:, m % 2, :], ps[:, out_bank(nb, t), :],
                                gates[:, 0 if t == 0 else 1, nb * WIDE:(nb + 1) * WIDE], ALU.mult).then_inc(d_gated.sem, 1)

            def add_part(m):
                nb, t = m // TILES, evac_order(m // TILES)[m % TILES]
                dve.wait_ge(d_gated.sem, d_gated.at(0, m + 1))
                x = x_res[:, t, nb * WIDE:(nb + 1) * WIDE]
                v.tensor_tensor(x, x, gated[:, m % 2, :], ALU.add).then_inc(d_ev.sem, 1)

            def finish(nb, first, last):
                for m in range(nb * TILES + first, nb * TILES + last):
                    gate_part(m)
                    if m > nb * TILES + first:
                        add_part(m - 1)
                add_part(nb * TILES + last - 1)

            def fin_step(i, count=[0]):
                count[0] += 1
                i.then_inc(fin_steps.sem, 1)
                dve.wait_ge(fin_steps.sem, fin_steps.at(0, count[0]))

            def variance(tokens, squares):
                dve.wait_ge(d_sq.sem, d_sq.at(OUT_BLOCKS - 1, squares))
                fin_step(v.reduce_sum(ssq_out[:, tokens], ssq4[:, tokens, :], AX_X))
                fin_step(v.tensor_scalar(var_o[:, tokens], ssq_out[:, tokens], 1.0 / D_MODEL, EPS, ALU.mult, ALU.add))

            def last_norm(group, tokens):
                dve.wait_ge(fin_act.sem, fin_act.at(group))
                newton(rstd_o[:, tokens], var_o[:, tokens], newt_o[:, tokens], fin_step)

            def finish_left(t):
                dve.wait_ge(weighted.sem, weighted.at(0))
                x = x_res[:, t, 0:D_MODEL - WIDE]
                v.tensor_scalar(x, x, rstd_o[:, t:t + 1], None, ALU.mult).then_inc(y_left[0].sem, 1)

            def finish_right(t):
                x, weight = x_res[:, t, D_MODEL - WIDE:], fnw[:, D_MODEL - WIDE:]
                v.scalar_tensor_tensor(out=x, in0=x, scalar=rstd_o[:, t:t + 1], in1=weight,
                                       op0=ALU.mult, op1=ALU.mult).then_inc(y_right.sem, 1)

            for m in range(WCHUNKS, OUT_CHUNKS):
                nb, j = m // WCHUNKS, m % WCHUNKS
                split_w(m)
                if nb < OUT_BLOCKS:
                    if j == 1:
                        finish(nb - 1, 0, 2)
                    if j == 2:
                        finish(nb - 1, 2, TILES)
                else:
                    if 1 <= j < 1 + EARLY:
                        finish(OUT_BLOCKS - 1, j - 1, j)
                    if j == 5:
                        variance(slice(0, EARLY), EARLY)
                    if j == 6:
                        last_norm(0, slice(0, EARLY))
                        finish_right(0)
                        finish_left(0)
                    if j == 7:
                        finish_right(1)
                        finish_right(2)
                        finish_left(2)
            finish(OUT_BLOCKS - 1, EARLY, TILES)
            variance(slice(EARLY, TILES), TILES)
            last_norm(1, slice(EARLY, TILES))
            finish_right(3)
            finish_right(4)
            finish_left(4)

        @block.gpsimd
        def _(pool):
            g = nc.gpsimd

            def items(n, h, prev):
                if prev is not None:
                    if n == 0:
                        pool.wait_ge(h_ekl.sem, h_ekl.at(prev))
                        g.tensor_tensor(KL, KL, K, ALU.mult).then_inc(h_kl.sem, 1)
                    if 1 <= n <= LEVELS:
                        level = n - 1
                        half = P >> (level + 1)
                        buf = XE[:, level % 2, 1, :]
                        bf, bb, x = blocks(B[:, 0, :], level), blocks(B[:, 1, :], level), blocks(buf, level)
                        kf, kb = blocks(K[:, 0, :], level), blocks(K[:, 1, :], level)
                        nblk = T // (2 * half)
                        left, right = slice(0, half), slice(half, 2 * half)
                        pool.wait_ge(h_scan.sem, h_scan.at(prev))
                        if due(pe_level, prev, level - 1):
                            pool.wait_ge(pe_level.sem, pe_level.at(prev, level - 1))
                        g.tensor_tensor(x[:, :, left], bf[:, :, half - 1:half].broadcast_to([P, nblk, half]), bf[:, :, left], ALU.subtract)
                        g.tensor_tensor(x[:, :, right], bb[:, :, half:half + 1].broadcast_to([P, nblk, half]), bb[:, :, right],
                                        ALU.subtract).then_inc(xa.sem, 1)
                        pool.wait_ge(xe.sem, xe.at(prev, level + 1))
                        g.tensor_tensor(x[:, :, left], x[:, :, left], kf[:, :, left], ALU.mult)
                        g.tensor_tensor(x[:, :, right], x[:, :, right], kb[:, :, right], ALU.mult).then_inc(la.sem, 1)
                    if n == LEVELS + 1:
                        if due(pe_level, prev, LEVELS - 1):
                            pool.wait_ge(pe_level.sem, pe_level.at(prev, LEVELS - 1))
                        g.tensor_tensor(XE[:, 1, 1, :], K[:, 0, :], K[:, 1, :], ALU.add).then_inc(la.sem, 1)
                if h is None:
                    return
                if n == 13:
                    if prev is None:
                        pool.wait_ge(con_in.sem, con_in.at(0))
                    pool.wait_ge(swapped.sem, swapped.at(h))
                    g.tensor_tensor(rq[:, P:T], rq[:, P:T], cos, ALU.mult)
                    g.tensor_tensor(rk[:, P:T], rk[:, P:T], cos, ALU.mult).then_inc(rope_cos.sem, 1)
                if n == 15:
                    pool.wait_ge(r_dec.sem, r_dec.at(h))
                    pool.wait_ge(roped.sem, roped.at(h))
                    for s in range(2):
                        i = g.tensor_tensor(rqd[:, s, :], rqd[:, s, :], rq[:, P:T], ALU.mult)
                    i.then_inc(r_qdec.sem, 1)

            def head(h, prev):
                for n in range(CHUNKS):
                    items(n, h, prev)

            def ada_block(nb, extra=None):
                for k in range(KT):
                    if on_pool(k):
                        j, w = k // WK, slice(k % WK * WIDE, (k % WK + 1) * WIDE)
                        pool.wait_ge(a_hi.sem, a_hi.at(nb, k + 1))
                        g.tensor_tensor(w_lo[:, j % 2, w], ada_raw[:, j, w], w_hi[:, j % 2, w].bitcast(F32),
                                        ALU.subtract).then_inc(a_lo_pool.sem, 1)
                    if extra is not None:
                        extra(k)

            def low_input(k):
                pool.wait_ge(h_hi.sem, h_hi.at(k))
                g.tensor_tensor(tiles(hT_lo[:, k, P:T]), x_in[:, 1:TILES, k::KT], tiles(hT_hi[:, k, P:T].bitcast(F32)),
                                ALU.subtract).then_inc(h_lo.sem, 1)

            def with_low_input(nb):
                def extra(k):
                    if k % WK == WK - 1:
                        for at in modulated_at((nb - ADA_INPUT - 1) * WCHUNKS + k // WK - 2):
                            low_input(at)
                return extra

            for nb in range(4):
                ada_block(nb)
            with pool.Fori(4, ADA_INPUT) as nb:
                ada_block(nb)
            for nb in range(ADA_INPUT, ADA_BLOCKS):
                ada_block(nb, with_low_input(nb))
            for chunk in range(3 * WCHUNKS - 2, 3 * WCHUNKS + 1):
                for k in modulated_at(chunk):
                    low_input(k)

            head(0, None)
            head(1, 0)
            with pool.Fori(2, HEADS) as h:
                head(h, h - 1)
            for n in range(LEVELS + 2):
                items(n, None, HEADS - 1)

            pool.wait_ge(fnw_in.sem, fnw_in.at(0))
            for m in range((OUT_BLOCKS - 1) * TILES):
                nb, t = m // TILES, evac_order(m // TILES)[m % TILES]
                at = slice(nb * WIDE, (nb + 1) * WIDE)
                pool.wait_ge(d_sq.sem, d_sq.at(0, m + 1))
                g.tensor_tensor(x_res[:, t, at], x_res[:, t, at], fnw[:, at], ALU.mult).then_inc(weighted.sem, 1)

        @block.tensor
        def _(pe):
            mm = nc.tensor.matmul
            pe.wait_ge(cs_ready.sem, cs_ready.at(0))

            def ada_block(nb, b, extra=None):
                for j in range(WCHUNKS):
                    if j == 0:
                        if due(a_row, nb - 2):
                            pe.wait_ge(a_row.sem, a_row.at(nb - 2))
                    for kk in range(WK):
                        k = j * WK + kk
                        if on_pool(k):
                            pe.wait_ge(a_lo_pool.sem, a_lo_pool.at(nb, lows(k)[1]))
                        else:
                            pe.wait_ge(a_lo.sem, a_lo.at(nb, lows(k)[0]))
                        w = slice(kk * WIDE, (kk + 1) * WIDE)
                        mm(ps[:, b, :], cs[:, k, :], w_hi[:, j % 2, w], start=k == 0, stop=False)
                        mm(ps[:, b, :], cs[:, k, :], w_lo[:, j % 2, w], start=False, stop=k == KT - 1).then_inc(a_used.sem, 1)
                    if extra is not None:
                        extra(j)

            def transposes(nb):
                def extra(j):
                    k = (nb - 2) * WCHUNKS + j
                    bank = 2 + 2 * (k % 3)
                    if k == 0:
                        pe.wait_ge(x_scaled.sem, x_scaled.at(TILES - 1))
                    if k >= 3:
                        if due(x_evac[(k - 3) % 2], (k - 3) // 2):
                            pe.wait_ge(x_evac[(k - 3) % 2].sem, x_evac[(k - 3) % 2].at((k - 3) // 2))
                    for t in range(1, TILES):
                        nc.tensor.transpose(ps[:, bank, tile_cols(t - 1)], x_in[:, t, k::KT], ident)
                    nc.tensor.transpose(ps[:, bank + 1, 0:P], x_in[:, 0, k::KT], ident).then_inc(x_tr.sem, 1)
                return extra

            ada_block(0, 0)
            pe.wait_ge(con_start.sem, con_start.at(0))
            pe.wait_ge(small_in.sem, small_in.at(4))
            nc.tensor.transpose(ps[:, A, 0:4 * HEADS], lb_in, con[0:4 * HEADS, C_IDENT:C_IDENT + 4 * HEADS]).then_inc(lb_pe.sem, 1)
            ada_block(1, 1)
            for nb in range(2, 4):
                ada_block(nb, nb % 2, transposes(nb))
            with pe.Fori(2, ADA_BLOCKS // 2) as pair:
                for b in range(2):
                    ada_block(2 * pair + b, b)
            freed = {0: (h_graw, 1, None), 1: (h_v, 1, None), 2: (r_q, 0, None), 3: (r_k, 0, None), 4: (r_v, 0, None),
                     5: (r_silu, 0, 4), 6: (h_q, 0, None), 7: (h_ez, 0, 1), 8: (h_ez, 0, 2)}

            def chunk(h, n):
                i, half = n // 2, n % 2
                if isinstance(h, int) and h == 0 and n < 2:
                    pe.wait_ge(ctx_lo.sem, ctx_lo.at(0, n + 1))
                    if due(h_lo, KC * (n + 1) - 1):
                        pe.wait_ge(h_lo.sem, h_lo.at(KC * (n + 1) - 1))
                pe.wait_ge(wt_lo.sem, wt_lo.at(h, n + 1))
                if half == 0:
                    signal, back, k = freed[i]
                    if due(signal, h - back, k):
                        pe.wait_ge(signal.sem, signal.at(h - back, k))
                out = [ps[:, 2 * (i % 2) + s, 0:HALF] for s in range(2)]
                for kk in range(KC):
                    k = half * KC + kk
                    w = slice(kk * P, (kk + 1) * P)
                    for step, (wt, x) in enumerate(((w_hi, hT_hi), (w_hi, hT_lo), (w_lo, hT_hi))):
                        for s in range(2):
                            ins = mm(out[s], wt[:, n % 2, w], x[:, k, s * HALF:(s + 1) * HALF],
                                     start=k == 0 and step == 0, stop=k == KT - 1 and step == 2)
                ins.then_inc(wt_used.sem, 1)

            def stage(n, h, prev):
                if prev is not None:
                    if n == 0:
                        pe.wait_ge(h_v.sem, h_v.at(prev))
                        pe.wait_ge(r_out.sem, r_out.at(prev, 1))
                        for t in range(1, TILES):
                            nc.tensor.transpose(ps[:, A, tile_cols(t - 1)], hvT[:, tile_cols(t)], ident)
                        nc.tensor.transpose(ps[:, BB, 0:P], hvT[:, 0:P], ident).then_inc(pe_htok.sem, 1)
                    if n == 1:
                        pe.wait_ge(h_kl.sem, h_kl.at(prev))
                        for i, t in enumerate((0, 1, 2, 3)):
                            nc.tensor.transpose(ps[:, C, tile_cols(i)], KL[:, 0, tile_cols(t)], ident)
                        for i, t in enumerate((0, 2, 3, 4)):
                            ins = nc.tensor.transpose(ps[:, DD, tile_cols(i)], KL[:, 1, tile_cols(t)], ident)
                        ins.then_inc(pe_hkl.sem, 1)
                    if n == 2:
                        pe.wait_ge(h_kltok.sem, h_kltok.at(prev))
                        pe.wait_ge(h_tok.sem, h_tok.at(prev))
                        for i, t in enumerate((0, 1, 2, 3)):
                            mm(ps[:, C, tile_cols(i)], kltok[:, i, :], htok[:, t, :], start=True, stop=True)
                        for i, t in enumerate((0, 2, 3, 4)):
                            ins = mm(ps[:, DD, tile_cols(i)], kltok[:, 4 + i, :], htok[:, t, :], start=True, stop=True)
                        ins.then_inc(pe_hu.sem, 1)
                    if 2 <= n < 2 + PRODUCTS:
                        level = n - 2
                        b = level % 2
                        pe.wait_ge(la.sem, la.at(prev, level + 1))
                        if level < LEVELS:
                            pe.wait_ge(lq.sem, lq.at(prev, level + 1))
                            q = XE[:, b, 0, :]
                        else:
                            q = hq
                        if level:
                            if due(h_sT, prev, level):
                                pe.wait_ge(h_sT.sem, h_sT.at(prev, level))
                        for t in range(1, TILES):
                            mm(ps[:, A, tile_cols(t - 1)], XE[:, b, 1, tile_cols(t)], q[:, tile_cols(t)], start=True, stop=True)
                        if h is None and level == 1:
                            pe.wait_ge(h_S.sem, h_S.at(prev))
                            pe.wait_ge(h_state.sem, h_state.at(prev))
                        mm(ctx_scores(h, level), XE[:, b, 1, 0:P], q[:, 0:P], start=True, stop=True).then_inc(pe_level.sem, 1)
                    if n == 10:
                        pe.wait_ge(h_sT.sem, h_sT.at(prev))
                        pe.wait_ge(h_S.sem, h_S.at(prev))
                        pe.wait_ge(h_qr.sem, h_qr.at(prev))
                        pe.wait_ge(h_state.sem, h_state.at(prev))
                        for t in range(1, TILES):
                            out = ps[:, C, tile_cols(t - 1)]
                            mm(out, htok[:, t, :], hsT[:, tile_cols(t)], start=True, stop=False)
                            mm(out, S[:, 0, t - 1, :], F[:, 0, tile_cols(t)], start=False, stop=False)
                            mm(out, S[:, 1, t - 1, :], F[:, 1, tile_cols(t)], start=False, stop=True)
                        mm(ps[:, DD, 0:P], htok[:, 0, :], hsT[:, 0:P], start=True, stop=True).then_inc(pe_ho.sem, 1)
                    if n == 11:
                        pe.wait_ge(h_sq.sem, h_sq.at(prev))
                        mm(ps[:, A, :], ones, hsq[:, P:T], start=True, stop=True)
                        mm(ctx_sums(h), ones, hsq[:, 0:P], start=True, stop=True).then_inc(pe_hss.sem, 1)
                if h is None:
                    return
                if n == 13:
                    pe.wait_ge(r_v.sem, r_v.at(h))
                    if due(h_out, h - 1, 1):
                        pe.wait_ge(h_out.sem, h_out.at(h - 1, 1))
                    for t in range(1, TILES):
                        nc.tensor.transpose(ps[:, C, tile_cols(t - 1)], rvT[:, tile_cols(t)], ident)
                    nc.tensor.transpose(ps[:, DD, 0:P], rvT[:, 0:P], ident)
                    nc.tensor.transpose(ps[:, DD, P:2 * P], rk[:, 0:P], ident).then_inc(pe_rtok.sem, 1)
                if n == 14:
                    if due(h_rms, h - 1, 1):
                        pe.wait_ge(h_rms.sem, h_rms.at(h - 1, 1))
                if n == 14 or n == 15:
                    pe.wait_ge(roped.sem, roped.at(h))
                    for jt in range(2 * (n - 14), 2 * (n - 14) + 2):
                        if jt >= 2:
                            if due(r_sT, h, jt - 1):
                                pe.wait_ge(r_sT.sem, r_sT.at(h, jt - 1))
                        mm(ps[:, A + jt % 2, :], rk[:, tile_cols(1 + jt)], rq[:, P:T], start=True, stop=True).then_inc(pe_rs.sem, 1)
                    if n == 15:
                        pe.wait_ge(r_tok.sem, r_tok.at(h))
                        mm(ps[:, C, 0:P], rk[:, 0:P], rq[:, 0:P], start=True, stop=True).then_inc(pe_rs.sem, 1)
                if n == 16:
                    pe.wait_ge(r_sT.sem, r_sT.at(h))
                    pe.wait_ge(r_qdec.sem, r_qdec.at(h))
                    pe.wait_ge(r_S0.sem, r_S0.at(h))
                    for jt in range(4):
                        mm(ps[:, A, :], rtok[:, 1 + jt, :], sT[:, jt * LAT:(jt + 1) * LAT], start=jt == 0, stop=False)
                    for s in range(2):
                        mm(ps[:, A, :], rS0[:, s, :], rqd[:, s, :], start=False, stop=s == 1)
                    mm(ps[:, BB, 0:P], rtok[:, 0, :], sT[:, 4 * LAT:4 * LAT + P], start=True, stop=True)
                    for s in range(2):
                        ins = mm(ps[:, DD, tile_cols(s)], kts[:, s, :], rtok[:, 0, :], start=True, stop=True)
                    ins.then_inc(pe_ro.sem, 1)
                if n == 17:
                    if prev is None:
                        pe.wait_ge(con_in.sem, con_in.at(0))
                    pe.wait_ge(r_sq.sem, r_sq.at(h))
                    pe.wait_ge(r_state.sem, r_state.at(h))
                    mm(ps[:, C, :], ones, rsq[:, P:T], start=True, stop=True)
                    mm(ps[:, DD, 0:P], ones, rsq[:, 0:P], start=True, stop=True).then_inc(pe_rss.sem, 1)

            def head(h, prev):
                for n in range(CHUNKS):
                    chunk(h, n)
                    stage(n, h, prev)

            head(0, None)
            head(1, 0)
            with pe.Fori(2, HEADS) as h:
                head(h, h - 1)
            last = HEADS - 1

            def out_tile(nb, j, kk, t):
                m, k = nb * WCHUNKS + j, j * WK + kk
                w = slice(kk * WIDE, (kk + 1) * WIDE)
                out = ps[:, out_bank(nb, t), :]
                mm(out, hT_hi[:, k, tile_cols(t)], w_hi[:, m % 2, w], start=k == 0, stop=False)
                mm(out, hT_hi[:, k, tile_cols(t)], w_lo[:, m % 2, w], start=False, stop=False)
                return mm(out, hT_lo[:, k, tile_cols(t)], w_hi[:, m % 2, w], start=False, stop=k == KT - 1)

            def first_block(j, kk, tokens=range(TILES)):
                pe.wait_ge(d_lo.sem, d_lo.at(0, j + 1))
                pe.wait_ge(o_lo.sem, o_lo.at(WK * j + kk))
                if j == 0 and kk == 0:
                    pe.wait_ge(h_graw.sem, h_graw.at(last))
                    pe.wait_ge(h_v.sem, h_v.at(last))
                for t in tokens:
                    i = out_tile(0, j, kk, t)
                if kk == WK - 1 and TILES - 1 in tokens:
                    i.then_inc(d_used.sem, 1)

            for n in range(12):
                stage(n, None, last)
                if n == 2:
                    for kk in range(WK):
                        first_block(0, kk, range(TILES - 1))
                if n == 3:
                    for kk in range(WK):
                        first_block(0, kk, range(TILES - 1, TILES))
                    first_block(1, 0)
                if 4 <= n < 10:
                    if n > 4:
                        first_block(n - 3, 0)
                    if n < 9:
                        first_block(n - 3, 1)
            first_block(WCHUNKS - 2, 1)
            first_block(WCHUNKS - 1, 0)
            first_block(WCHUNKS - 1, 1)

            def bank_read(nb, t):
                if nb == 1 and t == 3 or nb == 3 and t == 3:
                    if due(d_ev, nb - 1, 1):
                        pe.wait_ge(d_ev.sem, d_ev.at(nb - 1, 1))
                if nb == 1 and t == 4 or nb == 3 and t == 4:
                    if due(d_ev, nb - 1, 2):
                        pe.wait_ge(d_ev.sem, d_ev.at(nb - 1, 2))
                if nb == 2 and t < 2:
                    if due(d_ev, nb - 1, t + 1):
                        pe.wait_ge(d_ev.sem, d_ev.at(nb - 1, t + 1))
                if nb == 3 and t == 0:
                    if due(d_ev, nb - 2):
                        pe.wait_ge(d_ev.sem, d_ev.at(nb - 2))

            for nb in range(1, OUT_BLOCKS - 1):
                late = (3, 4) if nb % 2 else (0, 1)
                early = [t for t in range(TILES) if t not in late]
                for chunks, tokens in (((0, 1), early), ((0, 1), late)):
                    for j in chunks:
                        pe.wait_ge(d_lo.sem, d_lo.at(nb, j + 1))
                        for t in tokens:
                            if j == 0:
                                bank_read(nb, t)
                            for kk in range(WK):
                                i = out_tile(nb, j, kk, t)
                        if tokens is late:
                            i.then_inc(d_used.sem, 1)
                for j in range(2, WCHUNKS):
                    pe.wait_ge(d_lo.sem, d_lo.at(nb, j + 1))
                    for t in range(TILES):
                        for kk in range(WK):
                            i = out_tile(nb, j, kk, t)
                    i.then_inc(d_used.sem, 1)
            for half, tokens in enumerate((range(EARLY), range(EARLY, TILES))):
                for j in range(WCHUNKS):
                    pe.wait_ge(d_lo.sem, d_lo.at(OUT_BLOCKS - 1 + half, j + 1))
                    for t in tokens:
                        if j == 0:
                            bank_read(OUT_BLOCKS - 1, t)
                        for kk in range(WK):
                            i = out_tile(OUT_BLOCKS - 1, j, kk, t)
                        if half and j == WCHUNKS - 1 and t < TILES - 1:
                            i.then_inc(d_tile.sem, 1)
                    i.then_inc(d_used.sem, 1)


_INS = ["x_prompt", "x_sample", "state_ret_fwd", "state_ret_bwd", "state_hgrn_fwd", "state_hgrn_bwd", "c", "c_ctx",
        "norm_w", "w_ada", "b_ada", "w_in", "ret_decay", "hg_lower_bounds", "hg_norm_w", "w_out", "final_norm_w"]
_STATE = (1, 1, HEADS, P, P)
_OUTS = [(1, CTX, D_MODEL), (1, LAT, D_MODEL), _STATE, _STATE, _STATE, _STATE]


def _constants():
    import numpy as np

    con = np.zeros((P, NCONST), np.float32)
    p = np.arange(P)
    con[:, C_IDENT:C_IDENT + P] = np.eye(P)
    con[:, C_ONES:C_ONES + P] = 1.0
    quarter = P // 4
    freqs = (np.float32(ROPE_BASE) ** (-np.arange(quarter, dtype=np.float32) / np.float32(quarter))).astype(np.float32)
    tok = np.arange(LAT)
    pos = np.stack([tok // GRID_W, tok % GRID_W]).astype(np.float32)
    ang = (pos[p // (2 * quarter)] * freqs[p % quarter][:, None]).astype(np.float32)
    sign = np.where((p // quarter) % 2 == 0, -1.0, 1.0)[:, None]
    con[:, C_COS:C_COS + LAT] = np.cos(ang)
    con[:, C_SIN:C_SIN + LAT] = sign * np.sin(ang)
    con[:, C_REL:C_REL + REL] = np.arange(REL)[None, :] - (REL - LAT) - p[:, None]
    for level in range(1, PRODUCTS):
        size = P >> level
        con[:, C_MASK + (level - 1) * P:C_MASK + level * P] = p[:, None] // size == p[None, :] // size
    con[:, C_RESET:C_RESET + T] = np.arange(T) % P != 0
    con[:, C_POS:C_POS + 4] = np.stack([p + 1, LAT - p, P - 1 - p, p], 1)
    return con


def kernel(**inputs):
    import numpy as np
    import concourse.bacc as bacc
    from concourse.bass_utils import run_bass_kernel_spmd

    nc = bacc.Bacc("TRN2", target_bir_lowering=False, num_devices=1)
    arrays, args = {}, []
    for name in _INS:
        a = np.ascontiguousarray(inputs[name])
        arrays[f"in_{name}"] = a
        args.append(nc.dram_tensor(f"in_{name}", a.shape, F32, kind="ExternalInput").ap())
    con = _constants()
    arrays["in_constants"] = con
    args.append(nc.dram_tensor("in_constants", con.shape, F32, kind="ExternalInput").ap())
    for i, shape in enumerate(_OUTS):
        args.append(nc.dram_tensor(f"out_{i}", shape, F32, kind="ExternalOutput").ap())
    layer(nc, *args)
    r = run_bass_kernel_spmd(nc, [arrays], core_ids=[0])
    return tuple(r.results[0][f"out_{i}"] for i in range(len(_OUTS)))
```
